# Optimizing a Trainium2 kernel written in Bass

```python
import math
import jax, jax.numpy as jnp
from jax import lax
import numpy as np

D_MODEL = 1024
BATCH = 1
SEQ = 512
DEPTH = 2
DEC_BATCH = 8
DEC_SEQ = 1
PAST_LEN = 1024
PAGE_SIZE = 128

N_HEADS = 16
HEAD_DIM = 64
KV_HEADS_A = 4
KV_HEADS_B = 2
G_A = N_HEADS // KV_HEADS_A
G_B = N_HEADS // KV_HEADS_B
IDX_HEADS = 8
IDX_DIM = 64
TOPK_MAX = 256
WINDOW = 128
Q_BLOCK = 128
N_BUCKETS = 32
MAX_DISTANCE = 128
D_FF = 4 * D_MODEL
ALPHA = (2 * DEPTH) ** 0.25
BETA = (8 * DEPTH) ** -0.25
N_A_LAYERS = (DEPTH + 1) // 2
N_B_LAYERS = DEPTH // 2
LN_EPS = 1e-5
NEG = -1e30
ATTN_SCALE = HEAD_DIM ** -0.5
IDX_SCALE = IDX_HEADS ** -0.5 * IDX_DIM ** -0.5
A_SIZES = [N_HEADS * HEAD_DIM, KV_HEADS_A * HEAD_DIM, KV_HEADS_A * HEAD_DIM, IDX_HEADS * IDX_DIM, IDX_DIM, IDX_HEADS]
A_IN = sum(A_SIZES)
A_SPLIT_POINTS = [int(c) for c in np.cumsum(A_SIZES)[:-1]]
B_SIZES = [N_HEADS * HEAD_DIM, KV_HEADS_B * HEAD_DIM, KV_HEADS_B * HEAD_DIM]
B_IN = sum(B_SIZES)
B_SPLIT_POINTS = [int(c) for c in np.cumsum(B_SIZES)[:-1]]

kernel_name = 'dsa_swa_sink_hybrid_step'

def layer_norm(x, g, b):
    xf = x.astype(jnp.float32)
    mu = jnp.mean(xf, axis=-1, keepdims=True)
    var = jnp.mean(jnp.square(xf - mu), axis=-1, keepdims=True)
    y = (xf - mu) * lax.rsqrt(var + LN_EPS) * g.astype(jnp.float32) + b.astype(jnp.float32)
    return y.astype(x.dtype)

def post_norm(x, sub, g, b):
    return layer_norm(ALPHA * x + sub, g, b)

def squared_relu_mlp(x, w1, w2):
    h = jax.nn.relu(x @ w1)
    return (h * h) @ w2

def t5_bias(table, dist):
    n = jnp.maximum(dist, 0)
    max_exact = N_BUCKETS // 2
    nf = jnp.maximum(n, max_exact).astype(jnp.float32)
    large = max_exact + (jnp.log(nf / max_exact) / math.log(MAX_DISTANCE / max_exact) * (N_BUCKETS - max_exact)).astype(jnp.int32)
    large = jnp.minimum(large, N_BUCKETS - 1)
    bucket = jnp.where(n < max_exact, n, large)
    return table.astype(jnp.float32)[bucket]

def dsa_attend(q, qi, wi, q_pos, idx_keys, gather_kv, topk, table):
    B, Q = q.shape[0], q.shape[1]
    L = idx_keys.shape[1]
    s = jnp.einsum('bqhe,bse->bqhs', qi.astype(jnp.float32), idx_keys.astype(jnp.float32))
    score = jnp.einsum('bqhs,bqh->bqs', jax.nn.relu(s), wi.astype(jnp.float32)) * IDX_SCALE
    admissible = jnp.arange(L, dtype=jnp.int32)[None, :] <= q_pos[:, None]
    score = jnp.where(admissible[None], score, NEG)
    _, idx = lax.top_k(score, topk)
    valid = idx <= q_pos[None, :, None]
    k_sel, v_sel = gather_kv(idx)
    qg = q.reshape(B, Q, KV_HEADS_A, G_A, HEAD_DIM)
    logits = jnp.einsum('bqgrd,bqkgd->bqgrk', qg, k_sel).astype(jnp.float32) * ATTN_SCALE
    bias = t5_bias(table, q_pos[None, :, None] - idx)
    bias = bias.reshape(B, Q, topk, KV_HEADS_A, G_A).transpose(0, 1, 3, 4, 2)
    logits = jnp.where(valid[:, :, None, None, :], logits + bias, NEG)
    p = jax.nn.softmax(logits, axis=-1).astype(v_sel.dtype)
    out = jnp.einsum('bqgrk,bqkgd->bqgrd', p, v_sel)
    return out.reshape(B, Q, N_HEADS * HEAD_DIM)

def a_project(x, w_in, idx_g, idx_b):
    B, S, _ = x.shape
    q, k, v, qi, ki, wi = jnp.split(x @ w_in, A_SPLIT_POINTS, axis=-1)
    q = q.reshape(B, S, N_HEADS, HEAD_DIM)
    k = k.reshape(B, S, KV_HEADS_A, HEAD_DIM)
    v = v.reshape(B, S, KV_HEADS_A, HEAD_DIM)
    qi = qi.reshape(B, S, IDX_HEADS, IDX_DIM)
    ki = layer_norm(ki, idx_g, idx_b)
    return q, k, v, qi, ki, wi

def mixer_a_prompt(x, w_in, w_out, idx_g, idx_b, table):
    B, S, _ = x.shape
    q, k, v, qi, ki, wi = a_project(x, w_in, idx_g, idx_b)
    topk = min(TOPK_MAX, S // 4)
    nb = S // Q_BLOCK
    take = jax.vmap(lambda rows, ids: rows[ids])

    def gather_kv(idx):
        return take(k, idx), take(v, idx)

    def to_blocks(a):
        return a.reshape(B, nb, Q_BLOCK, *a.shape[2:]).swapaxes(0, 1)

    def one_block(args):
        n, qb, qib, wib = args
        q_pos = n * Q_BLOCK + jnp.arange(Q_BLOCK, dtype=jnp.int32)
        return dsa_attend(qb, qib, wib, q_pos, ki, gather_kv, topk, table)

    out = lax.map(one_block, (jnp.arange(nb, dtype=jnp.int32), to_blocks(q), to_blocks(qi), to_blocks(wi)))
    out = out.swapaxes(0, 1).reshape(B, S, N_HEADS * HEAD_DIM)
    return out @ w_out, k, v, ki

def mixer_a_sample(x, layer, cache_k, cache_v, cache_idx_k, page_table, w_in, w_out, idx_g, idx_b, table):
    DB, DS, _ = x.shape
    q, k, v, qi, ki, wi = a_project(x, w_in, idx_g, idx_b)
    past = page_table.shape[1] * PAGE_SIZE
    past_ki = cache_idx_k[layer, page_table].reshape(DB, past, IDX_DIM)
    keys_ki = jnp.concatenate([past_ki, ki.astype(past_ki.dtype)], axis=1)
    topk = min(TOPK_MAX, (past + DS) // 4)
    take = jax.vmap(lambda rows, ids: rows[ids])

    def gather_kv(idx):
        from_past = (idx < past)[..., None, None]
        pi = jnp.minimum(idx, past - 1)
        phys = take(page_table, pi // PAGE_SIZE)
        off = pi % PAGE_SIZE
        ni = jnp.clip(idx - past, 0, DS - 1)
        k_sel = jnp.where(from_past, cache_k[layer, phys, off], take(k, ni).astype(cache_k.dtype))
        v_sel = jnp.where(from_past, cache_v[layer, phys, off], take(v, ni).astype(cache_v.dtype))
        return k_sel, v_sel

    q_pos = past + jnp.arange(DS, dtype=jnp.int32)
    out = dsa_attend(q, qi, wi, q_pos, keys_ki, gather_kv, topk, table)
    return out @ w_out, k, v, ki

def sink_softmax(logits, sink):
    s = jnp.broadcast_to(sink.astype(jnp.float32).reshape(KV_HEADS_B, G_B, 1, 1), logits.shape[:-1] + (1,))
    return jax.nn.softmax(jnp.concatenate([logits, s], axis=-1), axis=-1)[..., :-1]

def b_project(x, w_in):
    B, S, _ = x.shape
    q, k, v = jnp.split(x @ w_in, B_SPLIT_POINTS, axis=-1)
    return (q.reshape(B, S, N_HEADS, HEAD_DIM), k.reshape(B, S, KV_HEADS_B, HEAD_DIM), v.reshape(B, S, KV_HEADS_B, HEAD_DIM))

def mixer_b_prompt(x, w_in, w_out, sink, table):
    B, S, _ = x.shape
    q, k, v = b_project(x, w_in)
    W = WINDOW
    nb = S // W
    qb = q.reshape(B, nb, W, KV_HEADS_B, G_B, HEAD_DIM)

    def band(a):
        ab = a.reshape(B, nb, W, KV_HEADS_B, HEAD_DIM)
        prev = jnp.pad(ab, ((0, 0), (1, 0), (0, 0), (0, 0), (0, 0)))[:, :-1]
        return jnp.concatenate([prev, ab], axis=2)

    keys, vals = band(k), band(v)
    logits = jnp.einsum('bnqgrd,bnkgd->bngrqk', qb, keys).astype(jnp.float32) * ATTN_SCALE
    i = jnp.arange(W, dtype=jnp.int32)
    j = jnp.arange(2 * W, dtype=jnp.int32)
    dist = i[:, None] + W - j[None, :]
    in_window = (dist >= 0) & (dist < WINDOW)
    key_pos = jnp.arange(nb, dtype=jnp.int32)[:, None] * W - W + j[None, :]
    mask = in_window[None] & (key_pos >= 0)[:, None, :]
    bias = t5_bias(table, dist).reshape(W, 2 * W, KV_HEADS_B, G_B).transpose(2, 3, 0, 1)
    logits = jnp.where(mask[None, :, None, None], logits + bias[None, None], NEG)
    p = sink_softmax(logits, sink).astype(vals.dtype)
    out = jnp.einsum('bngrqk,bnkgd->bnqgrd', p, vals).reshape(B, S, N_HEADS * HEAD_DIM)
    wb = min(WINDOW, S)
    return out @ w_out, k[:, S - wb:], v[:, S - wb:]

def mixer_b_sample(x, win_k, win_v, w_in, w_out, sink, table):
    DB, DS, _ = x.shape
    q, k, v = b_project(x, w_in)
    wb = win_k.shape[1]
    keys = jnp.concatenate([win_k, k.astype(win_k.dtype)], axis=1)
    vals = jnp.concatenate([win_v, v.astype(win_v.dtype)], axis=1)
    key_pos = PAST_LEN - wb + jnp.arange(wb + DS, dtype=jnp.int32)
    q_pos = PAST_LEN + jnp.arange(DS, dtype=jnp.int32)
    dist = q_pos[:, None] - key_pos[None, :]
    mask = (dist >= 0) & (dist < WINDOW)
    qg = q.reshape(DB, DS, KV_HEADS_B, G_B, HEAD_DIM)
    logits = jnp.einsum('bqgrd,bkgd->bgrqk', qg, keys).astype(jnp.float32) * ATTN_SCALE
    bias = t5_bias(table, dist).reshape(DS, wb + DS, KV_HEADS_B, G_B).transpose(2, 3, 0, 1)
    logits = jnp.where(mask[None, None, None], logits + bias[None], NEG)
    p = sink_softmax(logits, sink).astype(vals.dtype)
    out = jnp.einsum('bgrqk,bkgd->bqgrd', p, vals).reshape(DB, DS, N_HEADS * HEAD_DIM)
    return out @ w_out, keys[:, -wb:], vals[:, -wb:]

def setup_inputs(seed: int = 0) -> dict:
    key = jax.random.key(seed)
    ks = jax.random.split(key, 24)
    nrm = jax.random.normal
    n_pages = PAST_LEN // PAGE_SIZE
    n_used = DEC_BATCH * n_pages
    n_pool = n_used + n_used // 4
    wb = min(WINDOW, PAST_LEN)
    x_prompt = nrm(ks[0], (BATCH, SEQ, D_MODEL), jnp.float32)
    x_sample = nrm(ks[1], (DEC_BATCH, DEC_SEQ, D_MODEL), jnp.float32)
    cache_k = nrm(ks[2], (N_A_LAYERS, n_pool, PAGE_SIZE, KV_HEADS_A, HEAD_DIM), jnp.float32)
    cache_v = nrm(ks[3], (N_A_LAYERS, n_pool, PAGE_SIZE, KV_HEADS_A, HEAD_DIM), jnp.float32)
    cache_idx_k = nrm(ks[4], (N_A_LAYERS, n_pool, PAGE_SIZE, IDX_DIM), jnp.float32)
    state_win_k = nrm(ks[5], (N_B_LAYERS, DEC_BATCH, wb, KV_HEADS_B, HEAD_DIM), jnp.float32)
    state_win_v = nrm(ks[6], (N_B_LAYERS, DEC_BATCH, wb, KV_HEADS_B, HEAD_DIM), jnp.float32)
    page_table = jax.random.permutation(ks[7], n_pool)[:n_used].reshape(DEC_BATCH, n_pages).astype(jnp.int32)
    rel_bias_table = 0.1 * nrm(ks[8], (N_BUCKETS, N_HEADS), jnp.float32)
    a_col_scale = jnp.concatenate([jnp.ones((A_SIZES[0] + A_SIZES[1],), jnp.float32), jnp.full((A_SIZES[2],), BETA, jnp.float32), jnp.ones((sum(A_SIZES[3:]),), jnp.float32)])
    a_w_in = nrm(ks[9], (N_A_LAYERS, D_MODEL, A_IN), jnp.float32) * D_MODEL ** -0.5 * a_col_scale
    a_w_out = nrm(ks[10], (N_A_LAYERS, N_HEADS * HEAD_DIM, D_MODEL), jnp.float32) * (N_HEADS * HEAD_DIM) ** -0.5 * BETA
    a_idx_ln_g = 1.0 + 0.02 * nrm(ks[11], (N_A_LAYERS, IDX_DIM), jnp.float32)
    a_idx_ln_b = 0.02 * nrm(ks[12], (N_A_LAYERS, IDX_DIM), jnp.float32)
    b_col_scale = jnp.concatenate([jnp.ones((B_SIZES[0] + B_SIZES[1],), jnp.float32), jnp.full((B_SIZES[2],), BETA, jnp.float32)])
    b_w_in = nrm(ks[13], (N_B_LAYERS, D_MODEL, B_IN), jnp.float32) * D_MODEL ** -0.5 * b_col_scale
    b_w_out = nrm(ks[14], (N_B_LAYERS, N_HEADS * HEAD_DIM, D_MODEL), jnp.float32) * (N_HEADS * HEAD_DIM) ** -0.5 * BETA
    b_sink = nrm(ks[15], (N_B_LAYERS, N_HEADS), jnp.float32)
    ln1_g = 1.0 + 0.02 * nrm(ks[16], (DEPTH, D_MODEL), jnp.float32)
    ln1_b = 0.02 * nrm(ks[17], (DEPTH, D_MODEL), jnp.float32)
    ln2_g = 1.0 + 0.02 * nrm(ks[18], (DEPTH, D_MODEL), jnp.float32)
    ln2_b = 0.02 * nrm(ks[19], (DEPTH, D_MODEL), jnp.float32)
    mlp_w1 = nrm(ks[20], (DEPTH, D_MODEL, D_FF), jnp.float32) * D_MODEL ** -0.5 * BETA
    mlp_w2 = nrm(ks[21], (DEPTH, D_FF, D_MODEL), jnp.float32) * D_FF ** -0.5 * BETA
    return {'x_prompt': x_prompt, 'x_sample': x_sample, 'cache_k': cache_k, 'cache_v': cache_v, 'cache_idx_k': cache_idx_k, 'state_win_k': state_win_k, 'state_win_v': state_win_v, 'page_table': page_table, 'rel_bias_table': rel_bias_table, 'a_w_in': a_w_in, 'a_w_out': a_w_out, 'a_idx_ln_g': a_idx_ln_g, 'a_idx_ln_b': a_idx_ln_b, 'b_w_in': b_w_in, 'b_w_out': b_w_out, 'b_sink': b_sink, 'ln1_g': ln1_g, 'ln1_b': ln1_b, 'ln2_g': ln2_g, 'ln2_b': ln2_b, 'mlp_w1': mlp_w1, 'mlp_w2': mlp_w2}

def reference(x_prompt, x_sample, cache_k, cache_v, cache_idx_k, state_win_k, state_win_v, page_table, rel_bias_table, a_w_in, a_w_out, a_idx_ln_g, a_idx_ln_b, b_w_in, b_w_out, b_sink, ln1_g, ln1_b, ln2_g, ln2_b, mlp_w1, mlp_w2):
    B, S, _ = x_prompt.shape
    y_p, y_s = x_prompt, x_sample
    kp, vp, ikp, ks_, vs_, iks = [], [], [], [], [], []
    wkp, wvp, wks, wvs = [], [], [], []
    for i in range(DEPTH):
        j = i // 2
        if i % 2 == 0:
            m_p, k_p, v_p, ik_p = mixer_a_prompt(y_p, a_w_in[j], a_w_out[j], a_idx_ln_g[j], a_idx_ln_b[j], rel_bias_table)
            m_s, k_s, v_s, ik_s = mixer_a_sample(y_s, j, cache_k, cache_v, cache_idx_k, page_table, a_w_in[j], a_w_out[j], a_idx_ln_g[j], a_idx_ln_b[j], rel_bias_table)
            kp.append(k_p.reshape(B, S // PAGE_SIZE, PAGE_SIZE, KV_HEADS_A, HEAD_DIM))
            vp.append(v_p.reshape(B, S // PAGE_SIZE, PAGE_SIZE, KV_HEADS_A, HEAD_DIM))
            ikp.append(ik_p.reshape(B, S // PAGE_SIZE, PAGE_SIZE, IDX_DIM))
            ks_.append(k_s)
            vs_.append(v_s)
            iks.append(ik_s)
        else:
            m_p, wk_p, wv_p = mixer_b_prompt(y_p, b_w_in[j], b_w_out[j], b_sink[j], rel_bias_table)
            m_s, wk_s, wv_s = mixer_b_sample(y_s, state_win_k[j], state_win_v[j], b_w_in[j], b_w_out[j], b_sink[j], rel_bias_table)
            wkp.append(wk_p)
            wvp.append(wv_p)
            wks.append(wk_s)
            wvs.append(wv_s)
        y_p = post_norm(y_p, m_p, ln1_g[i], ln1_b[i])
        y_s = post_norm(y_s, m_s, ln1_g[i], ln1_b[i])
        y_p = post_norm(y_p, squared_relu_mlp(y_p, mlp_w1[i], mlp_w2[i]), ln2_g[i], ln2_b[i])
        y_s = post_norm(y_s, squared_relu_mlp(y_s, mlp_w1[i], mlp_w2[i]), ln2_g[i], ln2_b[i])
    return (y_p, y_s, jnp.stack(kp), jnp.stack(vp), jnp.stack(ikp), jnp.stack(ks_), jnp.stack(vs_), jnp.stack(iks), jnp.stack(wkp), jnp.stack(wvp), jnp.stack(wks), jnp.stack(wvs))


_drawn_inputs = setup_inputs


def setup_inputs(seed=0):
    import zlib

    import numpy as np

    out = dict(_drawn_inputs(seed))
    spreads = {}
    factors = {'rel_bias_table': 8.0, 'a_idx_ln_b': 3.118, 'b_sink': 8.0}
    for name, (base, spread) in spreads.items():
        noise = np.random.default_rng([zlib.crc32(name.encode()), seed]).standard_normal(out[name].shape)
        drawn = base * np.exp(spread * noise) if base else spread * noise
        out[name] = __import__('jax').numpy.asarray(drawn.astype(out[name].dtype))
    for name, factor in factors.items():
        out[name] = (out[name] * factor).astype(out[name].dtype)
    return out
```

```python
from contextlib import ExitStack
import math

import numpy as np

import concourse.bass as bass
from concourse import mybir

F32 = mybir.dt.float32
F32R = mybir.dt.float32r
I32 = mybir.dt.int32
ALU = mybir.AluOpType
ACT = mybir.ActivationFunctionType
AXX = mybir.AxisListType.X

P = 128
D = 1024
KT = D // P
SEQ, DB = 512, 8
TOK = SEQ + DB
TG = TOK // 2
NH, HD = 16, 64
PAST, PAGE = 1024, 128
NPG = PAST // PAGE
POOL_PAGES = 80
IDXH = 8
TOPK_P, TOPK_S = 128, 256
NB_, MAXD = 32, 128
ALPHA = (2 * 2) ** 0.25
NEG = -1e30
TAKEN = -3.0e38
EPS = 1e-5
QSCALE = HD ** -0.5
ISCALE = IDXH ** -0.5 * HD ** -0.5
QT = SEQ // P
NATW = HD + IDXH + 256
PAIRS = NH // 2

A_IN, A_OUT, MLP0, B_IN, B_OUT, MLP1, U_END = 0, 14, 22, 86, 96, 104, 168
CHUNKS = 4
SKEW = 768
POOL_LO = 16


def a_heads(p):
    return 8 * (p // 4) + p % 4, 8 * (p // 4) + p % 4 + 4


def b_heads(p):
    return p, p + 8


def bucket(dist):
    n = np.maximum(np.asarray(dist), 0)
    exact = NB_ // 2
    nf = np.maximum(n, exact).astype(np.float32)
    large = exact + (np.log(nf / np.float32(exact)) / np.float32(math.log(MAXD / exact))
                     * np.float32(NB_ - exact)).astype(np.int32)
    return np.where(n < exact, n, np.minimum(large, NB_ - 1))


def one_hot(dist):
    return (np.arange(NB_)[:, None] == bucket(dist)[None, :]).astype(np.float32)


C_ID, C_ONE, C_CAUS, C_WIN, C_WD, C_REP, C_END = 0, 128, 256, 384, 640, 704, 832
H_SEQ, H_DEC, H_WIN, H_END = 0, 640, 640 + 1025, 640 + 1025 + 128


def constants():
    c = np.zeros((P, C_END), np.float32)
    i, j = np.arange(P)[:, None], np.arange(P)[None, :]
    c[:, C_ID:C_ID + P] = np.eye(P)
    c[:, C_ONE:C_ONE + P] = 1.0 / D
    c[:, C_CAUS:C_CAUS + P] = np.where(j <= i, 0.0, NEG)
    dist = i + P - np.arange(2 * P)[None, :]
    c[:, C_WIN:C_WIN + 2 * P] = np.where((dist >= 0) & (dist < P), 0.0, NEG)
    for b in range(DB):
        c[b, C_WD + 8 * b:C_WD + 8 * b + 8] = 1.0
        c[b, C_REP + NH * b:C_REP + NH * b + NH] = 1.0
    h = np.concatenate([one_hot(511 - np.arange(640)), one_hot(PAST - np.arange(PAST + 1)),
                        one_hot(P - 1 - np.arange(P))], axis=1)
    return c, np.ascontiguousarray(h)


def program(nc, io):
    with ExitStack() as ctx:
        words = [0]
        base = nc.sbuf_base
        usable = nc.sbuf_usable_end

        def place(name, shape, dt=F32, at=None):
            n = int(np.prod(shape[1:]))
            if at is None:
                at = words[0]
                words[0] += (n + 7) // 8 * 8
            off = (base + 31) // 32 * 32 + 4 * at
            assert off + 4 * n <= usable, (name, off + 4 * n, usable)
            return nc.alloc_sbuf_tensor_at(name, shape, dt, offset=off)

        def sem(name):
            return ctx.enter_context(nc.semaphore(name))

        UQ = place("UQ", [P, 14, TOK])
        YA = place("YA", [P, KT, TOK], at=6 * TOK)
        SEQS = place("SEQS", [16, 640], at=12 * TOK)
        X32 = place("X32", [P, KT, TOK])
        xw = words[0]
        XH = place("XH", [P, KT, TOK], F32R)
        XL = place("XL", [P, KT, TOK], F32R)
        KVR = place("KVR", [P, 3, NPG, 256], at=xw)
        VNEW = place("VNEW", [1, DB, 256], at=xw + 3 * 2048)
        hw = words[0]
        HH = place("HH", [P, KT, TOK], F32R)
        HL = place("HL", [P, KT, TOK], F32R)
        SQ = place("SQ", [P, KT, TOK], at=hw)
        IK = place("IK", [P, 4, 1025], at=hw)
        SR = place("SR", [HD, 1025], at=hw + 4104)
        QB = place("QB", [P, 2176], at=hw + 4104 + 1032)
        PB = place("PB", [P, 2, 2, 512], at=hw)
        PTB = place("PTB", [P, 2, 2, 512], at=hw + 2048)
        PD = place("PD", [P, 1025], at=hw + 4096)
        KW = place("KW", [P, DB, 129], at=hw + 6304)
        BT = place("BT", [P, NH, 512])
        WRAW = place("WRAW", [P, 2, KT, P])
        WHI = place("WHI", [P, 2, KT, P], F32R)
        WLO = place("WLO", [P, 2, KT, P], F32R)
        rw = words[0]
        RL = place("RL", [P, TOK])
        S32 = place("S32", [P, TOK])
        PTD = place("PTD", [P, NPG, P], at=rw)
        NAT = place("NAT", [P, 5, NATW])
        KID = place("KID", [P, 5, 2, HD])
        KIT = place("KIT", [P, TOK])
        DS = place("DS", [DB, 1025])
        ww = words[0]
        WN = place("WN", [P, KT, NATW])
        SC = place("SC", [P, 3, 512], at=ww)
        RS = place("RS", [P, 2, 512], at=ww + 1536)
        VW = place("VW", [P, DB, P], at=ww)
        CST = place("CST", [P, C_END])
        CH = place("CH", [NB_, H_END - 640])
        CHS = place("CHS", [NB_, 640], at=11 * TOK - 120)
        TAB = place("TAB", [NB_, 16])
        TREP = place("TREP", [NB_, P])
        LNP = place("LNP", [P, 4, 2, KT])
        IGB = place("IGB", [P, 2, HD])
        SNK = place("SNK", [P, NH])
        SND = place("SND", [P, 1])
        WB = place("WB", [HD, DB])
        WD = place("WD", [DB, HD])
        PT = place("PT", [1, 64], I32)
        EPSC = place("EPSC", [P, 1])
        KST = place("KST", [P, 5, 6])
        KMV = place("KMV", [P, 5, 2])
        KSD = place("KSD", [P, 5])
        MX8 = place("MX8", [P, 8])
        MX = place("MX", [P, 2, 2])
        NMX = place("NMX", [P, 2, 2])
        SM = place("SM", [P, 2, 2])
        SKE = place("SKE", [P, 2, 2])
        DST = place("DST", [P, 4])
        PNEW = place("PNEW", [1, P])
        RSTD = place("RSTD", [P, TOK], at=None)

        ident = CST[:, C_ID:C_ID + P]
        ones = CST[:, C_ONE:C_ONE + P]
        caus = CST[:, C_CAUS:C_CAUS + P]
        ohd = CH[:, 0:1025]
        ohw = CH[:, 1025:1025 + P]

        PS = ctx.enter_context(nc.psum_tensor("PS", [P, 8, 512], F32))
        PSF = PS[:].rearrange("p a b -> p (a b)")
        bskew = nc.dram_tensor("bias_skewed", [P, NH, SKEW], F32, kind="Internal").ap()
        bseq = nc.dram_tensor("bias_seq", [16, 640], F32, kind="Internal").ap()

        x_in, wn_in, cst_in = sem("x_in"), sem("wn_in"), sem("cst_in")
        pt_in = sem("pt_in")
        raw_in = [sem("raw_in0"), sem("raw_in1")]
        idx_in = sem("idx_in")
        kv_in = [sem(f"kv_in{i}") for i in range(3)]
        vnew_in = sem("vnew_in")
        toe_out, toe_skew, toe_in = sem("toe_out"), sem("toe_skew"), sem("toe_in")
        win_in, vwin_in = sem("win_in"), sem("vwin_in")
        outs = sem("outs")
        hi_done = sem("hi_done")
        lo_pool, lo_dve = sem("lo_pool"), sem("lo_dve")
        unit_done = sem("unit_done")
        ev_act, ev_dve = sem("ev_act"), sem("ev_dve")
        relu_done = sem("relu_done")
        hh_done, hl_done = sem("hh_done"), sem("hl_done")
        x_hi, x_lo = sem("x_hi"), sem("x_lo")
        nat_mm, nat_ev = sem("nat_mm"), sem("nat_ev")
        kstat, ksd, kid = sem("kstat"), sem("ksd"), sem("kid")
        kit_mm, kit_ev = sem("kit_mm"), sem("kit_ev")
        seq_mm, seq_ev = sem("seq_mm"), sem("seq_ev")
        is_mm, is_relu, is_acc = sem("is_mm"), sem("is_relu"), sem("is_acc")
        qib_ready, ikn_ready = sem("qib_ready"), sem("ikn_ready")
        ds_mm, ds_relu, ds_sum, ds_ev = sem("ds_mm"), sem("ds_relu"), sem("ds_sum"), sem("ds_ev")
        wd_ready, wb_mm, wb_ev = sem("wd_ready"), sem("wb_mm"), sem("wb_ev")
        top_p, top_s = sem("top_p"), sem("top_s")
        qb_ready = sem("qb_ready")
        kv_used = sem("kv_used")
        dl_mm, d_mx, d_exp, d_p = sem("dl_mm"), sem("d_mx"), sem("d_exp"), sem("d_p")
        dt_mm, dt_ev, do_mm, do_hi, do_lo = (sem("dt_mm"), sem("dt_ev"), sem("do_mm"),
                                             sem("do_hi"), sem("do_lo"))
        qk_mm, smx, pexp, pnorm = sem("qk_mm"), sem("smx"), sem("pexp"), sem("pnorm")
        xbias = sem("xbias")
        pt_mm, pt_ev_a, pt_ev_v = sem("pt_mm"), sem("pt_ev_a"), sem("pt_ev_v")
        o_mm, o_hi, o_lo = sem("o_mm"), sem("o_hi"), sem("o_lo")
        mean_mm, dev, sqr, var_mm, std_d, x_new = (sem("mean_mm"), sem("dev"), sem("sqr"),
                                                   sem("var_mm"), sem("std_d"), sem("x_new"))
        ya_init = sem("ya_init")
        z_nat, z_qb, bwin = sem("z_nat"), sem("z_qb"), sem("bwin")
        vt_mm, vt_ev = sem("vt_mm"), sem("vt_ev")
        own = sem("own")
        own_p = sem("own_p")

        block = ctx.enter_context(nc.Block())

        @block.sync
        def _(sp):
            def load_unit(u, slot):
                sp.dma_start(WRAW[:, slot, :, :].rearrange("p k m -> p (k m)"),
                             io["wall"][bass.ds(u, 1), :, :].rearrange("o p n -> (o p) n")
                             ).then_inc(raw_in[slot], 16)

            sp.dma_start(PT[:], io["pt"]).then_inc(pt_in, 16)
            sp.dma_start(WN[:], io["wn"]).then_inc(wn_in, 16)
            sp.dma_start(X32[:], io["xT"]).then_inc(x_in, 16)
            for dst, src in ((CST[:], io["cst"]), (CH[:], io["csth"][:, 640:]),
                             (CHS[:], io["csth"][:, 0:640]), (TAB[:], io["table"]),
                             (TREP[:], io["trep"]), (LNP[:], io["lnp"]), (IGB[:], io["igb"]),
                             (SNK[:], io["snk"]), (SND[:], io["snd"])):
                sp.dma_start(dst, src).then_inc(cst_in, 16)
            load_unit(0, 0)
            load_unit(1, 1)
            sp.wait_ge(seq_ev, 1)
            sp.dma_start(bseq, SEQS[:]).then_inc(toe_out, 16)
            sp.wait_ge(toe_out, 16)
            sp.dma_start(bass.AP(tensor=bskew.tensor, offset=0,
                                 ap=[[NH * SKEW + 1, P], [SKEW, NH], [1, 640]]),
                         bass.AP(tensor=bseq.tensor, offset=0,
                                 ap=[[0, P], [640, NH], [1, 640]])).then_inc(toe_skew, 16)
            sp.wait_ge(toe_skew, 16)
            sp.dma_start(BT[:], bskew[:, :, 127:127 + 512]).then_inc(toe_in, 16)
            for u in range(2, 4):
                sp.wait_ge(lo_pool, u - 1)
                load_unit(u, u % 2)
            with sp.Fori(2, (POOL_LO + 2) // 2) as i:
                for s in range(2):
                    sp.wait_ge(lo_pool, i * 2 + (s - 1))
                    load_unit(i * 2 + s, s)
            with sp.Fori((POOL_LO + 2) // 2, (U_END + 2) // 2) as i:
                for s in range(2):
                    sp.wait_ge(lo_dve, i * 2 + (s - 1 - POOL_LO))
                    load_unit(i * 2 + s, s)
            for g in range(2):
                sp.wait_ge(x_new, 6 + g + 1)
                c = slice(TG * g, TG * g + TG)
                sp.dma_start(io["yT"][:, :, c], X32[:, :, c]).then_inc(outs, 16)
            sp.wait_ge(outs, 16 * 11)

        @block.gpsimd
        def _(pool):
            nc.gpsimd.memset(NAT[:, 4, :], 0.0).then_inc(z_nat, 1)
            nc.gpsimd.memset(QB[:], 0.0).then_inc(z_qb, 1)
            pool.wait_ge(pt_in, 16)
            for half in range(2):
                with pool.Fori(0, 4) as c:
                    for pg in range(NPG):
                        page = pool.value_load(PT[0:1, bass.ds(c * 16 + (8 * half + pg), 1)],
                                               min_val=0, max_val=POOL_PAGES - 1)
                        pool.dma_start(
                            IK[HD * half:HD * half + HD, bass.ds(c, 1), pg * P:(pg + 1) * P],
                            io["cacheI"][bass.ds(page, 1), :, :].rearrange("o d k -> d o k")
                        ).then_inc(idx_in, 16)

            def low_part(u, slot):
                pool.wait_ge(hi_done, u + 1)
                nc.gpsimd.tensor_tensor(WLO[:, slot], WRAW[:, slot], WHI[:, slot].bitcast(F32),
                                        ALU.subtract).then_inc(lo_pool, 1)

            for u in range(2):
                low_part(u, u)
            with pool.Fori(1, POOL_LO // 2) as i:
                for s in range(2):
                    low_part(i * 2 + s, s)

            pool.wait_ge(unit_done, A_OUT)
            pool.wait_ge(nat_ev, 5)
            for b in range(DB):
                pool.dma_start(VNEW[0:1, b, :], NAT[b:b + 1, 4, HD + IDXH:NATW]
                               ).then_inc(vnew_in, 16)
            for n in range(2 * DB):
                cache = io["cacheK"] if n < DB else io["cacheV"]
                b, slot = n % DB, n % 3
                if n >= 3:
                    pool.wait_ge(kv_used, n - 2)
                with pool.Fori(0, NPG) as pg:
                    page = pool.value_load(PT[0:1, bass.ds(pg + b * NPG, 1)],
                                           min_val=0, max_val=POOL_PAGES - 1)
                    pool.dma_start(KVR[:, slot, bass.ds(pg, 1), :].rearrange("p o n -> p (o n)"),
                                   cache[bass.ds(page, 1), :, :].rearrange("o p n -> (o p) n")
                                   ).then_inc(kv_in[slot], 16)
            for layer in range(2):
                for g in range(2):
                    pool.wait_ge(x_new, 4 * layer + g + 1)
                    c = slice(TG * g, TG * g + TG)
                    nc.gpsimd.tensor_scalar(YA[:, :, c], X32[:, :, c], float(ALPHA), None,
                                            ALU.mult).then_inc(ya_init, 1)
                if layer == 0:
                    for h in range(NH):
                        nc.gpsimd.tensor_tensor(BT[:, h, 256:512], BT[:, h, 256:512],
                                                CST[:, C_WIN:C_WIN + 2 * P], ALU.add
                                                ).then_inc(bwin, 1)
                    pool.wait_ge(var_mm, 4)
                    pool.dma_start(KW[:, :, 0:P], io["swk"]).then_inc(win_in, 16)
                    pool.dma_start(VW[0:P - 1, :, :],
                                   io["swv"][:, 1:P, :].rearrange("b k d -> k b d")
                                   ).then_inc(win_in, 16)
                    pool.wait_ge(vt_ev, 5)
                    for b in range(DB):
                        pool.dma_start(VW[P - 1:P, b, :], NAT[b:b + 1, 4, 0:P]
                                       ).then_inc(vwin_in, 16)
                    nc.gpsimd.memset(QB[:, 0:DB * 144], 0.0).then_inc(z_qb, 1)

        @block.tensor
        def _(pe):
            def unit(u, slot, hi, lo, waits=None):
                for k in range(KT):
                    if waits and k in waits:
                        waits[k]()
                    for w, parts in ((WHI, (hi, lo)), (WLO, (hi,))):
                        for x in parts:
                            for g in range(2):
                                mm = pe.matmul(PS[:, 2 * slot + g, 0:TG], w[:, slot, k, :],
                                               x[:, k, TG * g:TG * g + TG],
                                               start=(k == 0 and w is WHI and x is hi),
                                               stop=(k == KT - 1 and w is WLO))
                mm.then_inc(unit_done, 1)

            def wait_lo(u):
                if u < POOL_LO:
                    pe.wait_ge(lo_pool, u + 1)
                else:
                    pe.wait_ge(lo_dve, u + 1 - POOL_LO)

            def layer_norm_sums(n, ev_base):
                for k in range(KT):
                    if ev_base is not None:
                        pe.wait_ge(ev_dve, ev_base + k + 1)
                    for g in range(2):
                        mm = pe.matmul(PS[:, 4 + g, 0:TG], ones, YA[:, k, TG * g:TG * g + TG],
                                       start=(k == 0), stop=(k == KT - 1))
                mm.then_inc(mean_mm, 1)
                for g in range(2):
                    for k in range(KT):
                        if k % 4 == 0:
                            pe.wait_ge(sqr, 4 * n + 2 * g + k // 4 + 1)
                        mm = pe.matmul(PS[:, 6 + g, 0:TG], ones, SQ[:, k, TG * g:TG * g + TG],
                                       start=(k == 0), stop=(k == KT - 1))
                    mm.then_inc(var_mm, 1)

            def mlp(base, ev_base):
                with pe.Fori(0, CHUNKS) as c:
                    with pe.Fori(0, 4) as i:
                        for s in range(2):
                            j = c * 16 + i * 2 + s
                            pe.wait_ge(lo_dve, j + (base + 1 - POOL_LO))
                            pe.wait_ge(ev_dve, j + (ev_base - 1))
                            unit(None, s, XH, XL)
                    for s in range(2):
                        j = c * 16 + 8 + s
                        pe.wait_ge(lo_dve, j + (base + 1 - POOL_LO))
                        pe.wait_ge(ev_dve, j + (ev_base - 1))
                        hbase = 0 if base == MLP0 else 32
                        waits = {k: (lambda k=k: pe.wait_ge(hl_done, c * 8 + (hbase + k + 1)))
                                 for k in (5, 6, 7)} if s == 0 else None
                        if s == 0:
                            waits[0] = lambda: pe.wait_ge(hl_done, c * 8 + (hbase + 5))
                        unit(None, s, HH, HL, waits)
                    with pe.Fori(1, 4) as i:
                        for s in range(2):
                            j = c * 16 + i * 2 + (8 + s)
                            pe.wait_ge(lo_dve, j + (base + 1 - POOL_LO))
                            pe.wait_ge(ev_dve, j + (ev_base - 1))
                            unit(None, s, HH, HL)

            def prompt_attention(n0, heads, ktile, vtile, blocks):
                its = [(t, p) for t in range(QT) for p in range(PAIRS)]

                def logits(i):
                    t, p = its[i]
                    n = n0 + i
                    lo_, hi_ = blocks(t)
                    if i >= 2:
                        pe.wait_ge(smx, n - 1)
                    for e in range(2):
                        r = slice(HD * e, HD * e + HD)
                        mm = pe.matmul(PS[:, 2 * (i % 2) + e, 0:(hi_ - lo_) * P],
                                       UQ[r, 6 + p, t * P:(t + 1) * P],
                                       UQ[r, ktile(p), lo_ * P:hi_ * P], start=True, stop=True)
                    mm.then_inc(qk_mm, 1)

                def turn(i):
                    t, p = its[i]
                    n = n0 + i
                    lo_, hi_ = blocks(t)
                    pe.wait_ge(pnorm, n + 1)
                    if n >= 1:
                        pe.wait_ge(pt_ev_a, n)
                        pe.wait_ge(pt_ev_v, n)
                    for e in range(2):
                        for kb in range(hi_ - lo_):
                            mm = pe.transpose(PS[:, 4 + e, kb * P:(kb + 1) * P],
                                              PB[:, i % 2, e, kb * P:(kb + 1) * P], ident)
                    mm.then_inc(pt_mm, 1)

                def output(i):
                    t, p = its[i]
                    n = n0 + i
                    lo_, hi_ = blocks(t)
                    pe.wait_ge(pt_ev_a, n + 1)
                    pe.wait_ge(pt_ev_v, n + 1)
                    if n >= 2:
                        pe.wait_ge(o_lo, n - 1)
                    for e in range(2):
                        for kb in range(hi_ - lo_):
                            mm = pe.matmul(PS[HD * e:HD * e + HD, 6 + i % 2, 0:P],
                                           vtile(lo_ + kb, p, e),
                                           PTB[:, i % 2, e, kb * P:(kb + 1) * P],
                                           start=(kb == 0), stop=(kb == hi_ - lo_ - 1))
                    mm.then_inc(o_mm, 1)

                N = len(its)
                logits(0)
                for i in range(N + 1):
                    if i + 1 < N:
                        logits(i + 1)
                    if i < N:
                        turn(i)
                    if i >= 1:
                        output(i - 1)

            pe.wait_ge(x_in, 16)
            pe.wait_ge(wn_in, 16)
            for t in range(5):
                m = P if t < QT else DB
                for k in range(KT):
                    mm = pe.matmul(PS[0:m, t, 0:NATW], X32[:, k, t * P:t * P + m], WN[:, k, :],
                                   start=(k == 0), stop=(k == KT - 1))
                mm.then_inc(nat_mm, 1)
            pe.wait_ge(cst_in, 16 * 9)
            pe.matmul(PS[0:16, 6, 0:512], TAB[:], CHS[:, 0:512], start=True, stop=True)
            pe.matmul(PS[0:16, 7, 0:P], TAB[:], CHS[:, 512:640], start=True, stop=True
                      ).then_inc(seq_mm, 1)
            pe.wait_ge(nat_ev, 5)
            pe.wait_ge(x_lo, 1)
            items = [(t, h) for t in range(1, QT) for h in range(IDXH)]
            for u in range(8):
                if u == 2:
                    pe.wait_ge(kid, 1)
                    for t in range(QT):
                        pe.transpose(PS[:, 4, t * P:(t + 1) * P],
                                     KID[:, t, :, :].rearrange("p a d -> p (a d)"), ident)
                    pe.transpose(PS[:, 5, 0:DB], KID[0:DB, 4, :, :].rearrange("p a d -> p (a d)"),
                                 CST[0:DB, 0:DB])
                    pe.wait_ge(wd_ready, 1)
                    pe.wait_ge(seq_ev, 1)
                    pe.transpose(PS[0:HD, 6, 0:DB], WD[:], CST[0:DB, 0:DB]).then_inc(kit_mm, 1)
                if u >= 4:
                    for n in range(6 * (u - 4), 6 * (u - 4) + 6):
                        t, h = items[n]
                        if n == 0:
                            pe.wait_ge(kit_ev, 2)
                            pe.wait_ge(wb_ev, 1)
                            pe.wait_ge(ev_act, 4)
                        if n >= 4:
                            pe.wait_ge(is_relu, n - 3)
                        r = slice(HD * (h % 2), HD * (h % 2) + HD)
                        pe.matmul(PS[:, 4 + n % 4, 0:(t + 1) * P],
                                  UQ[r, h // 2, t * P:(t + 1) * P], KIT[r, 0:(t + 1) * P],
                                  start=True, stop=True).then_inc(is_mm, 1)
                wait_lo(u)
                if u >= 2:
                    pe.wait_ge(ev_act, u - 1)
                unit(u, u % 2, XH, XL)
            pe.wait_ge(is_relu, 24)
            pe.wait_ge(qib_ready, 1)
            pe.wait_ge(ikn_ready, 1)
            for c0, c1 in ((0, 512), (512, 1024), (1024, 1025)):
                for c in range(4):
                    mm = pe.matmul(PSF[0:HD, 2048 + c0:2048 + c1], QB[:, HD * c:HD * c + HD],
                                   IK[:, c, c0:c1], start=(c == 0), stop=(c == 3))
            mm.then_inc(ds_mm, 1)
            with pe.Fori(4, A_OUT // 2) as i:
                for s in range(2):
                    pe.wait_ge(lo_pool, i * 2 + (s + 1))
                    pe.wait_ge(ev_act, i * 2 + (s - 1))
                    unit(None, s, XH, XL)
            pe.wait_ge(ds_relu, 1)
            pe.wait_ge(wb_ev, 1)
            for c0, c1 in ((0, 512), (512, 1024), (1024, 1025)):
                mm = pe.matmul(PSF[0:DB, 2048 + c0:2048 + c1], WB[:], SR[:, c0:c1],
                               start=True, stop=True)
            mm.then_inc(ds_sum, 1)

            pe.wait_ge(ev_act, A_OUT)
            pe.wait_ge(qb_ready, 1)
            spans = ((0, 512), (512, 1024), (1024, 1025))
            for c0, c1 in spans:
                pe.matmul(PSF[:, c0:c1], TREP[:], ohd[:, c0:c1], start=True, stop=False)
            for b in range(DB):
                pe.wait_ge(kv_in[b % 3], 16 * NPG * (b // 3 + 1))
                for gp in range(2):
                    q = QB[:, (2 * b + gp) * P:(2 * b + gp + 1) * P]
                    for half in range(2):
                        mm = pe.matmul(PSF[:, 512 * half:512 * half + 512], q,
                                       KVR[:, b % 3, 4 * half:4 * half + 4, gp * P:(gp + 1) * P],
                                       start=False, stop=False)
                    pe.matmul(PSF[:, 1024:1025], q, UQ[:, 4 + gp, SEQ + b:SEQ + b + 1],
                              start=False, stop=False)
                mm.then_inc(kv_used, 1)
            pe.wait_ge(top_s, 1)
            for c0, c1 in spans:
                mm = pe.matmul(PSF[:, c0:c1], CST[0:DB, C_REP:C_REP + P], DS[:, c0:c1],
                               start=False, stop=True)
            mm.then_inc(dl_mm, 1)
            pe.wait_ge(d_p, 1)
            pe.wait_ge(ds_ev, 1)
            for k in range(NPG):
                pe.transpose(PS[:, 4 + k // 4, (k % 4) * P:(k % 4 + 1) * P],
                             PD[:, k * P:(k + 1) * P], ident)
            pe.transpose(PS[0:1, 6, 0:P], PD[:, 1024:1025], ident).then_inc(dt_mm, 1)
            pe.wait_ge(dt_ev, 1)
            pe.wait_ge(vnew_in, 16 * DB)
            for b in range(DB):
                n = DB + b
                pe.wait_ge(kv_in[n % 3], 16 * NPG * (n // 3 + 1))
                for gp in range(2):
                    o = PS[:, 7, (2 * b + gp) * 8:(2 * b + gp) * 8 + 8]
                    col = NH * b + 8 * gp
                    for k in range(NPG):
                        mm = pe.matmul(o, KVR[:, n % 3, k, gp * P:(gp + 1) * P],
                                       PTD[:, k, col:col + 8], start=(k == 0), stop=False)
                    last = pe.matmul(o, VNEW[0:1, b, gp * P:(gp + 1) * P], PNEW[0:1, col:col + 8],
                                     start=False, stop=True)
                mm.then_inc(kv_used, 1)
            last.then_inc(do_mm, 1)
            pe.wait_ge(do_lo, 1)
            pe.wait_ge(toe_in, 16)
            prompt_attention(0, a_heads, lambda p: 4 + p // 4,
                             lambda kb, p, e: NAT[:, kb, 72 + HD * (2 * (p // 4) + e):
                                                  72 + HD * (2 * (p // 4) + e) + HD],
                             lambda t: (0, t + 1))
            pe.wait_ge(o_lo, 32)
            for s in range(2):
                pe.wait_ge(lo_pool, A_OUT + s + 1)
                unit(None, s, XH, XL)
            with pe.Fori(1, 4) as i:
                for s in range(2):
                    pe.wait_ge(lo_dve, i * 2 + (A_OUT + s + 1 - POOL_LO))
                    pe.wait_ge(ev_dve, i * 2 + (s - 1))
                    unit(None, s, XH, XL)
            layer_norm_sums(0, 0)
            pe.wait_ge(x_lo, 3)
            mlp(MLP0, 8)
            layer_norm_sums(1, 8 + 64 - 8)
            pe.wait_ge(x_lo, 5)
            with pe.Fori(0, 5) as i:
                for s in range(2):
                    pe.wait_ge(lo_dve, i * 2 + (B_IN + s + 1 - POOL_LO))
                    pe.wait_ge(ev_act, i * 2 + (A_OUT + s - 1))
                    unit(None, s, XH, XL)
            pe.wait_ge(ev_act, A_OUT + 10)
            for t in range(QT):
                pe.transpose(PS[:, 4, t * P:(t + 1) * P], UQ[:, 5, t * P:(t + 1) * P], ident)
            pe.transpose(PS[0:DB, 5, 0:P], UQ[:, 5, SEQ:TOK], ident).then_inc(vt_mm, 1)
            pe.wait_ge(qb_ready, 2)
            pe.wait_ge(win_in, 32)
            pe.matmul(PS[:, 0, 0:P], TREP[:], ohw, start=True, stop=False)
            for b in range(DB):
                mm = pe.matmul(PS[:, 0, 0:P], QB[:, b * P:(b + 1) * P], KW[:, b, 1:129],
                               start=False, stop=(b == DB - 1))
            mm.then_inc(dl_mm, 1)
            pe.wait_ge(d_p, 2)
            pe.wait_ge(vt_ev, 5)
            pe.transpose(PS[:, 4, 0:P], PD[:, 0:P], ident).then_inc(dt_mm, 1)
            pe.wait_ge(dt_ev, 2)
            pe.wait_ge(vwin_in, 16 * DB)
            for b in range(DB):
                mm = pe.matmul(PS[:, 7, b * NH:(b + 1) * NH], VW[:, b, :],
                               PTD[:, 0, b * NH:(b + 1) * NH], start=True, stop=True)
            mm.then_inc(do_mm, 1)
            pe.wait_ge(do_lo, 2)
            prompt_attention(32, b_heads, lambda p: 4,
                             lambda kb, p, e: NAT[:, kb, HD * e:HD * e + HD],
                             lambda t: (max(t - 1, 0), t + 1))
            pe.wait_ge(o_lo, 64)
            with pe.Fori(0, 4) as i:
                for s in range(2):
                    pe.wait_ge(lo_dve, i * 2 + (B_OUT + s + 1 - POOL_LO))
                    pe.wait_ge(ev_dve, i * 2 + (72 + s - 1))
                    unit(None, s, XH, XL)
            layer_norm_sums(2, 72)
            pe.wait_ge(x_lo, 7)
            mlp(MLP1, 80)
            layer_norm_sums(3, 80 + 64 - 8)

        @block.scalar
        def _(act):
            def high_part(u, slot, static=True):
                if isinstance(u, int):
                    act.wait_ge(raw_in[slot], 16 * (u // 2 + 1))
                    if u >= 2:
                        act.wait_ge(unit_done, u - 1)
                nc.scalar.activation(WHI[:, slot], WRAW[:, slot], ACT.Copy).then_inc(hi_done, 1)

            def banks(slot):
                return PS[:, 2 * slot:2 * slot + 2, 0:TG]

            def mlp(base, ev_base):
                with act.Fori(0, CHUNKS) as c:
                    with act.Fori(0, 4) as i:
                        for s in range(2):
                            j = c * 16 + i * 2 + s
                            act.wait_ge(unit_done, j + (base + 1))
                            nc.scalar.activation(RL[:].rearrange("p (g t) -> p g t", g=2),
                                                 banks(s), ACT.Relu).then_inc(relu_done, 1)
                            act.wait_ge(ev_dve, j + (ev_base + 1))
                            nc.scalar.activation(HH[:, bass.ds(i * 2 + s, 1), :],
                                                 S32[:].rearrange("p (o t) -> p o t", o=1),
                                                 ACT.Copy).then_inc(hh_done, 1)
                            act.wait_ge(raw_in[s], (c * 8 + i + (base // 2 + 2)) * 16)
                            high_part(None, s)
                    with act.Fori(4, 8) as i:
                        for s in range(2):
                            j = c * 16 + i * 2 + s
                            act.wait_ge(unit_done, j + (base + 1))
                            act.wait_ge(raw_in[s], (c * 8 + i + (base // 2 + 2)) * 16)
                            high_part(None, s)

            def layer_norm(n, last):
                for g in range(2):
                    c = slice(TG * g, TG * g + TG)
                    for q in range(2):
                        act.wait_ge(dev, 4 * n + 2 * g + q + 1)
                        nc.scalar.activation(SQ[:, 4 * q:4 * q + 4, c], YA[:, 4 * q:4 * q + 4, c],
                                             ACT.Square).then_inc(sqr, 1)
                for g in range(2):
                    c = slice(TG * g, TG * g + TG)
                    act.wait_ge(var_mm, 2 * n + g + 1)
                    nc.scalar.activation(RSTD[:, c], PS[:, 6 + g, 0:TG], ACT.Sqrt,
                                         bias=EPSC[:]).then_inc(std_d, 1)
                if not last:
                    for g in range(2):
                        c = slice(TG * g, TG * g + TG)
                        act.wait_ge(x_new, 2 * n + g + 1)
                        nc.scalar.activation(XH[:, :, c], X32[:, :, c], ACT.Copy).then_inc(x_hi, 1)

            def prompt_attention(n0, heads, blocks, sink):
                its = [(t, p) for t in range(QT) for p in range(PAIRS)]

                def exps(i):
                    t, p = its[i]
                    n = n0 + i
                    w = (blocks(t)[1] - blocks(t)[0]) * P
                    act.wait_ge(smx, n + 1)
                    for e in range(2):
                        ins = nc.scalar.activation(PB[:, i % 2, e, 0:w], PB[:, i % 2, e, 0:w],
                                                   ACT.Exp, bias=NMX[:, i % 2, e:e + 1],
                                                   accum_out=SM[:, i % 2, e:e + 1])
                    if sink:
                        ins = nc.scalar.activation(SKE[:, i % 2, :], SKE[:, i % 2, :], ACT.Exp)
                    ins.then_inc(pexp, 1)

                def turned(i):
                    t, p = its[i]
                    n = n0 + i
                    w = (blocks(t)[1] - blocks(t)[0]) * P
                    act.wait_ge(pt_mm, n + 1)
                    nc.scalar.activation(PTB[:, i % 2, 0, 0:w], PS[:, 4, 0:w], ACT.Copy
                                         ).then_inc(pt_ev_a, 1)

                def out_high(i):
                    t, p = its[i]
                    act.wait_ge(o_mm, n0 + i + 1)
                    nc.scalar.activation(XH[:, p, t * P:(t + 1) * P], PS[:, 6 + i % 2, 0:P],
                                         ACT.Copy).then_inc(o_hi, 1)

                N = len(its)
                exps(0)
                for i in range(N + 1):
                    if i + 1 < N:
                        exps(i + 1)
                    if i < N:
                        turned(i)
                    if i >= 1:
                        out_high(i - 1)

            act.wait_ge(x_in, 16)
            nc.scalar.activation(XH[:], X32[:], ACT.Copy).then_inc(x_hi, 1)
            high_part(0, 0)
            high_part(1, 1)
            act.wait_ge(z_nat, 1)
            for t in range(5):
                m = P if t < QT else DB
                act.wait_ge(nat_mm, t + 1)
                nc.scalar.activation(NAT[0:m, t, :], PS[0:m, t, 0:NATW], ACT.Copy
                                     ).then_inc(nat_ev, 1)
            act.wait_ge(seq_mm, 1)
            nc.scalar.activation(SEQS[:], PSF[0:16, 3072:3072 + 640], ACT.Copy
                                 ).then_inc(seq_ev, 1)
            act.wait_ge(kstat, 1)
            nc.scalar.activation(KSD[:], KMV[:, :, 1], ACT.Sqrt, bias=EPSC[:]).then_inc(ksd, 1)
            items = [(t, h) for t in range(1, QT) for h in range(IDXH)]
            for u in range(8):
                if u >= 4:
                    for n in range(6 * (u - 4), 6 * (u - 4) + 6):
                        t, h = items[n]
                        act.wait_ge(is_mm, n + 1)
                        if n >= 2:
                            act.wait_ge(is_acc, n - 1)
                        nc.scalar.activation(RS[:, n % 2, 0:(t + 1) * P],
                                             PS[:, 4 + n % 4, 0:(t + 1) * P], ACT.Relu
                                             ).then_inc(is_relu, 1)
                act.wait_ge(unit_done, u + 1)
                high_part(u + 2, u % 2)
                if u < 6:
                    nc.scalar.activation(UQ[:, u, :].rearrange("p (g t) -> p g t", g=2),
                                         banks(u % 2), ACT.Copy).then_inc(ev_act, 1)
                else:
                    nc.scalar.activation(UQ[:, u, :].rearrange("p (g t) -> p g t", g=2),
                                         banks(u % 2), ACT.Copy, scale=QSCALE
                                         ).then_inc(ev_act, 1)
                if u == 2:
                    act.wait_ge(kit_mm, 1)
                    nc.scalar.activation(KIT[:, 0:512], PS[:, 4, :], ACT.Copy
                                         ).then_inc(kit_ev, 1)
                    nc.scalar.activation(KIT[:, 512:520], PS[:, 5, 0:DB], ACT.Copy
                                         ).then_inc(kit_ev, 1)
                    nc.scalar.activation(WB[:], PS[0:HD, 6, 0:DB], ACT.Copy).then_inc(wb_ev, 1)
                if u == 6:
                    act.wait_ge(nat_ev, 5)
                    act.dma_start(io["vp"], NAT[:, 0:QT, HD + IDXH:NATW]).then_inc(outs, 16)
                    act.dma_start(io["vs"], NAT[0:DB, 4, HD + IDXH:NATW]).then_inc(outs, 16)
                    act.wait_ge(kid, 1)
                    act.dma_start(io["kip"], KID[:, 0:QT, 0, :]).then_inc(outs, 16)
                    act.dma_start(io["kis"], KID[0:DB, 4, 0, :]).then_inc(outs, 16)
                    act.wait_ge(ev_act, 6)
                    act.dma_start(io["kT"], UQ[:, 4:6, :]).then_inc(outs, 16)
            act.wait_ge(ds_mm, 1)
            nc.scalar.activation(SR[:], PSF[0:HD, 2048:2048 + 1025], ACT.Relu
                                 ).then_inc(ds_relu, 1)

            act.wait_ge(toe_out, 16)
            with act.Fori(4, A_OUT // 2) as i:
                for s in range(2):
                    act.wait_ge(unit_done, i * 2 + (s + 1))
                    act.wait_ge(raw_in[s], (i + 2) * 16)
                    high_part(None, s)
                    nc.scalar.activation(
                        UQ[:, bass.ds(i * 2 + s, 1), :].rearrange("p o (g t) -> p (o g) t", g=2),
                        banks(s), ACT.Copy, scale=QSCALE).then_inc(ev_act, 1)

            act.wait_ge(d_mx, 1)
            nc.scalar.activation(PD[:], PSF[:, 0:1025], ACT.Exp, bias=DST[:, 1:2],
                                 accum_out=DST[:, 2:3]).then_inc(d_exp, 1)
            act.wait_ge(dt_mm, 1)
            nc.scalar.activation(PTD[:].rearrange("p k r -> p (k r)"), PSF[:, 2048:2048 + 1024],
                                 ACT.Copy)
            nc.scalar.activation(PNEW[:], PS[0:1, 6, 0:P], ACT.Copy).then_inc(dt_ev, 1)
            act.wait_ge(do_mm, 1)
            for gp in range(2):
                for e in range(2):
                    r = slice(HD * e, HD * e + HD)
                    src = PS[r, 7, 0:P].rearrange("p (b g j) -> p g j b", b=DB, g=2)
                    ins = nc.scalar.activation(XH[r, 4 * gp:4 * gp + 4, SEQ:TOK],
                                               src[:, gp, 4 * e:4 * e + 4, :], ACT.Copy)
            ins.then_inc(do_hi, 1)
            prompt_attention(0, a_heads, lambda t: (0, t + 1), False)
            with act.Fori(0, 4) as i:
                for s in range(2):
                    act.wait_ge(unit_done, i * 2 + (A_OUT + s + 1))
                    act.wait_ge(raw_in[s], (i + (A_OUT // 2 + 2)) * 16)
                    high_part(None, s)
            layer_norm(0, False)
            mlp(MLP0, 8)
            layer_norm(1, False)
            for s in range(2):
                act.wait_ge(unit_done, B_IN + s + 1)
                high_part(B_IN + 2 + s, s)
                if s == 0:
                    act.wait_ge(outs, 16 * 5)
                nc.scalar.activation(UQ[:, 4 + s, :].rearrange("p (g t) -> p g t", g=2),
                                     banks(s), ACT.Copy).then_inc(ev_act, 1)
            with act.Fori(1, 5) as i:
                for s in range(2):
                    act.wait_ge(unit_done, i * 2 + (B_IN + s + 1))
                    act.wait_ge(raw_in[s], (i + (B_IN // 2 + 2)) * 16)
                    high_part(None, s)
                    nc.scalar.activation(
                        UQ[:, bass.ds(i * 2 + (4 + s), 1), :].rearrange(
                            "p o (g t) -> p (o g) t", g=2),
                        banks(s), ACT.Copy, scale=QSCALE).then_inc(ev_act, 1)
            act.wait_ge(vt_mm, 1)
            for t in range(QT):
                nc.scalar.activation(NAT[:, t, 0:P], PS[:, 4, t * P:(t + 1) * P], ACT.Copy
                                     ).then_inc(vt_ev, 1)
            nc.scalar.activation(NAT[0:DB, 4, 0:P], PS[0:DB, 5, 0:P], ACT.Copy).then_inc(vt_ev, 1)
            act.wait_ge(vt_ev, 5)
            act.dma_start(io["wkT"], UQ[:, 4, SEQ - P:SEQ]).then_inc(outs, 16)
            act.dma_start(io["wv"], NAT[:, QT - 1, 0:P]).then_inc(outs, 16)
            act.wait_ge(qb_ready, 2)
            act.dma_start(io["wksT"], KW[:, :, 1:P + 1]).then_inc(outs, 16)
            act.wait_ge(vwin_in, 16 * DB)
            act.wait_ge(win_in, 32)
            act.dma_start(io["wvs"], VW[:]).then_inc(outs, 16)
            act.wait_ge(d_mx, 2)
            nc.scalar.activation(DST[:, 3:4], SND[:], ACT.Exp, bias=DST[:, 1:2])
            nc.scalar.activation(PD[:, 0:P], PS[:, 0, 0:P], ACT.Exp, bias=DST[:, 1:2],
                                 accum_out=DST[:, 2:3]).then_inc(d_exp, 1)
            act.wait_ge(dt_mm, 2)
            nc.scalar.activation(PTD[:, 0, :], PS[:, 4, 0:P], ACT.Copy).then_inc(dt_ev, 1)
            act.wait_ge(do_mm, 2)
            for e in range(2):
                r = slice(HD * e, HD * e + HD)
                src = PS[r, 7, 0:P].rearrange("p (b j) -> p j b", b=DB)
                ins = nc.scalar.activation(XH[r, :, SEQ:TOK], src[:, 8 * e:8 * e + 8, :], ACT.Copy)
            ins.then_inc(do_hi, 1)
            prompt_attention(32, b_heads, lambda t: (max(t - 1, 0), t + 1), True)
            with act.Fori(0, 4) as i:
                for s in range(2):
                    act.wait_ge(unit_done, i * 2 + (B_OUT + s + 1))
                    act.wait_ge(raw_in[s], (i + (B_OUT // 2 + 2)) * 16)
                    high_part(None, s)
            layer_norm(2, False)
            mlp(MLP1, 80)
            layer_norm(3, True)

        @block.vector
        def _(dve):
            V = nc.vector
            count = [0]

            def after(ins):
                count[0] += 1
                ins.then_inc(own, 1)
                dve.wait_ge(own, count[0])

            def low_part(u, slot):
                if isinstance(u, int):
                    dve.wait_ge(hi_done, u + 1)
                V.tensor_tensor(WLO[:, slot], WRAW[:, slot], WHI[:, slot].bitcast(F32),
                                ALU.subtract).then_inc(lo_dve, 1)

            def banks(slot):
                return PS[:, 2 * slot:2 * slot + 2, 0:TG]

            def add_residual(i, s):
                m = bass.ds(i * 2 + s, 1)
                V.scalar_tensor_tensor(
                    out=YA[:, m, :].rearrange("p o (g t) -> p (o g) t", g=2),
                    in0=X32[:, m, :].rearrange("p o (g t) -> p (o g) t", g=2),
                    scalar=float(ALPHA), in1=banks(s), op0=ALU.mult, op1=ALU.add
                ).then_inc(ev_dve, 1)

            def mlp(base, ev_base):
                sq0 = 0 if base == MLP0 else 32
                with dve.Fori(0, CHUNKS) as c:
                    with dve.Fori(0, 4) as i:
                        for s in range(2):
                            dve.wait_ge(lo_dve, c * 16 + i * 2 + (base + s + 2 - POOL_LO))
                            dve.wait_ge(relu_done, c * 8 + i * 2 + (sq0 + s + 1))
                            V.tensor_tensor(S32[:].rearrange("p (g t) -> p g t", g=2),
                                            RL[:].rearrange("p (g t) -> p g t", g=2),
                                            banks(s), ALU.mult
                                            ).then_inc(ev_dve, 1)
                            dve.wait_ge(hh_done, c * 8 + i * 2 + (sq0 + s + 1))
                            m = bass.ds(i * 2 + s, 1)
                            V.tensor_tensor(HL[:, m, :],
                                            S32[:].rearrange("p (o t) -> p o t", o=1),
                                            HH[:, m, :].bitcast(F32), ALU.subtract
                                            ).then_inc(hl_done, 1)
                            dve.wait_ge(hi_done, c * 16 + i * 2 + (base + s + 3))
                            low_part(None, s)
                    with dve.Fori(0, 4) as i:
                        for s in range(2):
                            dve.wait_ge(hi_done, c * 16 + i * 2 + (base + s + 11))
                            low_part(None, s)
                            dve.wait_ge(unit_done, c * 16 + i * 2 + (base + s + 9))
                            m = bass.ds(i * 2 + s, 1)
                            ya = YA[:, m, :].rearrange("p o (g t) -> p (o g) t", g=2)
                            V.tensor_tensor(ya, ya, banks(s), ALU.add).then_inc(ev_dve, 1)

            def layer_norm(n, ln, last):
                dve.wait_ge(mean_mm, n + 1)
                for g in range(2):
                    c = slice(TG * g, TG * g + TG)
                    for q in range(2):
                        y = YA[:, 4 * q:4 * q + 4, c]
                        V.tensor_tensor(y, y, PS[:, 4 + g:5 + g, 0:TG].broadcast_to([P, 4, TG]),
                                        ALU.subtract).then_inc(dev, 1)
                for g in range(2):
                    c = slice(TG * g, TG * g + TG)
                    dve.wait_ge(std_d, 2 * n + g + 1)
                    after(V.reciprocal(RSTD[:, c], RSTD[:, c]))
                    for q in range(2):
                        y = YA[:, 4 * q:4 * q + 4, c]
                        r = RSTD[:, c].rearrange("p (o t) -> p o t", o=1).broadcast_to([P, 4, TG])
                        ins = V.tensor_tensor(y, y, r, ALU.mult)
                        after(ins)
                    for k in range(KT):
                        ins = V.tensor_scalar(X32[:, k, c], YA[:, k, c], LNP[:, ln, 0, k:k + 1],
                                              LNP[:, ln, 1, k:k + 1], ALU.mult, ALU.add)
                    ins.then_inc(x_new, 1)
                    if not last and g == 1:
                        pass
                if not last:
                    for g in range(2):
                        c = slice(TG * g, TG * g + TG)
                        dve.wait_ge(x_hi, 1 + 2 * n + g + 1)
                        V.tensor_tensor(XL[:, :, c], X32[:, :, c], XH[:, :, c].bitcast(F32),
                                        ALU.subtract).then_inc(x_lo, 1)

            def prompt_attention(n0, heads, blocks, sink):
                its = [(t, p) for t in range(QT) for p in range(PAIRS)]

                def softmax_in(i):
                    t, p = its[i]
                    n = n0 + i
                    lo_, hi_ = blocks(t)
                    w = (hi_ - lo_) * P
                    dve.wait_ge(qk_mm, n + 1)
                    if n >= 2:
                        dve.wait_ge(pt_mm, n - 1)
                    for e in range(2):
                        h = heads(p)[e]
                        x = PB[:, i % 2, e, 0:w]
                        off = 384 - t * P + lo_ * P
                        bt = BT[:, h, off:off + w]
                        lg = PS[:, 2 * (i % 2) + e, 0:w]
                        if sink:
                            ins = V.tensor_tensor_reduce(out=x, in0=lg, in1=bt, scale=1.0, scalar=TAKEN,
                                                         op0=ALU.add, op1=ALU.max,
                                                         accum_out=MX[:, i % 2, e:e + 1])
                        else:
                            after(V.tensor_tensor(x, lg, bt, ALU.add))
                            mk = caus if t == 0 else SC[:, t - 1, 0:w]
                            ins = V.tensor_tensor_reduce(out=x, in0=x, in1=mk, scale=1.0,
                                                         scalar=TAKEN, op0=ALU.add, op1=ALU.max,
                                                         accum_out=MX[:, i % 2, e:e + 1])
                    after(ins)
                    if sink:
                        sk = SNK[:].rearrange("p (e j) -> p e j", e=2)[:, :, p]
                        after(V.tensor_tensor(MX[:, i % 2, :], MX[:, i % 2, :], sk, ALU.max))
                        V.tensor_tensor(SKE[:, i % 2, :], sk, MX[:, i % 2, :], ALU.subtract)
                    V.tensor_scalar(NMX[:, i % 2, :], MX[:, i % 2, :], -1.0, None, ALU.mult
                                    ).then_inc(smx, 1)

                def normalise(i):
                    t, p = its[i]
                    w = (blocks(t)[1] - blocks(t)[0]) * P
                    dve.wait_ge(pexp, n0 + i + 1)
                    if sink:
                        after(V.tensor_tensor(SM[:, i % 2, :], SM[:, i % 2, :], SKE[:, i % 2, :],
                                              ALU.add))
                    after(V.reciprocal(SM[:, i % 2, :], SM[:, i % 2, :]))
                    for e in range(2):
                        x = PB[:, i % 2, e, 0:w]
                        ins = V.tensor_scalar(x, x, SM[:, i % 2, e:e + 1], None, ALU.mult)
                    ins.then_inc(pnorm, 1)

                def turned(i):
                    t, p = its[i]
                    w = (blocks(t)[1] - blocks(t)[0]) * P
                    dve.wait_ge(pt_mm, n0 + i + 1)
                    V.tensor_copy(PTB[:, i % 2, 1, 0:w], PS[:, 5, 0:w]).then_inc(pt_ev_v, 1)

                def out_low(i):
                    t, p = its[i]
                    dve.wait_ge(o_hi, n0 + i + 1)
                    c = slice(t * P, (t + 1) * P)
                    V.tensor_tensor(XL[:, p, c], PS[:, 6 + i % 2, 0:P], XH[:, p, c].bitcast(F32),
                                    ALU.subtract).then_inc(o_lo, 1)

                N = len(its)
                softmax_in(0)
                for i in range(N + 1):
                    if i < N:
                        normalise(i)
                    if i + 1 < N:
                        softmax_in(i + 1)
                    if i < N:
                        turned(i)
                    if i >= 1:
                        out_low(i - 1)

            V.memset(EPSC[:], EPS).then_inc(own, 1)
            count[0] += 1
            dve.wait_ge(x_hi, 1)
            V.tensor_tensor(XL[:], X32[:], XH[:].bitcast(F32), ALU.subtract).then_inc(x_lo, 1)
            dve.wait_ge(nat_ev, 5)
            dve.wait_ge(cst_in, 16 * 9)
            V.tensor_tensor(WD[:].rearrange("p (b h) -> p b h", b=DB),
                            NAT[0:DB, 4:5, HD:HD + IDXH].broadcast_to([DB, DB, IDXH]),
                            CST[0:DB, C_WD:C_WD + HD].rearrange("p (b h) -> p b h", b=DB),
                            ALU.mult).then_inc(wd_ready, 1)
            for t in range(5):
                ins = V.bn_stats(KST[:, t, :], NAT[:, t, 0:HD])
            after(ins)
            for t in range(5):
                ins = V.bn_aggr(KMV[:, t, :], KST[:, t, :])
            ins.then_inc(kstat, 1)
            dve.wait_ge(kstat, 1)
            dve.wait_ge(ksd, 1)
            after(V.reciprocal(KSD[:], KSD[:]))
            z = KID[:, :, 0, :]

            def over_d(ap):
                return ap.rearrange("p (t o) -> p t o", o=1).broadcast_to([P, 5, HD])

            def over_t(ap):
                return ap.rearrange("p (o d) -> p o d", o=1).broadcast_to([P, 5, HD])

            after(V.tensor_tensor(z, NAT[:, :, 0:HD], over_d(KMV[:, :, 0]), ALU.subtract))
            after(V.tensor_tensor(z, z, over_d(KSD[:]), ALU.mult))
            after(V.tensor_tensor(z, z, over_t(IGB[:, 0, :]), ALU.mult))
            after(V.tensor_tensor(z, z, over_t(IGB[:, 1, :]), ALU.add))
            V.tensor_copy(KID[:, :, 1, :], z).then_inc(kid, 1)
            dve.wait_ge(kit_ev, 2)
            dve.wait_ge(idx_in, 16 * 64)
            for half in range(2):
                r = slice(HD * half, HD * half + HD)
                ins = V.tensor_copy(
                    IK[r, :, 1024:1025],
                    KIT[r, SEQ:TOK].rearrange("p (c s) -> p c s", s=2)[:, :, half:half + 1])
            ins.then_inc(ikn_ready, 1)
            dve.wait_ge(z_qb, 1)
            dve.wait_ge(ev_act, 4)
            qv = QB[:, 0:320].rearrange("p (c x) -> p c x", x=80)
            for half in range(2):
                for par in range(2):
                    src = UQ[HD * par:HD * par + HD, 0:4, SEQ:TOK].rearrange(
                        "p f (c s) -> p c s f", s=2)
                    ins = V.tensor_copy(qv[HD * half:HD * half + HD, :, 8 * half + par:
                                           8 * half + par + 8:2][:, :, 0:4], src[:, :, half, :])
            ins.then_inc(qib_ready, 1)
            items = [(t, h) for t in range(1, QT) for h in range(IDXH)]
            for n, (t, h) in enumerate(items):
                dve.wait_ge(is_relu, n + 1)
                w = (t + 1) * P
                wi = NAT[:, t, HD + h:HD + h + 1]
                if h == 0:
                    ins = V.tensor_scalar(SC[:, t - 1, 0:w], RS[:, n % 2, 0:w], wi, None, ALU.mult)
                else:
                    ins = V.scalar_tensor_tensor(out=SC[:, t - 1, 0:w], in0=RS[:, n % 2, 0:w],
                                                 scalar=wi, in1=SC[:, t - 1, 0:w],
                                                 op0=ALU.mult, op1=ALU.add)
                ins.then_inc(is_acc, 1)
                dve.wait_ge(is_acc, n + 1)
            for t in range(1, QT):
                V.tensor_scalar(SC[:, t - 1, 0:t * P], SC[:, t - 1, 0:t * P], float(ISCALE), None,
                                ALU.mult)
                d = SC[:, t - 1, t * P:(t + 1) * P]
                after(V.scalar_tensor_tensor(out=d, in0=d, scalar=float(ISCALE), in1=caus,
                                             op0=ALU.mult, op1=ALU.add))

            def take_top(sc, rows, k):
                for _ in range(k // 8):
                    after(V.max(MX8[0:rows, :], sc))
                    after(V.match_replace(sc, MX8[0:rows, :], sc, TAKEN))
                return V.tensor_scalar(sc, sc, -2.0e38, NEG, ALU.is_gt, ALU.mult)

            for t in range(1, QT):
                after(take_top(SC[:, t - 1, 0:(t + 1) * P], P, TOPK_P))
            dve.wait_ge(ds_sum, 1)
            V.tensor_scalar(DS[:], PSF[0:DB, 2048:2048 + 1025], float(ISCALE), None, ALU.mult
                            ).then_inc(ds_ev, 1)
            dve.wait_ge(ev_act, A_OUT)
            dve.wait_ge(ds_mm, 1)
            after(V.memset(QB[:], 0.0))
            qv = QB[:].rearrange("p (b x) -> p b x", x=272)
            for gp in range(2):
                for e in range(2):
                    r = slice(HD * e, HD * e + HD)
                    o = gp * 136 + 4 * e
                    src = UQ[r, 6 + 4 * gp:10 + 4 * gp, SEQ:TOK].rearrange("p j b -> p b j")
                    ins = V.tensor_copy(qv[r, :, o:o + 4], src)
            ins.then_inc(qb_ready, 1)
            dve.wait_ge(ds_ev, 1)
            take_top(DS[:], DB, TOPK_S).then_inc(top_s, 1)

            def sample_softmax(n, logits, w, sink):
                dve.wait_ge(dl_mm, n)
                after(V.tensor_reduce(DST[:, 0:1], logits, AXX, ALU.max))
                if sink:
                    after(V.tensor_tensor(DST[:, 0:1], DST[:, 0:1], SND[:], ALU.max))
                V.tensor_scalar(DST[:, 1:2], DST[:, 0:1], -1.0, None, ALU.mult).then_inc(d_mx, 1)
                dve.wait_ge(d_exp, n)
                if sink:
                    after(V.tensor_tensor(DST[:, 2:3], DST[:, 2:3], DST[:, 3:4], ALU.add))
                after(V.reciprocal(DST[:, 2:3], DST[:, 2:3]))
                V.tensor_scalar(PD[:, 0:w], PD[:, 0:w], DST[:, 2:3], None, ALU.mult
                                ).then_inc(d_p, 1)

            sample_softmax(1, PSF[:, 0:1025], 1025, False)
            dve.wait_ge(do_hi, 1)
            for gp in range(2):
                for e in range(2):
                    r = slice(HD * e, HD * e + HD)
                    src = PS[r, 7, 0:P].rearrange("p (b g j) -> p g j b", b=DB, g=2)
                    m = slice(4 * gp, 4 * gp + 4)
                    ins = V.tensor_tensor(XL[r, m, SEQ:TOK], src[:, gp, 4 * e:4 * e + 4, :],
                                          XH[r, m, SEQ:TOK].bitcast(F32), ALU.subtract)
            ins.then_inc(do_lo, 1)
            dve.wait_ge(toe_in, 16)
            prompt_attention(0, a_heads, lambda t: (0, t + 1), False)
            with dve.Fori(0, 4) as i:
                for s in range(2):
                    dve.wait_ge(hi_done, i * 2 + (A_OUT + s + 3))
                    low_part(None, s)
                    dve.wait_ge(unit_done, i * 2 + (A_OUT + s + 1))
                    add_residual(i, s)
            layer_norm(0, 0, False)
            dve.wait_ge(ya_init, 2)
            mlp(MLP0, 8)
            layer_norm(1, 1, False)
            with dve.Fori(0, 5) as i:
                for s in range(2):
                    dve.wait_ge(hi_done, i * 2 + (B_IN + s + 3))
                    low_part(None, s)
            dve.wait_ge(ev_act, A_OUT + 10)
            dve.wait_ge(win_in, 32)
            V.tensor_copy(KW[:, :, P:P + 1],
                          UQ[:, 4, SEQ:TOK].rearrange("p (b o) -> p b o", o=1))
            dve.wait_ge(z_qb, 2)
            qv = QB[:, 0:DB * 144].rearrange("p (b x) -> p b x", x=144)
            for e in range(2):
                r = slice(HD * e, HD * e + HD)
                ins = V.tensor_copy(qv[r, :, 8 * e:8 * e + 8],
                                    UQ[r, 6:14, SEQ:TOK].rearrange("p j b -> p b j"))
            ins.then_inc(qb_ready, 1)
            sample_softmax(2, PS[:, 0, 0:P], P, True)
            dve.wait_ge(do_hi, 2)
            for e in range(2):
                r = slice(HD * e, HD * e + HD)
                src = PS[r, 7, 0:P].rearrange("p (b j) -> p j b", b=DB)
                ins = V.tensor_tensor(XL[r, :, SEQ:TOK], src[:, 8 * e:8 * e + 8, :],
                                      XH[r, :, SEQ:TOK].bitcast(F32), ALU.subtract)
            ins.then_inc(do_lo, 1)
            dve.wait_ge(bwin, NH)
            prompt_attention(32, b_heads, lambda t: (max(t - 1, 0), t + 1), True)
            with dve.Fori(0, 4) as i:
                for s in range(2):
                    dve.wait_ge(hi_done, i * 2 + (B_OUT + s + 3))
                    low_part(None, s)
                    dve.wait_ge(unit_done, i * 2 + (B_OUT + s + 1))
                    add_residual(i, s)
            layer_norm(2, 2, False)
            dve.wait_ge(ya_init, 4)
            dve.wait_ge(outs, 16 * 9)
            mlp(MLP1, 80)
            layer_norm(3, 3, True)


def w_unit_list(w, cols):
    k = w.shape[0]
    u = w[:, np.concatenate(cols)].reshape(k // P, P, len(cols), P)
    return u.transpose(2, 1, 0, 3).reshape(len(cols), P, (k // P) * P)


def kernel(**inputs):
    import concourse.bacc as bacc
    from concourse.bass_utils import run_bass_kernel_spmd

    a = {k: np.asarray(v) for k, v in inputs.items()}
    ar = np.arange
    hcols = lambda h: ar(HD * h, HD * h + HD)
    wa, wb = a["a_w_in"][0], a["b_w_in"][0]
    q_a = [np.concatenate([hcols(h) for h in a_heads(p)]) for p in range(PAIRS)]
    q_b = [np.concatenate([hcols(h) for h in b_heads(p)]) for p in range(PAIRS)]
    o_k, o_v, o_qi, o_ki, o_wi = 1024, 1280, 1536, 2048, 2112
    tiles = lambda o, n: [ar(o + P * i, o + P * i + P) for i in range(n)]
    parts = [w_unit_list(wa, tiles(o_qi, 4) + tiles(o_k, 2) + q_a),
             w_unit_list(a["a_w_out"][0][np.concatenate(q_a)], tiles(0, 8))]

    def mlp_units(l):
        w1, w2 = a["mlp_w1"][l], a["mlp_w2"][l]
        out = []
        for c in range(CHUNKS):
            out.append(w_unit_list(w1, tiles(D * c, 8)))
            out.append(w_unit_list(w2[D * c:D * c + D], tiles(0, 8)))
        return out

    parts += mlp_units(0)
    parts += [w_unit_list(wb, tiles(1024, 2) + q_b),
              w_unit_list(a["b_w_out"][0][np.concatenate(q_b)], tiles(0, 8))]
    parts += mlp_units(1) + [np.zeros((2, P, D), np.float32)]
    x = np.concatenate([a["x_prompt"][0], a["x_sample"][:, 0]], axis=0)
    cst, csth = constants()
    ck = a["cache_k"][0].reshape(POOL_PAGES, PAGE, 2, P).transpose(0, 3, 2, 1)
    lnp = np.stack([np.stack([a[n][l].reshape(KT, P).T for n in (f"ln{i}_g", f"ln{i}_b")], 1)
                    for l in range(2) for i in (1, 2)], 1)
    arrays = {
        "xT": x.T.reshape(KT, P, TOK).transpose(1, 0, 2),
        "wn": wa[:, np.concatenate([ar(o_ki, o_ki + 72), ar(o_v, o_v + 256)])]
        .reshape(KT, P, NATW).transpose(1, 0, 2),
        "wall": np.concatenate(parts),
        "cacheK": ck.reshape(POOL_PAGES, P, 256),
        "cacheV": a["cache_v"][0].reshape(POOL_PAGES, P, 256),
        "cacheI": a["cache_idx_k"][0].transpose(0, 2, 1),
        "pt": a["page_table"].reshape(1, 64),
        "table": a["rel_bias_table"],
        "trep": np.tile(a["rel_bias_table"], (1, DB)),
        "lnp": lnp,
        "igb": np.broadcast_to(np.stack([a["a_idx_ln_g"][0], a["a_idx_ln_b"][0]]), (P, 2, HD)),
        "snk": np.broadcast_to(a["b_sink"], (P, NH)),
        "snd": np.tile(a["b_sink"][0], DB).reshape(P, 1),
        "swk": a["state_win_k"][0].reshape(DB, P, P).transpose(2, 0, 1),
        "swv": a["state_win_v"][0].reshape(DB, P, P),
        "cst": cst,
        "csth": csth,
    }
    out_shapes = {"yT": (P, KT, TOK), "kT": (P, 2, TOK), "vp": (P, QT, 256), "vs": (DB, 256),
                  "kip": (P, QT, HD), "kis": (DB, HD), "wkT": (P, P), "wv": (P, P),
                  "wksT": (P, DB, P), "wvs": (P, DB, P)}
    nc = bacc.Bacc("TRN2", target_bir_lowering=False, num_devices=1)
    io, feeds = {}, {}
    for n, v in arrays.items():
        feeds[n] = np.ascontiguousarray(v)
        io[n] = nc.dram_tensor(n, v.shape, mybir.dt.from_np(v.dtype), kind="ExternalInput").ap()
    for n, s in out_shapes.items():
        io[n] = nc.dram_tensor(n, s, F32, kind="ExternalOutput").ap()
    program(nc, io)
    r = run_bass_kernel_spmd(nc, [feeds], core_ids=[0]).results[0]
    y = r["yT"].transpose(2, 1, 0).reshape(TOK, D)
    k = r["kT"].transpose(2, 1, 0).reshape(TOK, 256)
    blocks = lambda v, w: v.transpose(1, 0, 2).reshape(1, 1, QT, P, *w)
    return (y[:SEQ].reshape(1, SEQ, D), y[SEQ:].reshape(DB, 1, D),
            k[:SEQ].reshape(1, 1, QT, P, 4, HD), blocks(r["vp"], (4, HD)), blocks(r["kip"], (HD,)),
            k[SEQ:].reshape(1, DB, 1, 4, HD), r["vs"].reshape(1, DB, 1, 4, HD),
            r["kis"].reshape(1, DB, 1, HD),
            r["wkT"].T.reshape(1, 1, P, 2, HD), r["wv"].reshape(1, 1, P, 2, HD),
            r["wksT"].transpose(1, 2, 0).reshape(1, DB, P, 2, HD),
            r["wvs"].transpose(1, 0, 2).reshape(1, DB, P, 2, HD))
```

```python
from contextlib import ExitStack
import math

import numpy as np

import concourse.bass as bass
from concourse import mybir

F32 = mybir.dt.float32
F32R = mybir.dt.float32r
I32 = mybir.dt.int32
ALU = mybir.AluOpType
ACT = mybir.ActivationFunctionType
AXX = mybir.AxisListType.X

P = 128
D = 1024
KT = D // P
SEQ, DB = 512, 8
TOK = SEQ + DB
TG = TOK // 2
NH, HD = 16, 64
PAST, PAGE = 1024, 128
NPG = PAST // PAGE
POOL_PAGES = 80
IDXH = 8
TOPK_P, TOPK_S = 128, 256
NB_, MAXD = 32, 128
ALPHA = (2 * 2) ** 0.25
NEG = -1e30
TAKEN = -3.0e38
EPS = 1e-5
QSCALE = HD ** -0.5
ISCALE = IDXH ** -0.5 * HD ** -0.5
QT = SEQ // P
NATW = HD + IDXH + 256
PAIRS = NH // 2

A_IN, A_OUT, MLP0, B_IN, B_OUT, MLP1, U_END = 0, 14, 22, 86, 96, 104, 168
CHUNKS = 4
SKEW = 768
POOL_LO = (8, 16)
LO_SKIP = POOL_LO[1] - POOL_LO[0]

KV_PLACE = (0, 1, 2, 3, 4, 5, 6, 0, 1, 2, 3, 4, 5, 6, 4, 5)
EARLY_ROUNDS = 10
SP_PAGES = 3


def kv_wait(n):
    mine = [m for m in range(n + 1) if KV_PLACE[m] == KV_PLACE[n]]
    by_sp = sum(NPG if m < 4 else SP_PAGES for m in mine)
    return KV_PLACE[n], 16 * (NPG * len(mine) - by_sp), 16 * by_sp


def kv_before(n):
    return max([m + 1 for m in range(n) if KV_PLACE[m] == KV_PLACE[n]], default=0)


def a_heads(p):
    return 8 * (p // 4) + p % 4, 8 * (p // 4) + p % 4 + 4


def b_heads(p):
    return p, p + 8


class Turns:

    def __init__(self, blocks):
        self.steps = []
        for t in range(QT):
            lo, hi = blocks(t)
            pairs = 512 // ((hi - lo) * P)
            self.steps += [(t, p, pairs, lo, hi) for p in range(0, PAIRS, pairs)]
        self.N = len(self.steps)
        self.n0 = 0

    def heads_at(self, i):
        t, p, pairs, lo, hi = self.steps[i]
        return [(e, g, 512 * e + g * (hi - lo) * P) for e in range(2) for g in range(pairs)]


def bucket(dist):
    n = np.maximum(np.asarray(dist), 0)
    exact = NB_ // 2
    nf = np.maximum(n, exact).astype(np.float32)
    large = exact + (np.log(nf / np.float32(exact)) / np.float32(math.log(MAXD / exact))
                     * np.float32(NB_ - exact)).astype(np.int32)
    return np.where(n < exact, n, np.minimum(large, NB_ - 1))


def one_hot(dist):
    return (np.arange(NB_)[:, None] == bucket(dist)[None, :]).astype(np.float32)


C_ID, C_ONE, C_CAUS, C_WIN, C_WD, C_REP, C_END = 0, 128, 256, 384, 640, 704, 832
H_SEQ, H_DEC, H_WIN, H_END = 0, 640, 640 + 1025, 640 + 1025 + 128


def constants():
    c = np.zeros((P, C_END), np.float32)
    i, j = np.arange(P)[:, None], np.arange(P)[None, :]
    c[:, C_ID:C_ID + P] = np.eye(P)
    c[:, C_ONE:C_ONE + P] = 1.0 / D
    c[:, C_CAUS:C_CAUS + P] = np.where(j <= i, 0.0, NEG)
    dist = i + P - np.arange(2 * P)[None, :]
    c[:, C_WIN:C_WIN + 2 * P] = np.where((dist >= 0) & (dist < P), 0.0, NEG)
    for b in range(DB):
        c[b, C_WD + 8 * b:C_WD + 8 * b + 8] = 1.0
        c[b, C_REP + NH * b:C_REP + NH * b + NH] = 1.0
    h = np.concatenate([one_hot(511 - np.arange(640)), one_hot(PAST - np.arange(PAST + 1)),
                        one_hot(P - 1 - np.arange(P))], axis=1)
    return c, np.ascontiguousarray(h)


def program(nc, io):
    with ExitStack() as ctx:
        words = [0]
        base = nc.sbuf_base
        usable = nc.sbuf_usable_end

        def place(name, shape, dt=F32, at=None):
            n = int(np.prod(shape[1:]))
            if at is None:
                at = words[0]
                words[0] += (n + 7) // 8 * 8
            off = (base + 31) // 32 * 32 + 4 * at
            assert off + 4 * n <= usable, (name, off + 4 * n, usable)
            return nc.alloc_sbuf_tensor_at(name, shape, dt, offset=off)

        def sem(name):
            return ctx.enter_context(nc.semaphore(name))

        UQ = place("UQ", [P, 14, TOK])
        YA = place("YA", [P, KT, TOK], at=6 * TOK)
        SEQS = place("SEQS", [16, 640], at=12 * TOK)
        X32 = place("X32", [P, KT, TOK])
        xw = words[0]
        XH = place("XH", [P, KT, TOK], F32R)
        XL = place("XL", [P, KT, TOK], F32R)
        KVR = place("KVR", [P, 3, NPG, 256], at=xw)
        BT = place("BT", [P, NH, 512], at=xw + 16640)
        KVB = place("KVB", [P, 4, NPG, 256], at=xw + 16640)
        VNEW = place("VNEW", [1, DB, 256], at=xw + 3 * 2048)
        hw = words[0]
        HH = place("HH", [P, KT, TOK], F32R)
        HL = place("HL", [P, KT, TOK], F32R)
        SQ = place("SQ", [P, KT, TOK], at=hw)
        IK = place("IK", [P, 4, 1025], at=hw)
        SR = place("SR", [HD, 1025], at=hw + 4104)
        QB = place("QB", [P, 2176], at=hw + 4104 + 1032)
        PB = place("PB", [P, 3, 1024], at=hw)
        PTB = place("PTB", [P, 2, 1024], at=hw + 3072)
        OV = place("OV", [NH, DB, 256], at=hw)
        BM = place("BM", [P, 2, 2, 512], at=0)
        PD = place("PD", [P, 1025], at=hw + 4096)
        KW = place("KW", [P, DB, 129], at=hw + 6304)
        words[0] = xw + 16640 + NH * 512
        WRAW = place("WRAW", [P, 2, KT, P])
        WHI = place("WHI", [P, 2, KT, P], F32R)
        WLO = place("WLO", [P, 2, KT, P], F32R)
        rw = words[0]
        RL = place("RL", [P, TOK])
        S32 = place("S32", [P, TOK])
        PTD = place("PTD", [P, NPG, P], at=rw)
        NAT = place("NAT", [P, 5, NATW])
        KID = place("KID", [P, 5, 2, HD])
        KIT = place("KIT", [P, TOK])
        DS = place("DS", [DB, 1025])
        ww = words[0]
        WN = place("WN", [P, KT, NATW])
        SC = place("SC", [P, 3, 512], at=ww)
        RS = place("RS", [P, 2, 512], at=ww + 1536)
        VW = place("VW", [P, DB, P], at=ww)
        CST = place("CST", [P, C_END])
        CH = place("CH", [NB_, H_END - 640])
        CHS = place("CHS", [NB_, 640], at=11 * TOK - 120)
        TAB = place("TAB", [NB_, 16])
        TREP = place("TREP", [NB_, P])
        LNP = place("LNP", [P, 4, 2, KT])
        IGB = place("IGB", [P, 2, HD])
        SNK = place("SNK", [P, NH])
        SND = place("SND", [P, 1])
        WB = place("WB", [HD, DB])
        WD = place("WD", [DB, HD])
        PT = place("PT", [1, 64], I32)
        EPSC = place("EPSC", [P, 1])
        KST = place("KST", [P, 5, 6])
        KMV = place("KMV", [P, 5, 2])
        KSD = place("KSD", [P, 5])
        MX8 = place("MX8", [P, 8])
        MX = place("MX", [P, 3, 8])
        NMX = place("NMX", [P, 3, 8])
        SM = place("SM", [P, 3, 8])
        SKE = place("SKE", [P, 3, 8])
        DST = place("DST", [P, 4])
        PNEW = place("PNEW", [1, P])
        RSTD = place("RSTD", [P, TOK], at=rw)

        ident = CST[:, C_ID:C_ID + P]
        ones = CST[:, C_ONE:C_ONE + P]
        caus = CST[:, C_CAUS:C_CAUS + P]
        ohd = CH[:, 0:1025]
        ohw = CH[:, 1025:1025 + P]

        PS = ctx.enter_context(nc.psum_tensor("PS", [P, 8, 512], F32))
        PSF = PS[:].rearrange("p a b -> p (a b)")
        bskew = nc.dram_tensor("bias_skewed", [P, NH, SKEW], F32, kind="Internal").ap()
        bseq = nc.dram_tensor("bias_seq", [16, 640], F32, kind="Internal").ap()

        x_in, wn_in, cst_in = sem("x_in"), sem("wn_in"), sem("cst_in")
        pt_in = sem("pt_in")
        raw_in = [sem("raw_in0"), sem("raw_in1")]
        idx_in = sem("idx_in")
        kv_pool = [sem(f"kv_pool{i}") for i in range(7)]
        kv_sp = [sem(f"kv_sp{i}") for i in range(7)]
        vnew_in = sem("vnew_in")
        toe_out, toe_skew, toe_in = sem("toe_out"), sem("toe_skew"), sem("toe_in")
        win_in, vwin_in = sem("win_in"), sem("vwin_in")
        outs = sem("outs")
        hi_done = sem("hi_done")
        lo_pool, lo_dve = sem("lo_pool"), sem("lo_dve")
        unit_done = sem("unit_done")
        ev_act, ev_dve = sem("ev_act"), sem("ev_dve")
        relu_done = sem("relu_done")
        hh_done, hl_done = sem("hh_done"), sem("hl_done")
        x_hi, x_lo = sem("x_hi"), sem("x_lo")
        nat_mm, nat_ev = sem("nat_mm"), sem("nat_ev")
        kstat, ksd, kid = sem("kstat"), sem("ksd"), sem("kid")
        kit_mm, kit_ev = sem("kit_mm"), sem("kit_ev")
        seq_mm, seq_ev = sem("seq_mm"), sem("seq_ev")
        is_mm, is_relu, is_acc = sem("is_mm"), sem("is_relu"), sem("is_acc")
        qib_ready, ikn_ready = sem("qib_ready"), sem("ikn_ready")
        ds_mm, ds_relu, ds_sum = sem("ds_mm"), sem("ds_relu"), sem("ds_sum")
        wd_ready, wb_mm, wb_ev = sem("wd_ready"), sem("wb_mm"), sem("wb_ev")
        top_p, top_s = sem("top_p"), sem("top_s")
        qb_ready = sem("qb_ready")
        kv_used = sem("kv_used")
        dl_mm, d_mx, d_exp, d_p = sem("dl_mm"), sem("d_mx"), sem("d_exp"), sem("d_p")
        dt_mm, dt_ev, do_mm, do_hi, do_lo = (sem("dt_mm"), sem("dt_ev"), sem("do_mm"),
                                             sem("do_hi"), sem("do_lo"))
        qk_mm, smx, pexp, pnorm = sem("qk_mm"), sem("smx"), sem("pexp"), sem("pnorm")
        pt_mm, pt_ev, bm_ready = sem("pt_mm"), sem("pt_ev"), sem("bm_ready")
        ov_mm, ov_ev = sem("ov_mm"), sem("ov_ev")
        o_mm, o_hi, o_lo = sem("o_mm"), sem("o_hi"), sem("o_lo")
        mean_mm, dev, sqr, var_mm, std_d, x_new = (sem("mean_mm"), sem("dev"), sem("sqr"),
                                                   sem("var_mm"), sem("std_d"), sem("x_new"))
        ya_init = sem("ya_init")
        z_nat, z_qb, bwin = sem("z_nat"), sem("z_qb"), sem("bwin")
        vt_mm, vt_ev = sem("vt_mm"), sem("vt_ev")
        own = sem("own")
        own_p = sem("own_p")

        def kv_place(n):
            pl = KV_PLACE[n]
            return KVB[:, pl] if pl < 4 else KVR[:, pl - 4]

        def load_page(eng, n, pg):
            pl, b = KV_PLACE[n], n % DB
            cache = io["cacheK"] if n < DB else io["cacheV"]
            dst = KVB[:, pl, bass.ds(pg, 1), :] if pl < 4 else KVR[:, pl - 4, bass.ds(pg, 1), :]
            page = eng.value_load(PT[0:1, bass.ds(pg + b * NPG, 1)],
                                  min_val=0, max_val=POOL_PAGES - 1)
            eng.dma_start(dst.rearrange("p o n -> p (o n)"),
                          cache[bass.ds(page, 1), :, :].rearrange("o p n -> (o p) n")
                          ).then_inc((kv_sp if eng is nc.sync else kv_pool)[pl], 16)

        def wait_place(eng, n):
            if n == 4:
                eng.wait_ge(unit_done, A_OUT)
            if kv_before(n):
                eng.wait_ge(kv_used, kv_before(n))

        turns_a = Turns(lambda t: (0, t + 1))
        turns_b = Turns(lambda t: (max(t - 1, 0), t + 1))
        turns_b.n0 = turns_a.N

        block = ctx.enter_context(nc.Block())

        @block.sync
        def _(sp):
            def load_unit(u, slot):
                sp.dma_start(WRAW[:, slot, :, :].rearrange("p k m -> p (k m)"),
                             io["wall"][bass.ds(u, 1), :, :].rearrange("o p n -> (o p) n")
                             ).then_inc(raw_in[slot], 16)

            sp.dma_start(PT[:], io["pt"]).then_inc(pt_in, 16)
            sp.dma_start(WN[:], io["wn"]).then_inc(wn_in, 16)
            sp.dma_start(X32[:], io["xT"]).then_inc(x_in, 16)
            for dst, src in ((CST[:], io["cst"]), (CH[:], io["csth"][:, 640:]),
                             (CHS[:], io["csth"][:, 0:640]), (TAB[:], io["table"]),
                             (TREP[:], io["trep"]), (LNP[:], io["lnp"]), (IGB[:], io["igb"]),
                             (SNK[:], io["snk"]), (SND[:], io["snd"])):
                sp.dma_start(dst, src).then_inc(cst_in, 16)
            load_unit(0, 0)
            load_unit(1, 1)
            sp.wait_ge(pt_in, 16)
            for b in range(2):
                with sp.Fori(0, NPG) as pg:
                    load_page(sp, b, pg)
            sp.wait_ge(seq_ev, 1)
            sp.dma_start(bseq, SEQS[:]).then_inc(toe_out, 16)
            with sp.Fori(1, POOL_LO[0] // 2 + 1) as i:
                for s in range(2):
                    sp.wait_ge(lo_dve, i * 2 + (s - 1))
                    load_unit(i * 2 + s, s)
                for b in range(2, 4):
                    for q in range(2):
                        load_page(sp, b, i * 2 + (q - 2))
            with sp.Fori(POOL_LO[0] // 2 + 1, POOL_LO[1] // 2 + 1) as i:
                for s in range(2):
                    sp.wait_ge(lo_pool, i * 2 + (s - 1 - POOL_LO[0]))
                    load_unit(i * 2 + s, s)
            for n in range(4, 2 * DB):
                wait_place(sp, n)
                with sp.Fori(NPG - SP_PAGES, NPG) as pg:
                    load_page(sp, n, pg)
            sp.wait_ge(toe_skew, 16 * 4)
            sp.wait_ge(kv_used, 11)
            sp.dma_start(BT[:], bskew[:, :, 127:127 + 512]).then_inc(toe_in, 16)
            with sp.Fori(POOL_LO[1] // 2 + 1, (U_END + 2) // 2) as i:
                for s in range(2):
                    sp.wait_ge(lo_dve, i * 2 + (s - 1 - LO_SKIP))
                    load_unit(i * 2 + s, s)
            for g in range(2):
                sp.wait_ge(x_new, 6 + g + 1)
                c = slice(TG * g, TG * g + TG)
                sp.dma_start(io["yT"][:, :, c], X32[:, :, c]).then_inc(outs, 16)
            sp.wait_ge(outs, 16 * 11)

        @block.gpsimd
        def _(pool):
            nc.gpsimd.memset(NAT[:, 4, :], 0.0).then_inc(z_nat, 1)
            nc.gpsimd.memset(QB[:], 0.0).then_inc(z_qb, 1)
            pool.wait_ge(pt_in, 16)
            for half in range(2):
                with pool.Fori(0, 4) as c:
                    for pg in range(NPG):
                        page = pool.value_load(PT[0:1, bass.ds(c * 16 + (8 * half + pg), 1)],
                                               min_val=0, max_val=POOL_PAGES - 1)
                        pool.dma_start(
                            IK[HD * half:HD * half + HD, bass.ds(c, 1), pg * P:(pg + 1) * P],
                            io["cacheI"][bass.ds(page, 1), :, :].rearrange("o d k -> d o k")
                        ).then_inc(idx_in, 16)

            def low_part(u, slot):
                pool.wait_ge(hi_done, u + 1)
                nc.gpsimd.tensor_tensor(WLO[:, slot], WRAW[:, slot], WHI[:, slot].bitcast(F32),
                                        ALU.subtract).then_inc(lo_pool, 1)

            with pool.Fori(POOL_LO[0] // 2, POOL_LO[1] // 2) as i:
                for s in range(2):
                    low_part(i * 2 + s, s)
            pool.wait_ge(ds_mm, 1)
            nc.gpsimd.memset(QB[:], 0.0).then_inc(z_qb, 1)

            for n in range(4, 2 * DB):
                wait_place(pool, n)
                with pool.Fori(0, NPG - SP_PAGES) as pg:
                    load_page(pool, n, pg)
                if n == DB - 1:
                    pool.wait_ge(nat_ev, 5)
                    for b in range(DB):
                        pool.dma_start(VNEW[0:1, b, :], NAT[b:b + 1, 4, HD + IDXH:NATW]
                                       ).then_inc(vnew_in, 16)
            pool.wait_ge(toe_in, 16)
            for i, (t, p, pairs, lo, hi) in enumerate(turns_a.steps):
                w = (hi - lo) * P
                off = 384 - t * P
                if t and p == 0:
                    pool.wait_ge(top_p, t)
                if i >= 2:
                    pool.wait_ge(smx, i - 1)
                mask = caus if t == 0 else SC[:, t - 1, 0:w]
                h, j = 8 * (p // 4), p % 4
                nc.gpsimd.tensor_tensor(
                    BM[:, i % 2, :, 0:pairs * w].rearrange("p e (g w) -> p e g w", w=w),
                    BT[:, h:h + 8, off:off + w].rearrange("p (e g) w -> p e g w", e=2)[
                        :, :, j:j + pairs, :],
                    mask.rearrange("p (a b w) -> p a b w", a=1, b=1).broadcast_to(
                        [P, 2, pairs, w]), ALU.add).then_inc(bm_ready, 1)
            for layer in range(2):
                for g in range(2):
                    pool.wait_ge(x_new, 4 * layer + g + 1)
                    c = slice(TG * g, TG * g + TG)
                    nc.gpsimd.tensor_scalar(YA[:, :, c], X32[:, :, c], float(ALPHA), None,
                                            ALU.mult).then_inc(ya_init, 1)
                if layer == 0:
                    for h in range(NH):
                        nc.gpsimd.tensor_tensor(BT[:, h, 256:512], BT[:, h, 256:512],
                                                CST[:, C_WIN:C_WIN + 2 * P], ALU.add
                                                ).then_inc(bwin, 1)
                    pool.wait_ge(var_mm, 4)
                    pool.dma_start(KW[:, :, 0:P], io["swk"]).then_inc(win_in, 16)
                    pool.dma_start(VW[0:P - 1, :, :],
                                   io["swv"][:, 1:P, :].rearrange("b k d -> k b d")
                                   ).then_inc(win_in, 16)
                    pool.wait_ge(vt_ev, 5)
                    for b in range(DB):
                        pool.dma_start(VW[P - 1:P, b, :], NAT[b:b + 1, 4, 0:P]
                                       ).then_inc(vwin_in, 16)
                    nc.gpsimd.memset(QB[:, 0:DB * 144], 0.0).then_inc(z_qb, 1)

        @block.tensor
        def _(pe):
            def unit(u, slot, hi, lo, waits=None):
                for k in range(KT):
                    if waits and k in waits:
                        waits[k]()
                    for w, parts in ((WHI, (hi, lo)), (WLO, (hi,))):
                        for x in parts:
                            for g in range(2):
                                mm = pe.matmul(PS[:, 2 * slot + g, 0:TG], w[:, slot, k, :],
                                               x[:, k, TG * g:TG * g + TG],
                                               start=(k == 0 and w is WHI and x is hi),
                                               stop=(k == KT - 1 and w is WLO))
                mm.then_inc(unit_done, 1)

            def wait_kv(n):
                pl, by_pool, by_sp = kv_wait(n)
                if by_pool:
                    pe.wait_ge(kv_pool[pl], by_pool)
                pe.wait_ge(kv_sp[pl], by_sp)

            def wait_lo(u):
                if u < POOL_LO[0]:
                    pe.wait_ge(lo_dve, u + 1)
                elif u < POOL_LO[1]:
                    pe.wait_ge(lo_pool, u + 1 - POOL_LO[0])
                else:
                    pe.wait_ge(lo_dve, u + 1 - LO_SKIP)

            def layer_norm_sums(n, ev_base):
                for k in range(KT):
                    if ev_base is not None:
                        pe.wait_ge(ev_dve, ev_base + k + 1)
                    for g in range(2):
                        mm = pe.matmul(PS[:, 4 + g, 0:TG], ones, YA[:, k, TG * g:TG * g + TG],
                                       start=(k == 0), stop=(k == KT - 1))
                mm.then_inc(mean_mm, 1)
                for g in range(2):
                    for k in range(KT):
                        if k % 4 == 0:
                            pe.wait_ge(sqr, 4 * n + 2 * g + k // 4 + 1)
                        mm = pe.matmul(PS[:, 6 + g, 0:TG], ones, SQ[:, k, TG * g:TG * g + TG],
                                       start=(k == 0), stop=(k == KT - 1))
                    mm.then_inc(var_mm, 1)

            def mlp(base, ev_base):
                with pe.Fori(0, CHUNKS) as c:
                    with pe.Fori(0, 4) as i:
                        for s in range(2):
                            j = c * 16 + i * 2 + s
                            pe.wait_ge(lo_dve, j + (base + 1 - LO_SKIP))
                            pe.wait_ge(ev_dve, j + (ev_base - 1))
                            unit(None, s, XH, XL)
                    for s in range(2):
                        j = c * 16 + 8 + s
                        pe.wait_ge(lo_dve, j + (base + 1 - LO_SKIP))
                        pe.wait_ge(ev_dve, j + (ev_base - 1))
                        hbase = 0 if base == MLP0 else 32
                        waits = {k: (lambda k=k: pe.wait_ge(hl_done, c * 8 + (hbase + k + 1)))
                                 for k in (5, 6, 7)} if s == 0 else None
                        if s == 0:
                            waits[0] = lambda: pe.wait_ge(hl_done, c * 8 + (hbase + 5))
                        unit(None, s, HH, HL, waits)
                    with pe.Fori(1, 4) as i:
                        for s in range(2):
                            j = c * 16 + i * 2 + (8 + s)
                            pe.wait_ge(lo_dve, j + (base + 1 - LO_SKIP))
                            pe.wait_ge(ev_dve, j + (ev_base - 1))
                            unit(None, s, HH, HL)

            def prompt_attention(tn, ktile, vtile):
                n0 = tn.n0

                def logits(i):
                    t, p, pairs, lo, hi = tn.steps[i]
                    if i >= 2:
                        pe.wait_ge(smx, n0 + i - 1)
                    for e, g, at in tn.heads_at(i):
                        r = slice(HD * e, HD * e + HD)
                        at += 1024 * (i % 2)
                        mm = pe.matmul(PSF[:, at:at + (hi - lo) * P],
                                       UQ[r, 6 + p + g, t * P:(t + 1) * P],
                                       UQ[r, ktile(p), lo * P:hi * P], start=True, stop=True)
                    mm.then_inc(qk_mm, 1)

                def turn(i):
                    t, p, pairs, lo, hi = tn.steps[i]
                    pe.wait_ge(pnorm, n0 + i + 1)
                    if i >= 1:
                        pe.wait_ge(pt_ev, n0 + i)
                    for e, g, at in tn.heads_at(i):
                        for o in range(at, at + (hi - lo) * P, P):
                            mm = pe.transpose(PSF[:, 2048 + o:2048 + o + P],
                                              PB[:, i % 3, o:o + P], ident)
                    mm.then_inc(pt_mm, 1)

                def output(i):
                    t, p, pairs, lo, hi = tn.steps[i]
                    pe.wait_ge(pt_ev, n0 + i + 1)
                    if i >= 2:
                        pe.wait_ge(o_lo, n0 + i - 1)
                    for e, g, at in tn.heads_at(i):
                        for kb in range(hi - lo):
                            b = at + kb * P
                            mm = pe.matmul(PS[HD * e:HD * e + HD, 6 + i % 2, g * P:(g + 1) * P],
                                           vtile(lo + kb, p, e), PTB[:, i % 2, b:b + P],
                                           start=(kb == 0), stop=(kb == hi - lo - 1))
                    mm.then_inc(o_mm, 1)

                logits(0)
                logits(1)
                for i in range(tn.N + 1):
                    if i + 2 < tn.N:
                        logits(i + 2)
                    if i < tn.N:
                        turn(i)
                    if i >= 1:
                        output(i - 1)

            pe.wait_ge(x_in, 16)
            pe.wait_ge(wn_in, 16)
            for t in range(5):
                m = P if t < QT else DB
                for k in range(KT):
                    mm = pe.matmul(PS[0:m, t, 0:NATW], X32[:, k, t * P:t * P + m], WN[:, k, :],
                                   start=(k == 0), stop=(k == KT - 1))
                mm.then_inc(nat_mm, 1)
            pe.wait_ge(cst_in, 16 * 9)
            pe.matmul(PS[0:16, 6, 0:512], TAB[:], CHS[:, 0:512], start=True, stop=True)
            pe.matmul(PS[0:16, 7, 0:P], TAB[:], CHS[:, 512:640], start=True, stop=True
                      ).then_inc(seq_mm, 1)
            pe.wait_ge(nat_ev, 5)
            pe.wait_ge(x_lo, 1)
            items = [(t, h) for t in range(1, QT) for h in range(IDXH)]
            for u in range(8):
                if u == 2:
                    pe.wait_ge(kid, 1)
                    for t in range(QT):
                        pe.transpose(PS[:, 4, t * P:(t + 1) * P],
                                     KID[:, t, :, :].rearrange("p a d -> p (a d)"), ident)
                    pe.transpose(PS[:, 5, 0:DB], KID[0:DB, 4, :, :].rearrange("p a d -> p (a d)"),
                                 CST[0:DB, 0:DB])
                    pe.wait_ge(wd_ready, 1)
                    pe.wait_ge(seq_ev, 1)
                    pe.transpose(PS[0:HD, 6, 0:DB], WD[:], CST[0:DB, 0:DB]).then_inc(kit_mm, 1)
                if u >= 4:
                    for n in range(6 * (u - 4), 6 * (u - 4) + 6):
                        t, h = items[n]
                        if n == 0:
                            pe.wait_ge(kit_ev, 2)
                            pe.wait_ge(wb_ev, 1)
                            pe.wait_ge(ev_act, 4)
                        if n >= 4:
                            pe.wait_ge(is_relu, n - 3)
                        r = slice(HD * (h % 2), HD * (h % 2) + HD)
                        pe.matmul(PS[:, 4 + n % 4, 0:(t + 1) * P],
                                  UQ[r, h // 2, t * P:(t + 1) * P], KIT[r, 0:(t + 1) * P],
                                  start=True, stop=True).then_inc(is_mm, 1)
                wait_lo(u)
                if u >= 2:
                    pe.wait_ge(ev_act, u - 1)
                unit(u, u % 2, XH, XL)
            pe.wait_ge(is_relu, 24)
            pe.wait_ge(qib_ready, 1)
            pe.wait_ge(ikn_ready, 1)
            for c0, c1 in ((0, 512), (512, 1024), (1024, 1025)):
                for c in range(4):
                    mm = pe.matmul(PSF[0:HD, 2048 + c0:2048 + c1], QB[:, HD * c:HD * c + HD],
                                   IK[:, c, c0:c1], start=(c == 0), stop=(c == 3))
            mm.then_inc(ds_mm, 1)
            for u in (8, 9):
                wait_lo(u)
                pe.wait_ge(ev_act, u - 1)
                unit(u, u % 2, XH, XL)
                if u == 8:
                    pe.wait_ge(ds_relu, 1)
                    pe.wait_ge(wb_ev, 1)
                    for c0, c1 in ((0, 512), (512, 1024), (1024, 1025)):
                        mm = pe.matmul(PSF[0:DB, 2048 + c0:2048 + c1], WB[:], SR[:, c0:c1],
                                       start=True, stop=True)
                    mm.then_inc(ds_sum, 1)
            with pe.Fori(5, A_OUT // 2) as i:
                for s in range(2):
                    pe.wait_ge(lo_pool, i * 2 + (s + 1 - POOL_LO[0]))
                    pe.wait_ge(ev_act, i * 2 + (s - 1))
                    unit(None, s, XH, XL)

            pe.wait_ge(ev_act, A_OUT)
            pe.wait_ge(qb_ready, 1)
            spans = ((0, 512), (512, 1024), (1024, 1025))
            for c0, c1 in spans:
                pe.matmul(PSF[:, c0:c1], TREP[:], ohd[:, c0:c1], start=True, stop=False)
            for b in range(DB):
                wait_kv(b)
                for gp in range(2):
                    q = QB[:, (2 * b + gp) * P:(2 * b + gp + 1) * P]
                    for half in range(2):
                        mm = pe.matmul(PSF[:, 512 * half:512 * half + 512], q,
                                       kv_place(b)[:, 4 * half:4 * half + 4, gp * P:(gp + 1) * P],
                                       start=False, stop=False)
                    pe.matmul(PSF[:, 1024:1025], q, UQ[:, 4 + gp, SEQ + b:SEQ + b + 1],
                              start=False, stop=False)
                mm.then_inc(kv_used, 1)
            pe.wait_ge(top_s, 1)
            for c0, c1 in spans:
                mm = pe.matmul(PSF[:, c0:c1], CST[0:DB, C_REP:C_REP + P], DS[:, c0:c1],
                               start=False, stop=True)
            mm.then_inc(dl_mm, 1)
            pe.wait_ge(d_p, 1)
            for k in range(NPG):
                pe.transpose(PS[:, 4 + k // 4, (k % 4) * P:(k % 4 + 1) * P],
                             PD[:, k * P:(k + 1) * P], ident)
            pe.transpose(PS[0:1, 6, 0:P], PD[:, 1024:1025], ident).then_inc(dt_mm, 1)
            pe.wait_ge(dt_ev, 1)
            pe.wait_ge(vnew_in, 16 * DB)
            for b in range(DB):
                n = DB + b
                wait_kv(n)
                o = PSF[0:NH, 2048 + 256 * b:2048 + 256 * b + 256]
                rows = slice(NH * b, NH * b + NH)
                for k in range(NPG):
                    mm = pe.matmul(o, PTD[:, k, rows], kv_place(n)[:, k, :], start=(k == 0),
                                   stop=False)
                mm.then_inc(kv_used, 1)
                pe.matmul(o, PNEW[0:1, rows], VNEW[0:1, b, :], start=False, stop=True
                          ).then_inc(ov_mm, 1)
            for b in range(DB):
                pe.wait_ge(ov_ev, b // 2 + 1)
                for gp in range(2):
                    c = (2 * b + gp) * NH
                    mm = pe.transpose(PS[:, 0, c:c + NH], OV[:, b, gp * P:(gp + 1) * P],
                                      CST[0:NH, 0:NH])
            mm.then_inc(do_mm, 1)
            pe.wait_ge(do_lo, 1)
            pe.wait_ge(toe_in, 16)
            prompt_attention(turns_a, lambda p: 4 + p // 4,
                             lambda kb, p, e: NAT[:, kb, 72 + HD * (2 * (p // 4) + e):
                                                  72 + HD * (2 * (p // 4) + e) + HD])
            pe.wait_ge(o_lo, turns_a.N)
            for s in range(2):
                pe.wait_ge(lo_pool, A_OUT + s + 1 - POOL_LO[0])
                unit(None, s, XH, XL)
            with pe.Fori(1, 4) as i:
                for s in range(2):
                    pe.wait_ge(lo_dve, i * 2 + (A_OUT + s + 1 - LO_SKIP))
                    pe.wait_ge(ev_dve, i * 2 + (s - 1))
                    unit(None, s, XH, XL)
            layer_norm_sums(0, 0)
            pe.wait_ge(x_lo, 3)
            mlp(MLP0, 8)
            layer_norm_sums(1, 8 + 64 - 8)
            pe.wait_ge(x_lo, 5)
            with pe.Fori(0, 5) as i:
                for s in range(2):
                    pe.wait_ge(lo_dve, i * 2 + (B_IN + s + 1 - LO_SKIP))
                    pe.wait_ge(ev_act, i * 2 + (A_OUT + s - 1))
                    unit(None, s, XH, XL)
            pe.wait_ge(ev_act, A_OUT + 10)
            for t in range(QT):
                pe.transpose(PS[:, 4, t * P:(t + 1) * P], UQ[:, 5, t * P:(t + 1) * P], ident)
            pe.transpose(PS[0:DB, 5, 0:P], UQ[:, 5, SEQ:TOK], ident).then_inc(vt_mm, 1)
            pe.wait_ge(qb_ready, 2)
            pe.wait_ge(win_in, 32)
            pe.matmul(PS[:, 0, 0:P], TREP[:], ohw, start=True, stop=False)
            for b in range(DB):
                mm = pe.matmul(PS[:, 0, 0:P], QB[:, b * P:(b + 1) * P], KW[:, b, 1:129],
                               start=False, stop=(b == DB - 1))
            mm.then_inc(dl_mm, 1)
            pe.wait_ge(d_p, 2)
            pe.wait_ge(vt_ev, 5)
            pe.transpose(PS[:, 4, 0:P], PD[:, 0:P], ident).then_inc(dt_mm, 1)
            pe.wait_ge(dt_ev, 2)
            pe.wait_ge(vwin_in, 16 * DB)
            for b in range(DB):
                mm = pe.matmul(PS[:, 7, b * NH:(b + 1) * NH], VW[:, b, :],
                               PTD[:, 0, b * NH:(b + 1) * NH], start=True, stop=True)
            mm.then_inc(do_mm, 1)
            pe.wait_ge(do_lo, 2)
            prompt_attention(turns_b, lambda p: 4,
                             lambda kb, p, e: NAT[:, kb, HD * e:HD * e + HD])
            pe.wait_ge(o_lo, turns_a.N + turns_b.N)
            with pe.Fori(0, 4) as i:
                for s in range(2):
                    pe.wait_ge(lo_dve, i * 2 + (B_OUT + s + 1 - LO_SKIP))
                    pe.wait_ge(ev_dve, i * 2 + (72 + s - 1))
                    unit(None, s, XH, XL)
            layer_norm_sums(2, 72)
            pe.wait_ge(x_lo, 7)
            mlp(MLP1, 80)
            layer_norm_sums(3, 80 + 64 - 8)

        @block.scalar
        def _(act):
            def high_part(u, slot, static=True):
                if isinstance(u, int):
                    act.wait_ge(raw_in[slot], 16 * (u // 2 + 1))
                    if u >= 2:
                        act.wait_ge(unit_done, u - 1)
                nc.scalar.activation(WHI[:, slot], WRAW[:, slot], ACT.Copy).then_inc(hi_done, 1)

            def banks(slot):
                return PS[:, 2 * slot:2 * slot + 2, 0:TG]

            def mlp(base, ev_base):
                with act.Fori(0, CHUNKS) as c:
                    with act.Fori(0, 4) as i:
                        for s in range(2):
                            j = c * 16 + i * 2 + s
                            act.wait_ge(unit_done, j + (base + 1))
                            nc.scalar.activation(RL[:].rearrange("p (g t) -> p g t", g=2),
                                                 banks(s), ACT.Relu).then_inc(relu_done, 1)
                            act.wait_ge(ev_dve, j + (ev_base + 1))
                            nc.scalar.activation(HH[:, bass.ds(i * 2 + s, 1), :],
                                                 S32[:].rearrange("p (o t) -> p o t", o=1),
                                                 ACT.Copy).then_inc(hh_done, 1)
                            act.wait_ge(raw_in[s], (c * 8 + i + (base // 2 + 2)) * 16)
                            high_part(None, s)
                    with act.Fori(4, 8) as i:
                        for s in range(2):
                            j = c * 16 + i * 2 + s
                            act.wait_ge(unit_done, j + (base + 1))
                            act.wait_ge(raw_in[s], (c * 8 + i + (base // 2 + 2)) * 16)
                            high_part(None, s)

            def layer_norm(n, last):
                for g in range(2):
                    c = slice(TG * g, TG * g + TG)
                    for q in range(2):
                        act.wait_ge(dev, 4 * n + 2 * g + q + 1)
                        nc.scalar.activation(SQ[:, 4 * q:4 * q + 4, c], YA[:, 4 * q:4 * q + 4, c],
                                             ACT.Square).then_inc(sqr, 1)
                for g in range(2):
                    c = slice(TG * g, TG * g + TG)
                    act.wait_ge(var_mm, 2 * n + g + 1)
                    nc.scalar.activation(RSTD[:, c], PS[:, 6 + g, 0:TG], ACT.Sqrt,
                                         bias=EPSC[:]).then_inc(std_d, 1)
                if not last:
                    for g in range(2):
                        c = slice(TG * g, TG * g + TG)
                        act.wait_ge(x_new, 2 * n + g + 1)
                        nc.scalar.activation(XH[:, :, c], X32[:, :, c], ACT.Copy).then_inc(x_hi, 1)

            def prompt_attention(tn, sink):
                n0 = tn.n0

                def exps(i):
                    t, p, pairs, lo, hi = tn.steps[i]
                    act.wait_ge(smx, n0 + i + 1)
                    for j, (e, g, at) in enumerate(tn.heads_at(i)):
                        x = PB[:, i % 3, at:at + (hi - lo) * P]
                        ins = nc.scalar.activation(x, x, ACT.Exp, bias=NMX[:, i % 3, j:j + 1],
                                                   accum_out=SM[:, i % 3, j:j + 1])
                    if sink:
                        x = SKE[:, i % 3, 0:2 * pairs]
                        ins = nc.scalar.activation(x, x, ACT.Exp)
                    ins.then_inc(pexp, 1)

                def turned(i):
                    t, p, pairs, lo, hi = tn.steps[i]
                    w = pairs * (hi - lo) * P
                    act.wait_ge(pt_mm, n0 + i + 1)
                    if i >= 2:
                        act.wait_ge(o_mm, n0 + i - 1)
                    nc.scalar.activation(
                        PTB[:, i % 2, :].rearrange("p (e w) -> p e w", e=2)[:, :, 0:w],
                        PS[:, 4:6, 0:w], ACT.Copy).then_inc(pt_ev, 1)

                def out_high(i):
                    t, p, pairs, lo, hi = tn.steps[i]
                    act.wait_ge(o_mm, n0 + i + 1)
                    nc.scalar.activation(
                        XH[:, p:p + pairs, t * P:(t + 1) * P],
                        PS[:, 6 + i % 2, 0:pairs * P].rearrange("p (g q) -> p g q", q=P),
                        ACT.Copy).then_inc(o_hi, 1)

                exps(0)
                exps(1)
                for i in range(tn.N + 1):
                    if i < tn.N:
                        turned(i)
                    if i + 2 < tn.N:
                        exps(i + 2)
                    if i >= 1:
                        out_high(i - 1)

            act.wait_ge(x_in, 16)
            nc.scalar.activation(XH[:], X32[:], ACT.Copy).then_inc(x_hi, 1)
            high_part(0, 0)
            high_part(1, 1)
            act.wait_ge(z_nat, 1)
            for t in range(5):
                m = P if t < QT else DB
                act.wait_ge(nat_mm, t + 1)
                nc.scalar.activation(NAT[0:m, t, :], PS[0:m, t, 0:NATW], ACT.Copy
                                     ).then_inc(nat_ev, 1)
            act.wait_ge(seq_mm, 1)
            nc.scalar.activation(SEQS[:], PSF[0:16, 3072:3072 + 640], ACT.Copy
                                 ).then_inc(seq_ev, 1)
            act.wait_ge(kstat, 1)
            nc.scalar.activation(KSD[:], KMV[:, :, 1], ACT.Sqrt, bias=EPSC[:]).then_inc(ksd, 1)
            items = [(t, h) for t in range(1, QT) for h in range(IDXH)]
            for u in range(8):
                if u >= 4:
                    for n in range(6 * (u - 4), 6 * (u - 4) + 6):
                        t, h = items[n]
                        act.wait_ge(is_mm, n + 1)
                        if n >= 2:
                            act.wait_ge(is_acc, n - 1)
                        nc.scalar.activation(RS[:, n % 2, 0:(t + 1) * P],
                                             PS[:, 4 + n % 4, 0:(t + 1) * P], ACT.Relu
                                             ).then_inc(is_relu, 1)
                act.wait_ge(unit_done, u + 1)
                high_part(u + 2, u % 2)
                if u < 6:
                    nc.scalar.activation(UQ[:, u, :].rearrange("p (g t) -> p g t", g=2),
                                         banks(u % 2), ACT.Copy).then_inc(ev_act, 1)
                else:
                    nc.scalar.activation(UQ[:, u, :].rearrange("p (g t) -> p g t", g=2),
                                         banks(u % 2), ACT.Copy, scale=QSCALE
                                         ).then_inc(ev_act, 1)
                if u == 2:
                    act.wait_ge(kit_mm, 1)
                    nc.scalar.activation(KIT[:, 0:512], PS[:, 4, :], ACT.Copy
                                         ).then_inc(kit_ev, 1)
                    nc.scalar.activation(KIT[:, 512:520], PS[:, 5, 0:DB], ACT.Copy
                                         ).then_inc(kit_ev, 1)
                    nc.scalar.activation(WB[:], PS[0:HD, 6, 0:DB], ACT.Copy).then_inc(wb_ev, 1)
                if u >= 4:
                    if u == 4:
                        act.wait_ge(toe_out, 16)
                    i0 = 32 * (u - 4)
                    act.dma_start(bass.AP(tensor=bskew.tensor, offset=i0 * (NH * SKEW + 1),
                                          ap=[[NH * SKEW + 1, 32], [SKEW, NH], [1, 640]]),
                                  bass.AP(tensor=bseq.tensor, offset=0,
                                          ap=[[0, 32], [640, NH], [1, 640]])
                                  ).then_inc(toe_skew, 16)
                if u == 6:
                    act.wait_ge(nat_ev, 5)
                    act.dma_start(io["vp"], NAT[:, 0:QT, HD + IDXH:NATW]).then_inc(outs, 16)
                    act.dma_start(io["vs"], NAT[0:DB, 4, HD + IDXH:NATW]).then_inc(outs, 16)
                    act.wait_ge(kid, 1)
                    act.dma_start(io["kip"], KID[:, 0:QT, 0, :]).then_inc(outs, 16)
                    act.dma_start(io["kis"], KID[0:DB, 4, 0, :]).then_inc(outs, 16)
                    act.wait_ge(ev_act, 6)
                    act.dma_start(io["kT"], UQ[:, 4:6, :]).then_inc(outs, 16)
            act.wait_ge(ds_mm, 1)
            nc.scalar.activation(SR[:], PSF[0:HD, 2048:2048 + 1025], ACT.Relu
                                 ).then_inc(ds_relu, 1)

            with act.Fori(4, A_OUT // 2) as i:
                for s in range(2):
                    act.wait_ge(unit_done, i * 2 + (s + 1))
                    act.wait_ge(raw_in[s], (i + 2) * 16)
                    high_part(None, s)
                    nc.scalar.activation(
                        UQ[:, bass.ds(i * 2 + s, 1), :].rearrange("p o (g t) -> p (o g) t", g=2),
                        banks(s), ACT.Copy, scale=QSCALE).then_inc(ev_act, 1)

            act.wait_ge(d_mx, 1)
            nc.scalar.activation(PD[:], PSF[:, 0:1025], ACT.Exp, bias=DST[:, 1:2],
                                 accum_out=DST[:, 2:3]).then_inc(d_exp, 1)
            act.wait_ge(dt_mm, 1)
            nc.scalar.activation(PTD[:].rearrange("p k r -> p (k r)"), PSF[:, 2048:2048 + 1024],
                                 ACT.Copy)
            nc.scalar.activation(PNEW[:], PS[0:1, 6, 0:P], ACT.Copy).then_inc(dt_ev, 1)
            for q in range(4):
                act.wait_ge(ov_mm, 2 * q + 2)
                nc.scalar.activation(OV[:, 2 * q:2 * q + 2, :].rearrange("p b n -> p (b n)"),
                                     PS[0:NH, 4 + q, :], ACT.Copy).then_inc(ov_ev, 1)
            act.wait_ge(do_mm, 1)
            for gp in range(2):
                for e in range(2):
                    r = slice(HD * e, HD * e + HD)
                    src = PS[r, 0, 0:2 * P].rearrange("p (b g j) -> p g j b", b=DB, g=2)
                    h = 8 * gp + 4 * e
                    ins = nc.scalar.activation(XH[r, 4 * gp:4 * gp + 4, SEQ:TOK],
                                               src[:, gp, h:h + 4, :], ACT.Copy)
            ins.then_inc(do_hi, 1)
            prompt_attention(turns_a, False)
            with act.Fori(0, 4) as i:
                for s in range(2):
                    act.wait_ge(unit_done, i * 2 + (A_OUT + s + 1))
                    act.wait_ge(raw_in[s], (i + (A_OUT // 2 + 2)) * 16)
                    high_part(None, s)
            layer_norm(0, False)
            mlp(MLP0, 8)
            layer_norm(1, False)
            for s in range(2):
                act.wait_ge(unit_done, B_IN + s + 1)
                high_part(B_IN + 2 + s, s)
                if s == 0:
                    act.wait_ge(outs, 16 * 5)
                nc.scalar.activation(UQ[:, 4 + s, :].rearrange("p (g t) -> p g t", g=2),
                                     banks(s), ACT.Copy).then_inc(ev_act, 1)
            with act.Fori(1, 5) as i:
                for s in range(2):
                    act.wait_ge(unit_done, i * 2 + (B_IN + s + 1))
                    act.wait_ge(raw_in[s], (i + (B_IN // 2 + 2)) * 16)
                    high_part(None, s)
                    nc.scalar.activation(
                        UQ[:, bass.ds(i * 2 + (4 + s), 1), :].rearrange(
                            "p o (g t) -> p (o g) t", g=2),
                        banks(s), ACT.Copy, scale=QSCALE).then_inc(ev_act, 1)
            act.wait_ge(vt_mm, 1)
            for t in range(QT):
                nc.scalar.activation(NAT[:, t, 0:P], PS[:, 4, t * P:(t + 1) * P], ACT.Copy
                                     ).then_inc(vt_ev, 1)
            nc.scalar.activation(NAT[0:DB, 4, 0:P], PS[0:DB, 5, 0:P], ACT.Copy).then_inc(vt_ev, 1)
            act.wait_ge(vt_ev, 5)
            act.dma_start(io["wkT"], UQ[:, 4, SEQ - P:SEQ]).then_inc(outs, 16)
            act.dma_start(io["wv"], NAT[:, QT - 1, 0:P]).then_inc(outs, 16)
            act.wait_ge(qb_ready, 2)
            act.dma_start(io["wksT"], KW[:, :, 1:P + 1]).then_inc(outs, 16)
            act.wait_ge(vwin_in, 16 * DB)
            act.wait_ge(win_in, 32)
            act.dma_start(io["wvs"], VW[:]).then_inc(outs, 16)
            act.wait_ge(d_mx, 2)
            nc.scalar.activation(DST[:, 3:4], SND[:], ACT.Exp, bias=DST[:, 1:2])
            nc.scalar.activation(PD[:, 0:P], PS[:, 0, 0:P], ACT.Exp, bias=DST[:, 1:2],
                                 accum_out=DST[:, 2:3]).then_inc(d_exp, 1)
            act.wait_ge(dt_mm, 2)
            nc.scalar.activation(PTD[:, 0, :], PS[:, 4, 0:P], ACT.Copy).then_inc(dt_ev, 1)
            act.wait_ge(do_mm, 2)
            for e in range(2):
                r = slice(HD * e, HD * e + HD)
                src = PS[r, 7, 0:P].rearrange("p (b j) -> p j b", b=DB)
                ins = nc.scalar.activation(XH[r, :, SEQ:TOK], src[:, 8 * e:8 * e + 8, :], ACT.Copy)
            ins.then_inc(do_hi, 1)
            prompt_attention(turns_b, True)
            with act.Fori(0, 4) as i:
                for s in range(2):
                    act.wait_ge(unit_done, i * 2 + (B_OUT + s + 1))
                    act.wait_ge(raw_in[s], (i + (B_OUT // 2 + 2)) * 16)
                    high_part(None, s)
            layer_norm(2, False)
            mlp(MLP1, 80)
            layer_norm(3, True)

        @block.vector
        def _(dve):
            V = nc.vector
            count = [0]

            def after(ins):
                count[0] += 1
                ins.then_inc(own, 1)
                dve.wait_ge(own, count[0])

            def low_part(u, slot):
                if isinstance(u, int):
                    dve.wait_ge(hi_done, u + 1)
                V.tensor_tensor(WLO[:, slot], WRAW[:, slot], WHI[:, slot].bitcast(F32),
                                ALU.subtract).then_inc(lo_dve, 1)

            def banks(slot):
                return PS[:, 2 * slot:2 * slot + 2, 0:TG]

            def add_residual(i, s):
                m = bass.ds(i * 2 + s, 1)
                V.scalar_tensor_tensor(
                    out=YA[:, m, :].rearrange("p o (g t) -> p (o g) t", g=2),
                    in0=X32[:, m, :].rearrange("p o (g t) -> p (o g) t", g=2),
                    scalar=float(ALPHA), in1=banks(s), op0=ALU.mult, op1=ALU.add
                ).then_inc(ev_dve, 1)

            def mlp(base, ev_base):
                sq0 = 0 if base == MLP0 else 32
                with dve.Fori(0, CHUNKS) as c:
                    with dve.Fori(0, 4) as i:
                        for s in range(2):
                            dve.wait_ge(lo_dve, c * 16 + i * 2 + (base + s + 2 - LO_SKIP))
                            dve.wait_ge(relu_done, c * 8 + i * 2 + (sq0 + s + 1))
                            V.tensor_tensor(S32[:].rearrange("p (g t) -> p g t", g=2),
                                            RL[:].rearrange("p (g t) -> p g t", g=2),
                                            banks(s), ALU.mult
                                            ).then_inc(ev_dve, 1)
                            dve.wait_ge(hh_done, c * 8 + i * 2 + (sq0 + s + 1))
                            m = bass.ds(i * 2 + s, 1)
                            V.tensor_tensor(HL[:, m, :],
                                            S32[:].rearrange("p (o t) -> p o t", o=1),
                                            HH[:, m, :].bitcast(F32), ALU.subtract
                                            ).then_inc(hl_done, 1)
                            dve.wait_ge(hi_done, c * 16 + i * 2 + (base + s + 3))
                            low_part(None, s)
                    with dve.Fori(0, 4) as i:
                        for s in range(2):
                            dve.wait_ge(hi_done, c * 16 + i * 2 + (base + s + 11))
                            low_part(None, s)
                            dve.wait_ge(unit_done, c * 16 + i * 2 + (base + s + 9))
                            m = bass.ds(i * 2 + s, 1)
                            ya = YA[:, m, :].rearrange("p o (g t) -> p (o g) t", g=2)
                            V.tensor_tensor(ya, ya, banks(s), ALU.add).then_inc(ev_dve, 1)

            def layer_norm(n, ln, last):
                dve.wait_ge(mean_mm, n + 1)
                for g in range(2):
                    c = slice(TG * g, TG * g + TG)
                    for q in range(2):
                        y = YA[:, 4 * q:4 * q + 4, c]
                        V.tensor_tensor(y, y, PS[:, 4 + g:5 + g, 0:TG].broadcast_to([P, 4, TG]),
                                        ALU.subtract).then_inc(dev, 1)
                for g in range(2):
                    c = slice(TG * g, TG * g + TG)
                    dve.wait_ge(std_d, 2 * n + g + 1)
                    after(V.reciprocal(RSTD[:, c], RSTD[:, c]))
                    for q in range(2):
                        y = YA[:, 4 * q:4 * q + 4, c]
                        r = RSTD[:, c].rearrange("p (o t) -> p o t", o=1).broadcast_to([P, 4, TG])
                        ins = V.tensor_tensor(y, y, r, ALU.mult)
                        after(ins)
                    for k in range(KT):
                        ins = V.tensor_scalar(X32[:, k, c], YA[:, k, c], LNP[:, ln, 0, k:k + 1],
                                              LNP[:, ln, 1, k:k + 1], ALU.mult, ALU.add)
                    ins.then_inc(x_new, 1)
                    if not last and g == 1:
                        pass
                if not last:
                    for g in range(2):
                        c = slice(TG * g, TG * g + TG)
                        dve.wait_ge(x_hi, 1 + 2 * n + g + 1)
                        V.tensor_tensor(XL[:, :, c], X32[:, :, c], XH[:, :, c].bitcast(F32),
                                        ALU.subtract).then_inc(x_lo, 1)

            def prompt_attention(tn, sink, between=None):
                n0 = tn.n0

                def softmax_in(i):
                    t, p, pairs, lo, hi = tn.steps[i]
                    w = (hi - lo) * P
                    dve.wait_ge(qk_mm, n0 + i + 1)
                    if i >= 3:
                        dve.wait_ge(pt_mm, n0 + i - 2)
                    if not sink:
                        dve.wait_ge(bm_ready, i + 1)
                    for j, (e, g, at) in enumerate(tn.heads_at(i)):
                        if sink:
                            off = 384 - t * P + lo * P
                            add = BT[:, b_heads(p + g)[e], off:off + w]
                        else:
                            add = BM[:, i % 2, e, g * w:(g + 1) * w]
                        lg = 1024 * (i % 2) + at
                        ins = V.tensor_tensor_reduce(out=PB[:, i % 3, at:at + w],
                                                     in0=PSF[:, lg:lg + w], in1=add,
                                                     scale=1.0, scalar=TAKEN,
                                                     op0=ALU.add, op1=ALU.max,
                                                     accum_out=MX[:, i % 3, j:j + 1])
                    after(ins)
                    mx = MX[:, i % 3, 0:2 * pairs]
                    if sink:
                        sk = SNK[:].rearrange("p (e j) -> p e j", e=2)[:, :, p:p + pairs]
                        mx2 = mx.rearrange("p (e j) -> p e j", e=2)
                        after(V.tensor_tensor(mx2, mx2, sk, ALU.max))
                        V.tensor_tensor(SKE[:, i % 3, 0:2 * pairs].rearrange(
                            "p (e j) -> p e j", e=2), sk, mx2, ALU.subtract)
                    V.tensor_scalar(NMX[:, i % 3, 0:2 * pairs], mx, -1.0, None, ALU.mult
                                    ).then_inc(smx, 1)

                def normalise(i):
                    t, p, pairs, lo, hi = tn.steps[i]
                    sm = SM[:, i % 3, 0:2 * pairs]
                    dve.wait_ge(pexp, n0 + i + 1)
                    if sink:
                        after(V.tensor_tensor(sm, sm, SKE[:, i % 3, 0:2 * pairs], ALU.add))
                    after(V.reciprocal(sm, sm))
                    for j, (e, g, at) in enumerate(tn.heads_at(i)):
                        x = PB[:, i % 3, at:at + (hi - lo) * P]
                        ins = V.tensor_scalar(x, x, SM[:, i % 3, j:j + 1], None, ALU.mult)
                    ins.then_inc(pnorm, 1)

                def out_low(i):
                    t, p, pairs, lo, hi = tn.steps[i]
                    dve.wait_ge(o_hi, n0 + i + 1)
                    m, c = slice(p, p + pairs), slice(t * P, (t + 1) * P)
                    V.tensor_tensor(XL[:, m, c], PS[:, 6 + i % 2, 0:pairs * P].rearrange(
                        "p (g q) -> p g q", q=P), XH[:, m, c].bitcast(F32), ALU.subtract
                        ).then_inc(o_lo, 1)

                softmax_in(0)
                softmax_in(1)
                for i in range(tn.N + 1):
                    if i < tn.N:
                        normalise(i)
                    if i + 2 < tn.N:
                        softmax_in(i + 2)
                    if between:
                        between(i)
                    if i >= 2:
                        out_low(i - 2)
                out_low(tn.N - 1)

            V.memset(EPSC[:], EPS).then_inc(own, 1)
            count[0] += 1
            dve.wait_ge(x_hi, 1)
            V.tensor_tensor(XL[:], X32[:], XH[:].bitcast(F32), ALU.subtract).then_inc(x_lo, 1)
            for u in range(2):
                low_part(u, u)
            dve.wait_ge(nat_ev, 5)
            dve.wait_ge(cst_in, 16 * 9)
            V.tensor_tensor(WD[:].rearrange("p (b h) -> p b h", b=DB),
                            NAT[0:DB, 4:5, HD:HD + IDXH].broadcast_to([DB, DB, IDXH]),
                            CST[0:DB, C_WD:C_WD + HD].rearrange("p (b h) -> p b h", b=DB),
                            ALU.mult).then_inc(wd_ready, 1)
            for t in range(5):
                ins = V.bn_stats(KST[:, t, :], NAT[:, t, 0:HD])
            after(ins)
            for t in range(5):
                ins = V.bn_aggr(KMV[:, t, :], KST[:, t, :])
            ins.then_inc(kstat, 1)
            dve.wait_ge(kstat, 1)
            dve.wait_ge(ksd, 1)
            after(V.reciprocal(KSD[:], KSD[:]))
            z = KID[:, :, 0, :]

            def over_d(ap):
                return ap.rearrange("p (t o) -> p t o", o=1).broadcast_to([P, 5, HD])

            def over_t(ap):
                return ap.rearrange("p (o d) -> p o d", o=1).broadcast_to([P, 5, HD])

            after(V.tensor_tensor(z, NAT[:, :, 0:HD], over_d(KMV[:, :, 0]), ALU.subtract))
            after(V.tensor_tensor(z, z, over_d(KSD[:]), ALU.mult))
            after(V.tensor_tensor(z, z, over_t(IGB[:, 0, :]), ALU.mult))
            after(V.tensor_tensor(z, z, over_t(IGB[:, 1, :]), ALU.add))
            V.tensor_copy(KID[:, :, 1, :], z).then_inc(kid, 1)
            items = [(t, h) for t in range(1, QT) for h in range(IDXH)]
            for u in range(2, 6):
                low_part(u, u % 2)
            for n, (t, h) in enumerate(items):
                if n in (6, 12):
                    low_part(5 + n // 6, (5 + n // 6) % 2)
                dve.wait_ge(is_relu, n + 1)
                w = (t + 1) * P
                wi = NAT[:, t, HD + h:HD + h + 1]
                if h == 0:
                    ins = V.tensor_scalar(SC[:, t - 1, 0:w], RS[:, n % 2, 0:w], wi, None, ALU.mult)
                else:
                    ins = V.scalar_tensor_tensor(out=SC[:, t - 1, 0:w], in0=RS[:, n % 2, 0:w],
                                                 scalar=wi, in1=SC[:, t - 1, 0:w],
                                                 op0=ALU.mult, op1=ALU.add)
                ins.then_inc(is_acc, 1)
                dve.wait_ge(is_acc, n + 1)
            dve.wait_ge(kit_ev, 2)
            dve.wait_ge(idx_in, 16 * 64)
            for half in range(2):
                r = slice(HD * half, HD * half + HD)
                ins = V.tensor_copy(
                    IK[r, :, 1024:1025],
                    KIT[r, SEQ:TOK].rearrange("p (c s) -> p c s", s=2)[:, :, half:half + 1])
            ins.then_inc(ikn_ready, 1)
            dve.wait_ge(z_qb, 1)
            dve.wait_ge(ev_act, 4)
            qv = QB[:, 0:320].rearrange("p (c x) -> p c x", x=80)
            for half in range(2):
                for par in range(2):
                    src = UQ[HD * par:HD * par + HD, 0:4, SEQ:TOK].rearrange(
                        "p f (c s) -> p c s f", s=2)
                    ins = V.tensor_copy(qv[HD * half:HD * half + HD, :, 8 * half + par:
                                           8 * half + par + 8:2][:, :, 0:4], src[:, :, half, :])
            ins.then_inc(qib_ready, 1)
            for t in range(1, QT):
                V.tensor_scalar(SC[:, t - 1, 0:t * P], SC[:, t - 1, 0:t * P], float(ISCALE), None,
                                ALU.mult)
                d = SC[:, t - 1, t * P:(t + 1) * P]
                after(V.scalar_tensor_tensor(out=d, in0=d, scalar=float(ISCALE), in1=caus,
                                             op0=ALU.mult, op1=ALU.add))

            def take_rounds(sc, rows, rounds):
                for _ in range(rounds):
                    after(V.max(MX8[0:rows, :], sc))
                    after(V.match_replace(sc, MX8[0:rows, :], sc, TAKEN))

            def to_mask(sc):
                return V.tensor_scalar(sc, sc, -2.0e38, NEG, ALU.is_gt, ALU.mult)

            dve.wait_ge(ds_sum, 1)
            after(V.tensor_scalar(DS[:], PSF[0:DB, 2048:2048 + 1025], float(ISCALE), None, ALU.mult
                                  ))
            take_rounds(DS[:], DB, EARLY_ROUNDS)
            dve.wait_ge(ev_act, A_OUT)
            dve.wait_ge(z_qb, 2)
            qv = QB[:].rearrange("p (b x) -> p b x", x=272)
            for gp in range(2):
                for e in range(2):
                    r = slice(HD * e, HD * e + HD)
                    o = gp * 136 + 4 * e
                    src = UQ[r, 6 + 4 * gp:10 + 4 * gp, SEQ:TOK].rearrange("p j b -> p b j")
                    ins = V.tensor_copy(qv[r, :, o:o + 4], src)
            ins.then_inc(qb_ready, 1)
            take_rounds(DS[:], DB, TOPK_S // 8 - EARLY_ROUNDS)
            to_mask(DS[:]).then_inc(top_s, 1)

            def sample_softmax(n, logits, w, sink):
                dve.wait_ge(dl_mm, n)
                after(V.tensor_reduce(DST[:, 0:1], logits, AXX, ALU.max))
                if sink:
                    after(V.tensor_tensor(DST[:, 0:1], DST[:, 0:1], SND[:], ALU.max))
                V.tensor_scalar(DST[:, 1:2], DST[:, 0:1], -1.0, None, ALU.mult).then_inc(d_mx, 1)
                dve.wait_ge(d_exp, n)
                if sink:
                    after(V.tensor_tensor(DST[:, 2:3], DST[:, 2:3], DST[:, 3:4], ALU.add))
                after(V.reciprocal(DST[:, 2:3], DST[:, 2:3]))
                V.tensor_scalar(PD[:, 0:w], PD[:, 0:w], DST[:, 2:3], None, ALU.mult
                                ).then_inc(d_p, 1)

            sample_softmax(1, PSF[:, 0:1025], 1025, False)
            for t in range(1, QT - 1):
                sc = SC[:, t - 1, 0:(t + 1) * P]
                take_rounds(sc, P, TOPK_P // 8)
                to_mask(sc).then_inc(top_p, 1)
            dve.wait_ge(do_hi, 1)
            for gp in range(2):
                for e in range(2):
                    r = slice(HD * e, HD * e + HD)
                    src = PS[r, 0, 0:2 * P].rearrange("p (b g j) -> p g j b", b=DB, g=2)
                    m, h = slice(4 * gp, 4 * gp + 4), 8 * gp + 4 * e
                    ins = V.tensor_tensor(XL[r, m, SEQ:TOK], src[:, gp, h:h + 4, :],
                                          XH[r, m, SEQ:TOK].bitcast(F32), ALU.subtract)
            ins.then_inc(do_lo, 1)

            def last_top(i):
                sc = SC[:, QT - 2, :]
                if i < TOPK_P // 16:
                    take_rounds(sc, P, 2)
                if i == TOPK_P // 16:
                    to_mask(sc).then_inc(top_p, 1)

            prompt_attention(turns_a, False, last_top)
            with dve.Fori(0, 4) as i:
                for s in range(2):
                    dve.wait_ge(hi_done, i * 2 + (A_OUT + s + 3))
                    low_part(None, s)
                    dve.wait_ge(unit_done, i * 2 + (A_OUT + s + 1))
                    add_residual(i, s)
            layer_norm(0, 0, False)
            dve.wait_ge(ya_init, 2)
            mlp(MLP0, 8)
            layer_norm(1, 1, False)
            with dve.Fori(0, 5) as i:
                for s in range(2):
                    dve.wait_ge(hi_done, i * 2 + (B_IN + s + 3))
                    low_part(None, s)
            dve.wait_ge(ev_act, A_OUT + 10)
            dve.wait_ge(win_in, 32)
            V.tensor_copy(KW[:, :, P:P + 1],
                          UQ[:, 4, SEQ:TOK].rearrange("p (b o) -> p b o", o=1))
            dve.wait_ge(z_qb, 3)
            qv = QB[:, 0:DB * 144].rearrange("p (b x) -> p b x", x=144)
            for e in range(2):
                r = slice(HD * e, HD * e + HD)
                ins = V.tensor_copy(qv[r, :, 8 * e:8 * e + 8],
                                    UQ[r, 6:14, SEQ:TOK].rearrange("p j b -> p b j"))
            ins.then_inc(qb_ready, 1)
            sample_softmax(2, PS[:, 0, 0:P], P, True)
            dve.wait_ge(do_hi, 2)
            for e in range(2):
                r = slice(HD * e, HD * e + HD)
                src = PS[r, 7, 0:P].rearrange("p (b j) -> p j b", b=DB)
                ins = V.tensor_tensor(XL[r, :, SEQ:TOK], src[:, 8 * e:8 * e + 8, :],
                                      XH[r, :, SEQ:TOK].bitcast(F32), ALU.subtract)
            ins.then_inc(do_lo, 1)
            dve.wait_ge(bwin, NH)
            prompt_attention(turns_b, True)
            with dve.Fori(0, 4) as i:
                for s in range(2):
                    dve.wait_ge(hi_done, i * 2 + (B_OUT + s + 3))
                    low_part(None, s)
                    dve.wait_ge(unit_done, i * 2 + (B_OUT + s + 1))
                    add_residual(i, s)
            layer_norm(2, 2, False)
            dve.wait_ge(ya_init, 4)
            dve.wait_ge(outs, 16 * 9)
            mlp(MLP1, 80)
            layer_norm(3, 3, True)


def w_unit_list(w, cols):
    k = w.shape[0]
    u = w[:, np.concatenate(cols)].reshape(k // P, P, len(cols), P)
    return u.transpose(2, 1, 0, 3).reshape(len(cols), P, (k // P) * P)


def kernel(**inputs):
    import concourse.bacc as bacc
    from concourse.bass_utils import run_bass_kernel_spmd

    a = {k: np.asarray(v) for k, v in inputs.items()}
    ar = np.arange
    hcols = lambda h: ar(HD * h, HD * h + HD)
    wa, wb = a["a_w_in"][0], a["b_w_in"][0]
    q_a = [np.concatenate([hcols(h) for h in a_heads(p)]) for p in range(PAIRS)]
    q_b = [np.concatenate([hcols(h) for h in b_heads(p)]) for p in range(PAIRS)]
    o_k, o_v, o_qi, o_ki, o_wi = 1024, 1280, 1536, 2048, 2112
    tiles = lambda o, n: [ar(o + P * i, o + P * i + P) for i in range(n)]
    parts = [w_unit_list(wa, tiles(o_qi, 4) + tiles(o_k, 2) + q_a),
             w_unit_list(a["a_w_out"][0][np.concatenate(q_a)], tiles(0, 8))]

    def mlp_units(l):
        w1, w2 = a["mlp_w1"][l], a["mlp_w2"][l]
        out = []
        for c in range(CHUNKS):
            out.append(w_unit_list(w1, tiles(D * c, 8)))
            out.append(w_unit_list(w2[D * c:D * c + D], tiles(0, 8)))
        return out

    parts += mlp_units(0)
    parts += [w_unit_list(wb, tiles(1024, 2) + q_b),
              w_unit_list(a["b_w_out"][0][np.concatenate(q_b)], tiles(0, 8))]
    parts += mlp_units(1) + [np.zeros((2, P, D), np.float32)]
    x = np.concatenate([a["x_prompt"][0], a["x_sample"][:, 0]], axis=0)
    cst, csth = constants()
    ck = a["cache_k"][0].reshape(POOL_PAGES, PAGE, 2, P).transpose(0, 3, 2, 1)
    lnp = np.stack([np.stack([a[n][l].reshape(KT, P).T for n in (f"ln{i}_g", f"ln{i}_b")], 1)
                    for l in range(2) for i in (1, 2)], 1)
    arrays = {
        "xT": x.T.reshape(KT, P, TOK).transpose(1, 0, 2),
        "wn": wa[:, np.concatenate([ar(o_ki, o_ki + 72), ar(o_v, o_v + 256)])]
        .reshape(KT, P, NATW).transpose(1, 0, 2),
        "wall": np.concatenate(parts),
        "cacheK": ck.reshape(POOL_PAGES, P, 256),
        "cacheV": a["cache_v"][0].reshape(POOL_PAGES, P, 256),
        "cacheI": a["cache_idx_k"][0].transpose(0, 2, 1),
        "pt": a["page_table"].reshape(1, 64),
        "table": a["rel_bias_table"],
        "trep": np.tile(a["rel_bias_table"], (1, DB)),
        "lnp": lnp,
        "igb": np.broadcast_to(np.stack([a["a_idx_ln_g"][0], a["a_idx_ln_b"][0]]), (P, 2, HD)),
        "snk": np.broadcast_to(a["b_sink"], (P, NH)),
        "snd": np.tile(a["b_sink"][0], DB).reshape(P, 1),
        "swk": a["state_win_k"][0].reshape(DB, P, P).transpose(2, 0, 1),
        "swv": a["state_win_v"][0].reshape(DB, P, P),
        "cst": cst,
        "csth": csth,
    }
    out_shapes = {"yT": (P, KT, TOK), "kT": (P, 2, TOK), "vp": (P, QT, 256), "vs": (DB, 256),
                  "kip": (P, QT, HD), "kis": (DB, HD), "wkT": (P, P), "wv": (P, P),
                  "wksT": (P, DB, P), "wvs": (P, DB, P)}
    nc = bacc.Bacc("TRN2", target_bir_lowering=False, num_devices=1)
    io, feeds = {}, {}
    for n, v in arrays.items():
        feeds[n] = np.ascontiguousarray(v)
        io[n] = nc.dram_tensor(n, v.shape, mybir.dt.from_np(v.dtype), kind="ExternalInput").ap()
    for n, s in out_shapes.items():
        io[n] = nc.dram_tensor(n, s, F32, kind="ExternalOutput").ap()
    program(nc, io)
    r = run_bass_kernel_spmd(nc, [feeds], core_ids=[0]).results[0]
    y = r["yT"].transpose(2, 1, 0).reshape(TOK, D)
    k = r["kT"].transpose(2, 1, 0).reshape(TOK, 256)
    blocks = lambda v, w: v.transpose(1, 0, 2).reshape(1, 1, QT, P, *w)
    return (y[:SEQ].reshape(1, SEQ, D), y[SEQ:].reshape(DB, 1, D),
            k[:SEQ].reshape(1, 1, QT, P, 4, HD), blocks(r["vp"], (4, HD)), blocks(r["kip"], (HD,)),
            k[SEQ:].reshape(1, DB, 1, 4, HD), r["vs"].reshape(1, DB, 1, 4, HD),
            r["kis"].reshape(1, DB, 1, HD),
            r["wkT"].T.reshape(1, 1, P, 2, HD), r["wv"].reshape(1, 1, P, 2, HD),
            r["wksT"].transpose(1, 2, 0).reshape(1, DB, P, 2, HD),
            r["wvs"].transpose(1, 0, 2).reshape(1, DB, P, 2, HD))
```

```python
from contextlib import ExitStack
import math

import numpy as np

import concourse.bass as bass
from concourse import mybir

F32 = mybir.dt.float32
F32R = mybir.dt.float32r
I32 = mybir.dt.int32
ALU = mybir.AluOpType
ACT = mybir.ActivationFunctionType
AXX = mybir.AxisListType.X

P = 128
D = 1024
KT = D // P
SEQ, DB = 512, 8
TOK = SEQ + DB
TG = TOK // 2
NH, HD = 16, 64
PAST, PAGE = 1024, 128
NPG = PAST // PAGE
POOL_PAGES = 80
IDXH = 8
TOPK_P, TOPK_S = 128, 256
NB_, MAXD = 32, 128
ALPHA = (2 * 2) ** 0.25
NEG = -1e30
TAKEN = -3.0e38
EPS = 1e-5
QSCALE = HD ** -0.5
ISCALE = IDXH ** -0.5 * HD ** -0.5
QT = SEQ // P
NATW = HD + IDXH + 256
PAIRS = NH // 2

A_IN, A_OUT, MLP0, B_IN, B_OUT, MLP1, U_END = 0, 14, 22, 86, 96, 104, 168
CHUNKS = 4
SKEW = 768
POOL_LO = (8, 16)
LO_SKIP = POOL_LO[1] - POOL_LO[0]

KV_PLACE = (0, 1, 2, 3, 7, 8, 4, 5, 6, 7, 8, 4, 5, 3, 6, 7)
EARLY_ROUNDS = 17
TOP_STEPS = 9
EARLY_TOP = 6
SP_FROM = (0, 0, 8, 8, 8, 6) + 10 * (5,)
IDX_SP = 2
STATIC_UNITS = 10


def kv_wait(n):
    mine = [m for m in range(n + 1) if KV_PLACE[m] == KV_PLACE[n]]
    by_sp = sum(NPG - SP_FROM[m] for m in mine)
    return KV_PLACE[n], 16 * (NPG * len(mine) - by_sp), 16 * by_sp


def kv_before(n):
    return max([m + 1 for m in range(n) if KV_PLACE[m] == KV_PLACE[n]], default=0)


def a_heads(p):
    return 8 * (p // 4) + p % 4, 8 * (p // 4) + p % 4 + 4


def b_heads(p):
    return p, p + 8


class Turns:

    def __init__(self, blocks):
        self.steps = []
        for t in range(QT):
            lo, hi = blocks(t)
            pairs = 512 // ((hi - lo) * P)
            self.steps += [(t, p, pairs, lo, hi) for p in range(0, PAIRS, pairs)]
        self.N = len(self.steps)
        self.n0 = 0

    def heads_at(self, i):
        t, p, pairs, lo, hi = self.steps[i]
        return [(e, g, 512 * e + g * (hi - lo) * P) for e in range(2) for g in range(pairs)]


def bucket(dist):
    n = np.maximum(np.asarray(dist), 0)
    exact = NB_ // 2
    nf = np.maximum(n, exact).astype(np.float32)
    large = exact + (np.log(nf / np.float32(exact)) / np.float32(math.log(MAXD / exact))
                     * np.float32(NB_ - exact)).astype(np.int32)
    return np.where(n < exact, n, np.minimum(large, NB_ - 1))


def one_hot(dist):
    return (np.arange(NB_)[:, None] == bucket(dist)[None, :]).astype(np.float32)


C_ID, C_ONE, C_CAUS, C_WIN, C_WD, C_REP, C_END = 0, 128, 256, 384, 640, 704, 832
H_SEQ, H_DEC, H_WIN, H_END = 0, 640, 640 + 1025, 640 + 1025 + 128


def constants():
    c = np.zeros((P, C_END), np.float32)
    i, j = np.arange(P)[:, None], np.arange(P)[None, :]
    c[:, C_ID:C_ID + P] = np.eye(P)
    c[:, C_ONE:C_ONE + P] = 1.0 / D
    c[:, C_CAUS:C_CAUS + P] = np.where(j <= i, 0.0, NEG)
    dist = i + P - np.arange(2 * P)[None, :]
    c[:, C_WIN:C_WIN + 2 * P] = np.where((dist >= 0) & (dist < P), 0.0, NEG)
    for b in range(DB):
        c[b, C_WD + 8 * b:C_WD + 8 * b + 8] = 1.0
        c[b, C_REP + NH * b:C_REP + NH * b + NH] = 1.0
    h = np.concatenate([one_hot(511 - np.arange(640)), one_hot(PAST - np.arange(PAST + 1)),
                        one_hot(P - 1 - np.arange(P))], axis=1)
    return c, np.ascontiguousarray(h)


def program(nc, io):
    with ExitStack() as ctx:
        words = [0]
        base = nc.sbuf_base
        usable = nc.sbuf_usable_end

        def place(name, shape, dt=F32, at=None):
            n = int(np.prod(shape[1:]))
            if at is None:
                at = words[0]
                words[0] += (n + 7) // 8 * 8
            off = (base + 31) // 32 * 32 + 4 * at
            assert off + 4 * n <= usable, (name, off + 4 * n, usable)
            return nc.alloc_sbuf_tensor_at(name, shape, dt, offset=off)

        def sem(name):
            return ctx.enter_context(nc.semaphore(name))

        UQ = place("UQ", [P, 14, TOK])
        YA = place("YA", [P, KT, TOK], at=6 * TOK)
        SEQS = place("SEQS", [16, 640], at=12 * TOK)
        X32 = place("X32", [P, KT, TOK])
        xw = words[0]
        XH = place("XH", [P, KT, TOK], F32R)
        XL = place("XL", [P, KT, TOK], F32R)
        KVR = place("KVR", [P, 3, NPG, 256], at=xw)
        BT = place("BT", [P, NH, 512], at=xw + 16640)
        KVB = place("KVB", [P, 4, NPG, 256], at=xw + 16640)
        VNEW = place("VNEW", [1, DB, 256], at=xw + 3 * 2048)
        hw = words[0]
        HH = place("HH", [P, KT, TOK], F32R)
        HL = place("HL", [P, KT, TOK], F32R)
        SQ1 = place("SQ1", [P, KT, TG], at=hw)
        IK = place("IK", [P, 4, 1025], at=hw)
        SR = place("SR", [HD, 1025], at=hw + 4104)
        QB = place("QB", [P, 2176], at=hw + 4104 + 1032)
        PB = place("PB", [P, 3, 1024], at=hw)
        PTB = place("PTB", [P, 2, 1024], at=hw + 3072)
        OV = place("OV", [NH, DB, 256], at=hw + 4104 + 1032)
        KVI = place("KVI", [P, 2, NPG, 256], at=hw)
        BM = place("BM", [P, 2, 2, 512], at=0)
        PD = place("PD", [P, 1025], at=hw + 4096)
        PDW = place("PDW", [P, P], at=hw + 7344)
        KW = place("KW", [P, DB, 129], at=hw + 6304)
        words[0] = xw + 16640 + NH * 512
        WRAW = place("WRAW", [P, 2, KT, P])
        WHI = place("WHI", [P, 2, KT, P], F32R)
        WLO = place("WLO", [P, 2, KT, P], F32R)
        rw = words[0]
        RL = place("RL", [P, TOK])
        S32 = place("S32", [P, TOK])
        PTD = place("PTD", [P, NPG, P], at=rw)
        NAT = place("NAT", [P, 5, NATW])
        KID = place("KID", [P, 5, 2, HD])
        KIT = place("KIT", [P, TOK])
        DS = place("DS", [DB, 1025])
        ww = words[0]
        WN = place("WN", [P, KT, NATW])
        SC = place("SC", [P, 3, 512], at=ww)
        RS = place("RS", [P, 2, 512], at=ww + 1536)
        VW = place("VW", [P, DB, P], at=ww)
        SQ0 = place("SQ0", [P, KT, TG], at=ww)
        CST = place("CST", [P, C_END])
        CH = place("CH", [NB_, H_END - 640])
        CHS = place("CHS", [NB_, 640], at=11 * TOK - 120)
        TAB = place("TAB", [NB_, 16])
        TREP = place("TREP", [NB_, P])
        LNP = place("LNP", [P, 4, 2, KT])
        IGB = place("IGB", [P, 2, HD])
        SNK = place("SNK", [P, NH])
        SND = place("SND", [P, 1])
        WB = place("WB", [HD, DB])
        WD = place("WD", [DB, HD])
        PT = place("PT", [1, 64], I32)
        EPSC = place("EPSC", [P, 1])
        KST = place("KST", [P, 5, 6])
        KMV = place("KMV", [P, 5, 2])
        KSD = place("KSD", [P, 5])
        MX8 = place("MX8", [P, 8])
        MX = place("MX", [P, 3, 8])
        NMX = place("NMX", [P, 3, 8])
        SM = place("SM", [P, 3, 8])
        SKE = place("SKE", [P, 3, 8])
        DST = place("DST", [P, 4])
        PNEW = place("PNEW", [1, P])
        YS = place("YS", [P, TOK], at=rw)
        RSTD = place("RSTD", [P, TOK], at=rw + TOK)

        ident = CST[:, C_ID:C_ID + P]
        ones = CST[:, C_ONE:C_ONE + P]
        caus = CST[:, C_CAUS:C_CAUS + P]
        ohd = CH[:, 0:1025]
        ohw = CH[:, 1025:1025 + P]

        PS = ctx.enter_context(nc.psum_tensor("PS", [P, 8, 512], F32))
        PSF = PS[:].rearrange("p a b -> p (a b)")
        bskew = nc.dram_tensor("bias_skewed", [P, NH, SKEW], F32, kind="Internal").ap()
        bseq = nc.dram_tensor("bias_seq", [16, 640], F32, kind="Internal").ap()

        x_in = [sem(f"x_in{q}") for q in range(4)]
        cst_in = sem("cst_in")
        pt_in = sem("pt_in")
        raw_in = [sem("raw_in0"), sem("raw_in1")]
        idx_in, idx_sp = sem("idx_in"), sem("idx_sp")
        kv_pool = [sem(f"kv_pool{i}") for i in range(9)]
        kv_sp = [sem(f"kv_sp{i}") for i in range(9)]
        vnew_in = sem("vnew_in")
        toe_out, toe_skew, toe_in = sem("toe_out"), sem("toe_skew"), sem("toe_in")
        win_in, vwin_in = sem("win_in"), sem("vwin_in")
        outs = sem("outs")
        hi_done = sem("hi_done")
        lo_pool, lo_dve = sem("lo_pool"), sem("lo_dve")
        unit_done = sem("unit_done")
        ev_act, ev_dve = sem("ev_act"), sem("ev_dve")
        relu_done = sem("relu_done")
        hh_done, hl_done = sem("hh_done"), sem("hl_done")
        x_hi, x_lo = sem("x_hi"), sem("x_lo")
        nat_mm, nat_ev = sem("nat_mm"), sem("nat_ev")
        kstat, ksd, kid = sem("kstat"), sem("ksd"), sem("kid")
        kit_mm, kit_ev = sem("kit_mm"), sem("kit_ev")
        seq_mm, seq_ev = sem("seq_mm"), sem("seq_ev")
        is_mm, is_relu, is_acc = sem("is_mm"), sem("is_relu"), sem("is_acc")
        qib_ready, ikn_ready = sem("qib_ready"), sem("ikn_ready")
        ds_mm, ds_relu, ds_sum = sem("ds_mm"), sem("ds_relu"), sem("ds_sum")
        ds_ev = sem("ds_ev")
        wd_ready, wb_mm, wb_ev = sem("wd_ready"), sem("wb_mm"), sem("wb_ev")
        top_p, top_s = sem("top_p"), sem("top_s")
        qb_ready = sem("qb_ready")
        kv_used = sem("kv_used")
        dl_mm, d_mx, d_exp, d_p = sem("dl_mm"), sem("d_mx"), sem("d_exp"), sem("d_p")
        dt_mm, dt_ev, do_mm, do_hi, do_lo = (sem("dt_mm"), sem("dt_ev"), sem("do_mm"),
                                             sem("do_hi"), sem("do_lo"))
        qk_mm, smx, pexp, pnorm = sem("qk_mm"), sem("smx"), sem("pexp"), sem("pnorm")
        pt_mm, pt_ev, bm_ready = sem("pt_mm"), sem("pt_ev"), sem("bm_ready")
        ov_mm, ov_ev = sem("ov_mm"), sem("ov_ev")
        o_mm, o_hi, o_lo = sem("o_mm"), sem("o_hi"), sem("o_lo")
        mean_mm, dev, sqr, var_mm, std_d, x_new = (sem("mean_mm"), sem("dev"), sem("sqr"),
                                                   sem("var_mm"), sem("std_d"), sem("x_new"))
        ya_init = sem("ya_init")
        half_done = sem("half_done")
        scaled, x_odd = sem("scaled"), sem("x_odd")
        ys_done = sem("ys_done")
        z_nat, z_qb, bwin = sem("z_nat"), sem("z_qb"), sem("bwin")
        vt_mm, vt_ev = sem("vt_mm"), sem("vt_ev")
        own = sem("own")
        own_p = sem("own_p")

        def kv_place(n):
            pl = KV_PLACE[n]
            return KVB[:, pl] if pl < 4 else KVR[:, pl - 4] if pl < 7 else KVI[:, pl - 7]

        def load_page(eng, n, pg):
            pl, b = KV_PLACE[n], n % DB
            cache = io["cacheK"] if n < DB else io["cacheV"]
            dst = kv_place(n)[:, bass.ds(pg, 1), :]
            page = eng.value_load(PT[0:1, bass.ds(pg + b * NPG, 1)],
                                  min_val=0, max_val=POOL_PAGES - 1)
            eng.dma_start(dst.rearrange("p o n -> p (o n)"),
                          cache[bass.ds(page, 1), :, :].rearrange("o p n -> (o p) n")
                          ).then_inc((kv_sp if eng is nc.sync else kv_pool)[pl], 16)

        def load_index_page(eng, half, c, pg, done):
            page = eng.value_load(PT[0:1, bass.ds(c * 16 + (8 * half + pg), 1)],
                                  min_val=0, max_val=POOL_PAGES - 1)
            eng.dma_start(IK[HD * half:HD * half + HD, bass.ds(c, 1), pg * P:(pg + 1) * P],
                          io["cacheI"][bass.ds(page, 1), :, :].rearrange("o d k -> d o k")
                          ).then_inc(done, 16)

        def wait_place(eng, n):
            if n == 4:
                eng.wait_ge(ds_sum, 1)
            if n == 6:
                eng.wait_ge(unit_done, A_OUT)
            if kv_before(n):
                eng.wait_ge(kv_used, kv_before(n))

        turns_a = Turns(lambda t: (0, t + 1))
        turns_b = Turns(lambda t: (max(t - 1, 0), t + 1))
        turns_b.n0 = turns_a.N

        block = ctx.enter_context(nc.Block())

        @block.sync
        def _(sp):
            def load_unit(u, slot):
                sp.dma_start(WRAW[:, slot, :, :].rearrange("p k m -> p (k m)"),
                             io["wall"][bass.ds(u, 1), :, :].rearrange("o p n -> (o p) n")
                             ).then_inc(raw_in[slot], 16)

            def load_bias(pl):
                h = slice(4 * pl, 4 * pl + 4)
                sp.dma_start(BT[:, h, :], bskew[:, h, 127:127 + 512]).then_inc(toe_in, 16)

            sp.dma_start(PT[:], io["pt"]).then_inc(pt_in, 16)
            for q in range(4):
                k = slice(2 * q, 2 * q + 2)
                sp.dma_start(WN[:, k, :], io["wn"][:, k, :]).then_inc(x_in[q], 16)
                sp.dma_start(X32[:, k, :], io["xT"][:, k, :]).then_inc(x_in[q], 16)
            for dst, src in ((CST[:], io["cst"]), (CH[:], io["csth"][:, 640:]),
                             (CHS[:], io["csth"][:, 0:640]), (TAB[:], io["table"]),
                             (TREP[:], io["trep"]), (LNP[:], io["lnp"]), (IGB[:], io["igb"]),
                             (SNK[:], io["snk"]), (SND[:], io["snd"])):
                sp.dma_start(dst, src).then_inc(cst_in, 16)
            load_unit(0, 0)
            load_unit(1, 1)
            sp.wait_ge(pt_in, 16)
            with sp.Fori(4 - IDX_SP, 4) as c:
                for pg in range(NPG):
                    load_index_page(sp, 1, c, pg, idx_sp)
            sp.wait_ge(seq_ev, 1)
            sp.dma_start(bseq, SEQS[:]).then_inc(toe_out, 16)
            with sp.Fori(1, POOL_LO[0] // 2 + 1) as i:
                for s in range(2):
                    sp.wait_ge(lo_dve, i * 2 + (s - 1))
                    load_unit(i * 2 + s, s)
                for b in range(2):
                    for q in range(2):
                        load_page(sp, b, i * 2 + (q - 2))
            with sp.Fori(POOL_LO[0] // 2 + 1, POOL_LO[1] // 2 + 1) as i:
                for s in range(2):
                    sp.wait_ge(lo_pool, i * 2 + (s - 1 - POOL_LO[0]))
                    load_unit(i * 2 + s, s)
            sp.wait_ge(ds_sum, 1)
            for n in range(5, 2 * DB):
                wait_place(sp, n)
                with sp.Fori(SP_FROM[n], NPG) as pg:
                    load_page(sp, n, pg)
                if n == DB + 1:
                    sp.wait_ge(toe_skew, 16 * 4)
                    for pl in range(3):
                        sp.wait_ge(kv_used, pl + 1)
                        load_bias(pl)
            sp.wait_ge(kv_used, KV_PLACE.index(3, 4) + 1)
            load_bias(3)
            with sp.Fori(POOL_LO[1] // 2 + 1, (U_END + 2) // 2) as i:
                for s in range(2):
                    sp.wait_ge(lo_dve, i * 2 + (s - 1 - LO_SKIP))
                    load_unit(i * 2 + s, s)
            for g in range(2):
                for q in range(4):
                    sp.wait_ge(x_new, 24 + 4 * g + q + 1)
                    sp.wait_ge(x_odd, 24 + 4 * g + q + 1)
                    k, c = slice(2 * q, 2 * q + 2), slice(TG * g, TG * g + TG)
                    sp.dma_start(io["yT"][:, k, c], X32[:, k, c]).then_inc(outs, 16)
            sp.wait_ge(outs, 16 * (9 + 8))

        @block.gpsimd
        def _(pool):
            nc.gpsimd.memset(NAT[:, 4, :], 0.0).then_inc(z_nat, 1)
            nc.gpsimd.memset(QB[:], 0.0).then_inc(z_qb, 1)
            pool.wait_ge(pt_in, 16)
            for half in range(2):
                with pool.Fori(0, 4 - half * IDX_SP) as c:
                    for pg in range(NPG):
                        load_index_page(pool, half, c, pg, idx_in)

            def low_part(u, slot):
                pool.wait_ge(hi_done, u + 1)
                nc.gpsimd.tensor_tensor(WLO[:, slot], WRAW[:, slot], WHI[:, slot].bitcast(F32),
                                        ALU.subtract).then_inc(lo_pool, 1)

            for n in (2, 3):
                with pool.Fori(0, NPG) as pg:
                    load_page(pool, n, pg)
            pool.wait_ge(ds_mm, 3)
            nc.gpsimd.memset(QB[:], 0.0).then_inc(z_qb, 1)
            wait_place(pool, 4)
            with pool.Fori(0, 4) as pg:
                load_page(pool, 4, pg)
            for u in range(POOL_LO[0], POOL_LO[0] + 2):
                low_part(u, u % 2)
                for q in range(2):
                    load_page(pool, 4, 4 + 2 * (u % 2) + q)
            with pool.Fori(POOL_LO[0] // 2 + 1, POOL_LO[1] // 2) as i:
                for s in range(2):
                    low_part(i * 2 + s, s)
                    load_page(pool, 5, i * 2 + (s - POOL_LO[0] - 2))

            for n in range(6, 2 * DB):
                wait_place(pool, n)
                with pool.Fori(0, SP_FROM[n]) as pg:
                    load_page(pool, n, pg)
                if n == DB - 1:
                    pool.wait_ge(nat_ev, 5)
                    for b in range(DB):
                        pool.dma_start(VNEW[0:1, b, :], NAT[b:b + 1, 4, HD + IDXH:NATW]
                                       ).then_inc(vnew_in, 16)
            pool.wait_ge(toe_in, 64)
            for i, (t, p, pairs, lo, hi) in enumerate(turns_a.steps):
                w = (hi - lo) * P
                off = 384 - t * P
                if t and p == 0:
                    pool.wait_ge(top_p, t)
                if i >= 2:
                    pool.wait_ge(smx, i - 1)
                mask = caus if t == 0 else SC[:, t - 1, 0:w]
                h, j = 8 * (p // 4), p % 4
                nc.gpsimd.tensor_tensor(
                    BM[:, i % 2, :, 0:pairs * w].rearrange("p e (g w) -> p e g w", w=w),
                    BT[:, h:h + 8, off:off + w].rearrange("p (e g) w -> p e g w", e=2)[
                        :, :, j:j + pairs, :],
                    mask.rearrange("p (a b w) -> p a b w", a=1, b=1).broadcast_to(
                        [P, 2, pairs, w]), ALU.add).then_inc(bm_ready, 1)
            for layer in range(2):
                for g in range(2):
                    pool.wait_ge(x_new, 16 * layer + 4 * g + 4)
                    pool.wait_ge(x_odd, 16 * layer + 4 * g + 4)
                    c = slice(TG * g, TG * g + TG)
                    nc.gpsimd.tensor_scalar(YA[:, :, c], X32[:, :, c], float(ALPHA), None,
                                            ALU.mult).then_inc(ya_init, 1)
                if layer == 0:
                    for h in range(NH):
                        nc.gpsimd.tensor_tensor(BT[:, h, 256:512], BT[:, h, 256:512],
                                                CST[:, C_WIN:C_WIN + 2 * P], ALU.add
                                                ).then_inc(bwin, 1)
                    pool.wait_ge(var_mm, 4)
                    pool.dma_start(KW[:, :, 0:P], io["swk"]).then_inc(win_in, 16)
                    pool.dma_start(VW[0:P - 1, :, :],
                                   io["swv"][:, 1:P, :].rearrange("b k d -> k b d")
                                   ).then_inc(win_in, 16)
                    nc.gpsimd.memset(QB[:, 0:DB * 144], 0.0).then_inc(z_qb, 1)
                    pool.wait_ge(vt_ev, 5)
                    for b in range(DB):
                        pool.dma_start(VW[P - 1:P, b, :], NAT[b:b + 1, 4, 0:P]
                                       ).then_inc(vwin_in, 16)

        @block.tensor
        def _(pe):
            def unit(u, slot, hi, lo, waits=None):
                for k in range(KT):
                    if waits and k in waits:
                        waits[k]()
                    for w, parts in ((WHI, (hi, lo)), (WLO, (hi,))):
                        for x in parts:
                            for g in range(2):
                                mm = pe.matmul(PS[:, 2 * slot + g, 0:TG], w[:, slot, k, :],
                                               x[:, k, TG * g:TG * g + TG],
                                               start=(k == 0 and w is WHI and x is hi),
                                               stop=(k == KT - 1 and w is WLO))
                mm.then_inc(unit_done, 1)

            def wait_kv(n):
                pl, by_pool, by_sp = kv_wait(n)
                if by_pool:
                    pe.wait_ge(kv_pool[pl], by_pool)
                if by_sp:
                    pe.wait_ge(kv_sp[pl], by_sp)

            def wait_lo(u):
                if u < POOL_LO[0]:
                    pe.wait_ge(lo_dve, u + 1)
                elif u < POOL_LO[1]:
                    pe.wait_ge(lo_pool, u + 1 - POOL_LO[0])
                else:
                    pe.wait_ge(lo_dve, u + 1 - LO_SKIP)

            def mean_mms(n, g, ev):
                pe.wait_ge(ev_dve, ev)
                pe.wait_ge(ys_done, 7 * (n + 1))
                c = slice(TG * g, TG * g + TG)
                pe.matmul(PS[:, 4 + g, 0:TG], ones, YS[:, c], start=True, stop=False)
                pe.matmul(PS[:, 4 + g, 0:TG], ones, YA[:, KT - 2, c], start=False, stop=False)
                pe.matmul(PS[:, 4 + g, 0:TG], ones, YA[:, KT - 1, c], start=False, stop=True
                          ).then_inc(mean_mm, 1)

            def variance_mms(n, g):
                sq = (SQ0, SQ1)[g]
                for k in range(KT):
                    if k % 2 == 0:
                        pe.wait_ge(sqr, 8 * n + 4 * g + k // 2 + 1)
                    mm = pe.matmul(PS[:, 6 + g, 0:TG], ones, sq[:, k, :],
                                   start=(k == 0), stop=(k == KT - 1))
                mm.then_inc(var_mm, 1)

            def part(g, s, k, hi, lo, done=None):
                for w, parts in ((WHI, (hi, lo)), (WLO, (hi,))):
                    for x in parts:
                        mm = pe.matmul(PS[:, 2 * s + g, 0:TG], w[:, s, k, :],
                                       x[:, k, TG * g:TG * g + TG],
                                       start=(k == 0 and w is WHI and x is hi),
                                       stop=(k == KT - 1 and w is WLO))
                if k == KT - 1 and done is not None:
                    mm.then_inc(done, 1)

            def last_pair(n, u, hi, lo, ev):
                for s in range(2):
                    pe.wait_ge(lo_dve, u + s + 1 - LO_SKIP)
                    pe.wait_ge(ev_dve, ev - 1 + s)
                    for k in range(KT):
                        part(0, s, k, hi, lo, half_done if s else None)
                for s in range(2):
                    for k in range(KT):
                        if s == 0 and k == 5:
                            mean_mms(n, 0, ev + 1)
                        part(1, s, k, hi, lo, unit_done)
                mean_mms(n, 1, ev + 2)
                variance_mms(n, 0)
                variance_mms(n, 1)

            def first_pair(n, u):
                pe.wait_ge(lo_dve, u + 2 - LO_SKIP)

                def x_there(g, k):
                    if k % 2 == 0:
                        pe.wait_ge(x_lo, 8 * n + 4 * g + k // 2 + 2)

                for k in range(KT):
                    x_there(0, k)
                    for s in range(2):
                        part(0, s, k, XH, XL)
                for k in range(KT):
                    x_there(1, k)
                    part(1, 0, k, XH, XL, unit_done)
                    if k < 2:
                        part(1, 1, k, XH, XL)
                for k in range(2, KT):
                    part(1, 1, k, XH, XL, unit_done)

            def mlp(n, base, ev_base):
                hbase = 0 if base == MLP0 else 32

                def two(j, hi, lo, waits=None):
                    for s in range(2):
                        pe.wait_ge(lo_dve, j + (s + base + 1 - LO_SKIP))
                        pe.wait_ge(ev_dve, j + (s + ev_base - 1))
                        unit(None, s, hi, lo, waits if s == 0 else None)

                def first_half(c, i0):
                    with pe.Fori(i0, 4) as i:
                        two(c * 16 + i * 2, XH, XL)

                def second_half(c, i1):
                    waits = {k: (lambda k=k: pe.wait_ge(hl_done, c * 8 + (hbase + k + 1)))
                             for k in (5, 6, 7)}
                    waits[0] = lambda: pe.wait_ge(hl_done, c * 8 + (hbase + 5))
                    two(c * 16 + 8, HH, HL, waits)
                    with pe.Fori(1, i1) as i:
                        two(c * 16 + i * 2 + 8, HH, HL)

                first_pair(n, base)
                first_half(0, 1)
                second_half(0, 4)
                with pe.Fori(1, CHUNKS - 1) as c:
                    first_half(c, 0)
                    second_half(c, 4)
                first_half(CHUNKS - 1, 0)
                second_half(CHUNKS - 1, 3)
                last_pair(n + 1, base + 62, HH, HL, ev_base + 62)

            def prompt_attention(tn, ktile, vtile, between=None):
                n0 = tn.n0

                def logits(i):
                    t, p, pairs, lo, hi = tn.steps[i]
                    if i >= 2:
                        pe.wait_ge(smx, n0 + i - 1)
                    for e, g, at in tn.heads_at(i):
                        r = slice(HD * e, HD * e + HD)
                        at += 1024 * (i % 2)
                        mm = pe.matmul(PSF[:, at:at + (hi - lo) * P],
                                       UQ[r, 6 + p + g, t * P:(t + 1) * P],
                                       UQ[r, ktile(p), lo * P:hi * P], start=True, stop=True)
                    mm.then_inc(qk_mm, 1)

                def turn(i):
                    t, p, pairs, lo, hi = tn.steps[i]
                    pe.wait_ge(pnorm, n0 + i + 1)
                    if i >= 1:
                        pe.wait_ge(pt_ev, n0 + i)
                    for e, g, at in tn.heads_at(i):
                        for o in range(at, at + (hi - lo) * P, P):
                            mm = pe.transpose(PSF[:, 2048 + o:2048 + o + P],
                                              PB[:, i % 3, o:o + P], ident)
                    mm.then_inc(pt_mm, 1)

                def output(i):
                    t, p, pairs, lo, hi = tn.steps[i]
                    pe.wait_ge(pt_ev, n0 + i + 1)
                    if i >= 2:
                        pe.wait_ge(o_lo, n0 + i - 1)
                    w = (hi - lo) * P
                    for e in range(2):
                        probs = PTB[:, i % 2, 512 * e:512 * e + pairs * w].rearrange(
                            "p (g w) -> p g w", w=w)
                        for kb in range(hi - lo):
                            mm = pe.matmul(PS[HD * e:HD * e + HD, 6 + i % 2, 0:pairs * P],
                                           vtile(lo + kb, p, e),
                                           probs[:, :, kb * P:(kb + 1) * P],
                                           start=(kb == 0), stop=(kb == hi - lo - 1))
                    mm.then_inc(o_mm, 1)

                logits(0)
                logits(1)
                if between:
                    between(-1)
                for i in range(tn.N + 1):
                    if i + 2 < tn.N:
                        logits(i + 2)
                    if i < tn.N:
                        turn(i)
                    if between:
                        between(i)
                    if i >= 1:
                        output(i - 1)

            for k in range(KT):
                if k % 2 == 0:
                    pe.wait_ge(x_in[k // 2], 32)
                for t in range(5):
                    m = P if t < QT else DB
                    mm = pe.matmul(PS[0:m, t, 0:NATW], X32[:, k, t * P:t * P + m], WN[:, k, :],
                                   start=(k == 0), stop=(k == KT - 1))
                    if k == KT - 1:
                        mm.then_inc(nat_mm, 1)
            pe.wait_ge(cst_in, 16 * 9)
            pe.matmul(PS[0:16, 6, 0:512], TAB[:], CHS[:, 0:512], start=True, stop=True)
            pe.matmul(PS[0:16, 7, 0:P], TAB[:], CHS[:, 512:640], start=True, stop=True
                      ).then_inc(seq_mm, 1)
            pe.wait_ge(nat_ev, 5)
            pe.wait_ge(x_lo, 1)
            items = [(t, h) for t in range(1, QT) for h in range(IDXH)]
            spans = ((0, 512), (512, 1024), (1024, 1025))
            for u in range(STATIC_UNITS):
                if u == 2:
                    pe.wait_ge(kid, 1)
                    for t in range(QT):
                        pe.transpose(PS[:, 4, t * P:(t + 1) * P],
                                     KID[:, t, :, :].rearrange("p a d -> p (a d)"), ident)
                    pe.transpose(PS[:, 5, 0:DB], KID[0:DB, 4, :, :].rearrange("p a d -> p (a d)"),
                                 CST[0:DB, 0:DB])
                    pe.wait_ge(wd_ready, 1)
                    pe.wait_ge(seq_ev, 1)
                    pe.transpose(PS[0:HD, 6, 0:DB], WD[:], CST[0:DB, 0:DB]).then_inc(kit_mm, 1)
                if u == 5:
                    pe.wait_ge(kit_ev, 2)
                    pe.wait_ge(wb_ev, 1)
                    pe.wait_ge(qib_ready, 1)
                    pe.wait_ge(ikn_ready, 1)
                    for c0, c1 in spans:
                        for c in range(4):
                            mm = pe.matmul(PSF[0:HD, 2048 + c0:2048 + c1],
                                           QB[:, HD * c:HD * c + HD], IK[:, c, c0:c1],
                                           start=(c == 0), stop=(c == 3))
                        mm.then_inc(ds_mm, 1)
                if u == 6:
                    for n, (c0, c1) in enumerate(spans):
                        pe.wait_ge(ds_relu, n + 1)
                        mm = pe.matmul(PSF[0:DB, 2048 + c0:2048 + c1], WB[:], SR[:, c0:c1],
                                       start=True, stop=True)
                    mm.then_inc(ds_sum, 1)
                if u >= STATIC_UNITS - 3:
                    n0 = IDXH * (u - STATIC_UNITS + 3)
                    for n in range(n0, n0 + IDXH):
                        t, h = items[n]
                        if n == 0:
                            pe.wait_ge(ds_ev, 1)
                            pe.wait_ge(ev_act, 4)
                        if n >= 4:
                            pe.wait_ge(is_relu, n - 3)
                        r = slice(HD * (h % 2), HD * (h % 2) + HD)
                        pe.matmul(PS[:, 4 + n % 4, 0:(t + 1) * P],
                                  UQ[r, h // 2, t * P:(t + 1) * P], KIT[r, 0:(t + 1) * P],
                                  start=True, stop=True).then_inc(is_mm, 1)
                wait_lo(u)
                if u >= 2:
                    pe.wait_ge(ev_act, u - 1)
                unit(u, u % 2, XH, XL)
            with pe.Fori(STATIC_UNITS // 2, A_OUT // 2) as i:
                for s in range(2):
                    pe.wait_ge(lo_pool, i * 2 + (s + 1 - POOL_LO[0]))
                    pe.wait_ge(ev_act, i * 2 + (s - 1))
                    unit(None, s, XH, XL)

            pe.wait_ge(ev_act, A_OUT)
            pe.wait_ge(qb_ready, 1)
            pe.wait_ge(is_relu, len(items))
            for c0, c1 in spans:
                pe.matmul(PSF[:, c0:c1], TREP[:], ohd[:, c0:c1], start=True, stop=False)
            for b in range(DB):
                wait_kv(b)
                for gp in range(2):
                    q = QB[:, (2 * b + gp) * P:(2 * b + gp + 1) * P]
                    for half in range(2):
                        mm = pe.matmul(PSF[:, 512 * half:512 * half + 512], q,
                                       kv_place(b)[:, 4 * half:4 * half + 4, gp * P:(gp + 1) * P],
                                       start=False, stop=False)
                    pe.matmul(PSF[:, 1024:1025], q, UQ[:, 4 + gp, SEQ + b:SEQ + b + 1],
                              start=False, stop=False)
                mm.then_inc(kv_used, 1)
            pe.wait_ge(top_s, 1)
            for c0, c1 in spans:
                mm = pe.matmul(PSF[:, c0:c1], CST[0:DB, C_REP:C_REP + P], DS[:, c0:c1],
                               start=False, stop=True)
            mm.then_inc(dl_mm, 1)
            pe.wait_ge(d_p, 1)
            for k in range(NPG):
                pe.transpose(PS[:, 4 + k // 4, (k % 4) * P:(k % 4 + 1) * P],
                             PD[:, k * P:(k + 1) * P], ident)
            pe.transpose(PS[0:1, 6, 0:P], PD[:, 1024:1025], ident).then_inc(dt_mm, 1)
            pe.wait_ge(dt_ev, 1)
            pe.wait_ge(vnew_in, 16 * DB)
            for b in range(DB):
                n = DB + b
                wait_kv(n)
                o = PSF[0:NH, 2048 + 256 * b:2048 + 256 * b + 256]
                rows = slice(NH * b, NH * b + NH)
                for k in range(NPG):
                    mm = pe.matmul(o, PTD[:, k, rows], kv_place(n)[:, k, :], start=(k == 0),
                                   stop=False)
                mm.then_inc(kv_used, 1)
                pe.matmul(o, PNEW[0:1, rows], VNEW[0:1, b, :], start=False, stop=True
                          ).then_inc(ov_mm, 1)
            for b in range(DB):
                pe.wait_ge(ov_ev, b // 2 + 1)
                for gp in range(2):
                    c = (2 * b + gp) * NH
                    mm = pe.transpose(PS[:, 0, c:c + NH], OV[:, b, gp * P:(gp + 1) * P],
                                      CST[0:NH, 0:NH])
            mm.then_inc(do_mm, 1)
            pe.wait_ge(do_lo, 1)
            prompt_attention(turns_a, lambda p: 4 + p // 4,
                             lambda kb, p, e: NAT[:, kb, 72 + HD * (2 * (p // 4) + e):
                                                  72 + HD * (2 * (p // 4) + e) + HD])
            pe.wait_ge(o_lo, turns_a.N)
            for s in range(2):
                pe.wait_ge(lo_pool, A_OUT + s + 1 - POOL_LO[0])
                unit(None, s, XH, XL)
            with pe.Fori(1, 3) as i:
                for s in range(2):
                    pe.wait_ge(lo_dve, i * 2 + (A_OUT + s + 1 - LO_SKIP))
                    pe.wait_ge(ev_dve, i * 2 + (s - 1))
                    unit(None, s, XH, XL)
            last_pair(0, A_OUT + 6, XH, XL, 6)
            mlp(0, MLP0, 8)
            first_pair(1, B_IN)
            def input_units(i0, i1):
                with pe.Fori(i0, i1) as i:
                    for s in range(2):
                        pe.wait_ge(lo_dve, i * 2 + (B_IN + s + 1 - LO_SKIP))
                        pe.wait_ge(ev_act, i * 2 + (A_OUT + s - 1))
                        unit(None, s, XH, XL)

            input_units(1, 2)
            pe.wait_ge(ev_act, A_OUT + 2)
            for t in range(QT):
                pe.transpose(PS[:, 4, t * P:(t + 1) * P], UQ[:, 5, t * P:(t + 1) * P], ident)
            pe.transpose(PS[0:DB, 5, 0:P], UQ[:, 5, SEQ:TOK], ident).then_inc(vt_mm, 1)
            input_units(2, 5)
            pe.wait_ge(ev_act, A_OUT + 10)
            pe.wait_ge(vt_ev, 5)

            def sample_b(i):
                if i == -1:
                    pe.wait_ge(qb_ready, 2)
                    pe.wait_ge(win_in, 32)
                    pe.matmul(PS[:, 6, 0:P], TREP[:], ohw, start=True, stop=False)
                    for b in range(DB):
                        mm = pe.matmul(PS[:, 6, 0:P], QB[:, b * P:(b + 1) * P],
                                       KW[:, b, 1:129], start=False, stop=(b == DB - 1))
                    mm.then_inc(dl_mm, 1)
                if i == 1:
                    pe.wait_ge(d_p, 2)
                    pe.transpose(PS[:, 7, 0:P], PDW[:], ident).then_inc(dt_mm, 1)
                if i == 2:
                    pe.wait_ge(dt_ev, 2)
                    pe.wait_ge(vwin_in, 16 * DB)
                    for b in range(DB):
                        mm = pe.matmul(PS[:, 7, b * NH:(b + 1) * NH], VW[:, b, :],
                                       PTD[:, 0, b * NH:(b + 1) * NH], start=True, stop=True)
                    mm.then_inc(do_mm, 1)
                    pe.wait_ge(do_lo, 2)

            prompt_attention(turns_b, lambda p: 4,
                             lambda kb, p, e: NAT[:, kb, HD * e:HD * e + HD], sample_b)
            pe.wait_ge(o_lo, turns_a.N + turns_b.N)
            with pe.Fori(0, 3) as i:
                for s in range(2):
                    pe.wait_ge(lo_dve, i * 2 + (B_OUT + s + 1 - LO_SKIP))
                    pe.wait_ge(ev_dve, i * 2 + (72 + s - 1))
                    unit(None, s, XH, XL)
            last_pair(2, B_OUT + 6, XH, XL, 72 + 6)
            mlp(2, MLP1, 80)

        @block.scalar
        def _(act):
            def high_part(u, slot, static=True):
                if isinstance(u, int):
                    act.wait_ge(raw_in[slot], 16 * (u // 2 + 1))
                    if u >= 2:
                        act.wait_ge(unit_done, u - 1)
                nc.scalar.activation(WHI[:, slot], WRAW[:, slot], ACT.Copy).then_inc(hi_done, 1)

            def banks(slot):
                return PS[:, 2 * slot:2 * slot + 2, 0:TG]

            def mlp(base, ev_base):
                def first_half(c):
                    with act.Fori(0, 4) as i:
                        for s in range(2):
                            j = c * 16 + i * 2 + s
                            act.wait_ge(unit_done, j + (base + 1))
                            act.wait_ge(raw_in[s], (c * 8 + i + (base // 2 + 2)) * 16)
                            high_part(None, s)
                            nc.scalar.activation(RL[:].rearrange("p (g t) -> p g t", g=2),
                                                 banks(s), ACT.Relu).then_inc(relu_done, 1)
                            act.wait_ge(ev_dve, j + (ev_base + 1))
                            nc.scalar.activation(HH[:, bass.ds(i * 2 + s, 1), :],
                                                 S32[:].rearrange("p (o t) -> p o t", o=1),
                                                 ACT.Copy).then_inc(hh_done, 1)

                def second_half(c, i1):
                    with act.Fori(4, i1) as i:
                        for s in range(2):
                            j = c * 16 + i * 2 + s
                            act.wait_ge(unit_done, j + (base + 1))
                            act.wait_ge(raw_in[s], (c * 8 + i + (base // 2 + 2)) * 16)
                            high_part(None, s)

                with act.Fori(0, CHUNKS - 1) as c:
                    first_half(c)
                    second_half(c, 8)
                first_half(CHUNKS - 1)
                second_half(CHUNKS - 1, 7)

            def layer_norm(n, nxt, last=False):
                def squares(g):
                    c = slice(TG * g, TG * g + TG)
                    for q in range(4):
                        act.wait_ge(dev, 8 * n + 4 * g + q + 1)
                        nc.scalar.activation((SQ0, SQ1)[g][:, 2 * q:2 * q + 2, :],
                                             YA[:, 2 * q:2 * q + 2, c],
                                             ACT.Square).then_inc(sqr, 1)

                if n == 2:
                    act.wait_ge(outs, 16 * 9)
                squares(0)
                for s in range(2):
                    high_part(nxt + s, s)
                squares(1)
                for g in range(2):
                    c = slice(TG * g, TG * g + TG)
                    act.wait_ge(var_mm, 2 * n + g + 1)
                    nc.scalar.activation(RSTD[:, c], PS[:, 6 + g, 0:TG], ACT.Sqrt,
                                         bias=EPSC[:]).then_inc(std_d, 1)
                for g in range(2):
                    c = slice(TG * g, TG * g + TG)
                    for q in range(4):
                        m, k = 8 * n + 4 * g + q + 1, 2 * q + 1
                        act.wait_ge(scaled, m)
                        nc.scalar.activation(X32[:, k, c], YA[:, k, c], ACT.Identity,
                                             scale=LNP[:, n, 0, k:k + 1],
                                             bias=LNP[:, n, 1, k:k + 1]).then_inc(x_odd, 1)
                        if not last:
                            act.wait_ge(x_new, m)
                            act.wait_ge(x_odd, m)
                            nc.scalar.activation(XH[:, k - 1:k + 1, c], X32[:, k - 1:k + 1, c],
                                                 ACT.Copy).then_inc(x_hi, 1)

            def prompt_attention(tn, sink, between=None):
                n0 = tn.n0

                def exps(i):
                    t, p, pairs, lo, hi = tn.steps[i]
                    act.wait_ge(smx, n0 + i + 1)
                    for j, (e, g, at) in enumerate(tn.heads_at(i)):
                        x = PB[:, i % 3, at:at + (hi - lo) * P]
                        ins = nc.scalar.activation(x, x, ACT.Exp, bias=NMX[:, i % 3, j:j + 1],
                                                   accum_out=SM[:, i % 3, j:j + 1])
                    if sink:
                        x = SKE[:, i % 3, 0:2 * pairs]
                        ins = nc.scalar.activation(x, x, ACT.Exp)
                    ins.then_inc(pexp, 1)

                def turned(i):
                    t, p, pairs, lo, hi = tn.steps[i]
                    w = pairs * (hi - lo) * P
                    act.wait_ge(pt_mm, n0 + i + 1)
                    if i >= 2:
                        act.wait_ge(o_mm, n0 + i - 1)
                    nc.scalar.activation(
                        PTB[:, i % 2, :].rearrange("p (e w) -> p e w", e=2)[:, :, 0:w],
                        PS[:, 4:6, 0:w], ACT.Copy).then_inc(pt_ev, 1)

                def out_high(i):
                    t, p, pairs, lo, hi = tn.steps[i]
                    act.wait_ge(o_mm, n0 + i + 1)
                    nc.scalar.activation(
                        XH[:, p:p + pairs, t * P:(t + 1) * P],
                        PS[:, 6 + i % 2, 0:pairs * P].rearrange("p (g q) -> p g q", q=P),
                        ACT.Copy).then_inc(o_hi, 1)

                exps(0)
                exps(1)
                if between:
                    between(-1)
                for i in range(tn.N + 1):
                    if i < tn.N:
                        turned(i)
                    if i + 2 < tn.N:
                        exps(i + 2)
                    if between:
                        between(i)
                    if i >= 1:
                        out_high(i - 1)

            for q in range(4):
                act.wait_ge(x_in[q], 32)
                k = slice(2 * q, 2 * q + 2)
                ins = nc.scalar.activation(XH[:, k, :], X32[:, k, :], ACT.Copy)
            ins.then_inc(x_hi, 1)
            high_part(0, 0)
            high_part(1, 1)
            act.wait_ge(z_nat, 1)
            for t in range(5):
                m = P if t < QT else DB
                act.wait_ge(nat_mm, t + 1)
                nc.scalar.activation(NAT[0:m, t, :], PS[0:m, t, 0:NATW], ACT.Copy
                                     ).then_inc(nat_ev, 1)
            act.wait_ge(seq_mm, 1)
            nc.scalar.activation(SEQS[:], PSF[0:16, 3072:3072 + 640], ACT.Copy
                                 ).then_inc(seq_ev, 1)
            act.wait_ge(kstat, 1)
            nc.scalar.activation(KSD[:], KMV[:, :, 1], ACT.Sqrt, bias=EPSC[:]).then_inc(ksd, 1)
            items = [(t, h) for t in range(1, QT) for h in range(IDXH)]
            for u in range(STATIC_UNITS):
                if u >= STATIC_UNITS - 3:
                    n0 = IDXH * (u - STATIC_UNITS + 3)
                    for n in range(n0, n0 + IDXH):
                        t, h = items[n]
                        act.wait_ge(is_mm, n + 1)
                        if n >= 2:
                            act.wait_ge(is_acc, n - 1)
                        nc.scalar.activation(RS[:, n % 2, 0:(t + 1) * P],
                                             PS[:, 4 + n % 4, 0:(t + 1) * P], ACT.Relu
                                             ).then_inc(is_relu, 1)
                act.wait_ge(unit_done, u + 1)
                high_part(u + 2, u % 2)
                if u < 6:
                    nc.scalar.activation(UQ[:, u, :].rearrange("p (g t) -> p g t", g=2),
                                         banks(u % 2), ACT.Copy).then_inc(ev_act, 1)
                else:
                    nc.scalar.activation(UQ[:, u, :].rearrange("p (g t) -> p g t", g=2),
                                         banks(u % 2), ACT.Copy, scale=QSCALE
                                         ).then_inc(ev_act, 1)
                if u == 2:
                    act.wait_ge(kit_mm, 1)
                    nc.scalar.activation(KIT[:, 0:512], PS[:, 4, :], ACT.Copy
                                         ).then_inc(kit_ev, 1)
                    nc.scalar.activation(KIT[:, 512:520], PS[:, 5, 0:DB], ACT.Copy
                                         ).then_inc(kit_ev, 1)
                    nc.scalar.activation(WB[:], PS[0:HD, 6, 0:DB], ACT.Copy).then_inc(wb_ev, 1)
                if u == 4:
                    for n, (c0, c1) in enumerate(((0, 512), (512, 1024), (1024, 1025))):
                        act.wait_ge(ds_mm, n + 1)
                        nc.scalar.activation(SR[:, c0:c1], PSF[0:HD, 2048 + c0:2048 + c1],
                                             ACT.Relu).then_inc(ds_relu, 1)
                if u >= STATIC_UNITS - 4:
                    if u == STATIC_UNITS - 4:
                        act.wait_ge(toe_out, 16)
                    i0 = 32 * (u - STATIC_UNITS + 4)
                    act.dma_start(bass.AP(tensor=bskew.tensor, offset=i0 * (NH * SKEW + 1),
                                          ap=[[NH * SKEW + 1, 32], [SKEW, NH], [1, 640]]),
                                  bass.AP(tensor=bseq.tensor, offset=0,
                                          ap=[[0, 32], [640, NH], [1, 640]])
                                  ).then_inc(toe_skew, 16)

            def query_evac(i, s):
                nc.scalar.activation(
                    UQ[:, bass.ds(i * 2 + s, 1), :].rearrange("p o (g t) -> p (o g) t", g=2),
                    banks(s), ACT.Copy, scale=QSCALE).then_inc(ev_act, 1)

            with act.Fori(STATIC_UNITS // 2, A_OUT // 2 - 1) as i:
                for s in range(2):
                    act.wait_ge(unit_done, i * 2 + (s + 1))
                    act.wait_ge(raw_in[s], (i + 2) * 16)
                    high_part(None, s)
                    query_evac(i, s)
            for s in range(2):
                act.wait_ge(unit_done, A_OUT - 2 + s + 1)
                query_evac(A_OUT // 2 - 1, s)
                high_part(A_OUT + s, s)
            act.wait_ge(nat_ev, 5)
            act.dma_start(io["vp"], NAT[:, 0:QT, HD + IDXH:NATW]).then_inc(outs, 16)
            act.dma_start(io["vs"], NAT[0:DB, 4, HD + IDXH:NATW]).then_inc(outs, 16)
            act.wait_ge(kid, 1)
            act.dma_start(io["kip"], KID[:, 0:QT, 0, :]).then_inc(outs, 16)
            act.dma_start(io["kis"], KID[0:DB, 4, 0, :]).then_inc(outs, 16)
            act.wait_ge(ev_act, 6)
            act.dma_start(io["kT"], UQ[:, 4:6, :]).then_inc(outs, 16)

            act.wait_ge(d_mx, 1)
            nc.scalar.activation(PD[:], PSF[:, 0:1025], ACT.Exp, bias=DST[:, 1:2],
                                 accum_out=DST[:, 2:3]).then_inc(d_exp, 1)
            act.wait_ge(dt_mm, 1)
            nc.scalar.activation(PTD[:].rearrange("p k r -> p (k r)"), PSF[:, 2048:2048 + 1024],
                                 ACT.Copy)
            nc.scalar.activation(PNEW[:], PS[0:1, 6, 0:P], ACT.Copy).then_inc(dt_ev, 1)
            for q in range(4):
                act.wait_ge(ov_mm, 2 * q + 2)
                nc.scalar.activation(OV[:, 2 * q:2 * q + 2, :].rearrange("p b n -> p (b n)"),
                                     PS[0:NH, 4 + q, :], ACT.Copy).then_inc(ov_ev, 1)
            act.wait_ge(do_mm, 1)
            for gp in range(2):
                for e in range(2):
                    r = slice(HD * e, HD * e + HD)
                    src = PS[r, 0, 0:2 * P].rearrange("p (b g j) -> p g j b", b=DB, g=2)
                    h = 8 * gp + 4 * e
                    ins = nc.scalar.activation(XH[r, 4 * gp:4 * gp + 4, SEQ:TOK],
                                               src[:, gp, h:h + 4, :], ACT.Copy)
            ins.then_inc(do_hi, 1)
            prompt_attention(turns_a, False)
            with act.Fori(0, 3) as i:
                for s in range(2):
                    act.wait_ge(unit_done, i * 2 + (A_OUT + s + 1))
                    act.wait_ge(raw_in[s], (i + (A_OUT // 2 + 2)) * 16)
                    high_part(None, s)
            layer_norm(0, MLP0)
            mlp(MLP0, 8)
            layer_norm(1, B_IN)
            for s in range(2):
                act.wait_ge(unit_done, B_IN + s + 1)
                high_part(B_IN + 2 + s, s)
                if s == 0:
                    act.wait_ge(outs, 16 * 5)
                nc.scalar.activation(UQ[:, 4 + s, :].rearrange("p (g t) -> p g t", g=2),
                                     banks(s), ACT.Copy).then_inc(ev_act, 1)
            def query_units(i0, i1):
                with act.Fori(i0, i1) as i:
                    for s in range(2):
                        act.wait_ge(unit_done, i * 2 + (B_IN + s + 1))
                        nc.scalar.activation(
                            UQ[:, bass.ds(i * 2 + (4 + s), 1), :].rearrange(
                                "p o (g t) -> p (o g) t", g=2),
                            banks(s), ACT.Copy, scale=QSCALE).then_inc(ev_act, 1)
                        act.wait_ge(raw_in[s], (i + (B_IN // 2 + 2)) * 16)
                        high_part(None, s)

            query_units(1, 2)
            act.wait_ge(vt_mm, 1)
            for t in range(QT):
                nc.scalar.activation(NAT[:, t, 0:P], PS[:, 4, t * P:(t + 1) * P], ACT.Copy
                                     ).then_inc(vt_ev, 1)
            nc.scalar.activation(NAT[0:DB, 4, 0:P], PS[0:DB, 5, 0:P], ACT.Copy).then_inc(vt_ev, 1)
            act.wait_ge(vt_ev, 5)
            act.dma_start(io["wkT"], UQ[:, 4, SEQ - P:SEQ]).then_inc(outs, 16)
            act.dma_start(io["wv"], NAT[:, QT - 1, 0:P]).then_inc(outs, 16)
            query_units(2, 5)

            def sample_b(i):
                if i == -1:
                    act.wait_ge(d_mx, 2)
                    nc.scalar.activation(DST[:, 3:4], SND[:], ACT.Exp, bias=DST[:, 1:2])
                    nc.scalar.activation(PDW[:], PS[:, 6, 0:P], ACT.Exp, bias=DST[:, 1:2],
                                         accum_out=DST[:, 2:3]).then_inc(d_exp, 1)
                if i == 1:
                    act.wait_ge(dt_mm, 2)
                    nc.scalar.activation(PTD[:, 0, :], PS[:, 7, 0:P], ACT.Copy
                                         ).then_inc(dt_ev, 1)
                if i == 2:
                    act.wait_ge(do_mm, 2)
                    for e in range(2):
                        r = slice(HD * e, HD * e + HD)
                        src = PS[r, 7, 0:P].rearrange("p (b j) -> p j b", b=DB)
                        ins = nc.scalar.activation(XH[r, :, SEQ:TOK], src[:, 8 * e:8 * e + 8, :],
                                                   ACT.Copy)
                    ins.then_inc(do_hi, 1)
                    act.wait_ge(qb_ready, 2)
                    act.dma_start(io["wksT"], KW[:, :, 1:P + 1]).then_inc(outs, 16)
                    act.wait_ge(vwin_in, 16 * DB)
                    act.wait_ge(win_in, 32)
                    act.dma_start(io["wvs"], VW[:]).then_inc(outs, 16)

            prompt_attention(turns_b, True, sample_b)
            with act.Fori(0, 3) as i:
                for s in range(2):
                    act.wait_ge(unit_done, i * 2 + (B_OUT + s + 1))
                    act.wait_ge(raw_in[s], (i + (B_OUT // 2 + 2)) * 16)
                    high_part(None, s)
            layer_norm(2, MLP1)
            mlp(MLP1, 80)
            layer_norm(3, U_END, True)

        @block.vector
        def _(dve):
            V = nc.vector
            count = [0]

            def after(ins):
                count[0] += 1
                ins.then_inc(own, 1)
                dve.wait_ge(own, count[0])

            def low_part(u, slot):
                if isinstance(u, int):
                    dve.wait_ge(hi_done, u + 1)
                V.tensor_tensor(WLO[:, slot], WRAW[:, slot], WHI[:, slot].bitcast(F32),
                                ALU.subtract).then_inc(lo_dve, 1)

            def banks(slot):
                return PS[:, 2 * slot:2 * slot + 2, 0:TG]

            def add_residual(i, s):
                m = bass.ds(i * 2 + s, 1)
                V.scalar_tensor_tensor(
                    out=YA[:, m, :].rearrange("p o (g t) -> p (o g) t", g=2),
                    in0=X32[:, m, :].rearrange("p o (g t) -> p (o g) t", g=2),
                    scalar=float(ALPHA), in1=banks(s), op0=ALU.mult, op1=ALU.add
                ).then_inc(ev_dve, 1)

            def sum_tile(n, i, s, ev):
                dve.wait_ge(ev_dve, i * 2 + (ev + s + 1))
                dve.wait_ge(ys_done, i * 2 + (7 * n + s + 1))
                ya = YA[:, bass.ds(i * 2 + s, 1), :].rearrange("p o t -> p (o t)")
                V.tensor_tensor(YS[:], YS[:], ya, ALU.add).then_inc(ys_done, 1)

            def output_units(n, u, ev):
                V.memset(YS[:], 0.0).then_inc(ys_done, 1)
                with dve.Fori(0, 3) as i:
                    for s in range(2):
                        dve.wait_ge(hi_done, i * 2 + (u + s + 3))
                        low_part(None, s)
                        dve.wait_ge(unit_done, i * 2 + (u + s + 1))
                        add_residual(i, s)
                        sum_tile(n, i, s, ev)

            def mlp(n, base, ev_base):
                sq0 = 0 if base == MLP0 else 32

                def first_half(c):
                    with dve.Fori(0, 4) as i:
                        for s in range(2):
                            dve.wait_ge(hi_done, c * 16 + i * 2 + (base + s + 3))
                            low_part(None, s)
                            dve.wait_ge(lo_dve, c * 16 + i * 2 + (base + s + 3 - LO_SKIP))
                            dve.wait_ge(relu_done, c * 8 + i * 2 + (sq0 + s + 1))
                            V.tensor_tensor(S32[:].rearrange("p (g t) -> p g t", g=2),
                                            RL[:].rearrange("p (g t) -> p g t", g=2),
                                            banks(s), ALU.mult
                                            ).then_inc(ev_dve, 1)
                            dve.wait_ge(hh_done, c * 8 + i * 2 + (sq0 + s + 1))
                            m = bass.ds(i * 2 + s, 1)
                            V.tensor_tensor(HL[:, m, :],
                                            S32[:].rearrange("p (o t) -> p o t", o=1),
                                            HH[:, m, :].bitcast(F32), ALU.subtract
                                            ).then_inc(hl_done, 1)

                def second_half(c, i1, total):
                    dve.wait_ge(ya_init, n + 1)
                    with dve.Fori(0, i1) as i:
                        for s in range(2):
                            dve.wait_ge(hi_done, c * 16 + i * 2 + (base + s + 11))
                            low_part(None, s)
                            dve.wait_ge(unit_done, c * 16 + i * 2 + (base + s + 9))
                            m = bass.ds(i * 2 + s, 1)
                            ya = YA[:, m, :].rearrange("p o (g t) -> p (o g) t", g=2)
                            V.tensor_tensor(ya, ya, banks(s), ALU.add).then_inc(ev_dve, 1)
                            if total:
                                sum_tile(n, i, s, ev_base + c * 16 + 8)

                with dve.Fori(0, CHUNKS - 1) as c:
                    first_half(c)
                    second_half(c, 4, False)
                first_half(CHUNKS - 1)
                dve.wait_ge(hl_done, sq0 + 32)
                V.memset(YS[:], 0.0).then_inc(ys_done, 1)
                second_half(CHUNKS - 1, 3, True)

            def layer_norm(n, u, residual, last=False):
                def last_tiles(g):
                    c = slice(TG * g, TG * g + TG)
                    for s in range(2):
                        k = KT - 2 + s
                        ya, new = YA[:, k, c], PS[:, 2 * s + g, 0:TG]
                        if residual:
                            ins = V.scalar_tensor_tensor(out=ya, in0=X32[:, k, c],
                                                         scalar=float(ALPHA), in1=new,
                                                         op0=ALU.mult, op1=ALU.add)
                        else:
                            ins = V.tensor_tensor(ya, ya, new, ALU.add)
                    ins.then_inc(ev_dve, 1)

                def deviations(g):
                    c = slice(TG * g, TG * g + TG)
                    dve.wait_ge(mean_mm, 2 * n + g + 1)
                    for q in range(4):
                        y = YA[:, 2 * q:2 * q + 2, c]
                        V.tensor_tensor(y, y, PS[:, 4 + g:5 + g, 0:TG].broadcast_to([P, 2, TG]),
                                        ALU.subtract).then_inc(dev, 1)

                def new_x(g, q):
                    c = slice(TG * g, TG * g + TG)
                    y = YA[:, 2 * q:2 * q + 2, c]
                    r = RSTD[:, c].rearrange("p (o t) -> p o t", o=1).broadcast_to([P, 2, TG])
                    V.tensor_tensor(y, y, r, ALU.mult).then_inc(scaled, 1)
                    dve.wait_ge(scaled, 8 * n + 4 * g + q + 1)
                    k = 2 * q
                    V.tensor_scalar(X32[:, k, c], YA[:, k, c], LNP[:, n, 0, k:k + 1],
                                    LNP[:, n, 1, k:k + 1], ALU.mult, ALU.add
                                    ).then_inc(x_new, 1)

                def x_low(g, q):
                    if last:
                        return
                    c = slice(TG * g, TG * g + TG)
                    k = slice(2 * q, 2 * q + 2)
                    dve.wait_ge(x_hi, 8 * n + 4 * g + q + 2)
                    V.tensor_tensor(XL[:, k, c], X32[:, k, c], XH[:, k, c].bitcast(F32),
                                    ALU.subtract).then_inc(x_lo, 1)

                dve.wait_ge(half_done, n + 1)
                last_tiles(0)
                deviations(0)
                dve.wait_ge(unit_done, u + 2)
                last_tiles(1)
                low_part(u + 2, 0)
                deviations(1)
                low_part(u + 3, 1)
                for g in range(2):
                    c = slice(TG * g, TG * g + TG)
                    dve.wait_ge(std_d, 2 * n + g + 1)
                    after(V.reciprocal(RSTD[:, c], RSTD[:, c]))
                    for q in range(4):
                        new_x(g, q)
                        if q:
                            x_low(g, q - 1)
                    x_low(g, 3)

            def prompt_attention(tn, sink, between=None):
                n0 = tn.n0

                def softmax_in(i):
                    t, p, pairs, lo, hi = tn.steps[i]
                    w = (hi - lo) * P
                    dve.wait_ge(qk_mm, n0 + i + 1)
                    if i >= 3:
                        dve.wait_ge(pt_mm, n0 + i - 2)
                    if not sink:
                        dve.wait_ge(bm_ready, i + 1)
                    for j, (e, g, at) in enumerate(tn.heads_at(i)):
                        if sink:
                            off = 384 - t * P + lo * P
                            add = BT[:, b_heads(p + g)[e], off:off + w]
                        else:
                            add = BM[:, i % 2, e, g * w:(g + 1) * w]
                        lg = 1024 * (i % 2) + at
                        ins = V.tensor_tensor_reduce(out=PB[:, i % 3, at:at + w],
                                                     in0=PSF[:, lg:lg + w], in1=add,
                                                     scale=1.0, scalar=TAKEN,
                                                     op0=ALU.add, op1=ALU.max,
                                                     accum_out=MX[:, i % 3, j:j + 1])
                    after(ins)
                    mx = MX[:, i % 3, 0:2 * pairs]
                    if sink:
                        sk = SNK[:].rearrange("p (e j) -> p e j", e=2)[:, :, p:p + pairs]
                        mx2 = mx.rearrange("p (e j) -> p e j", e=2)
                        after(V.tensor_tensor(mx2, mx2, sk, ALU.max))
                        V.tensor_tensor(SKE[:, i % 3, 0:2 * pairs].rearrange(
                            "p (e j) -> p e j", e=2), sk, mx2, ALU.subtract)
                    V.tensor_scalar(NMX[:, i % 3, 0:2 * pairs], mx, -1.0, None, ALU.mult
                                    ).then_inc(smx, 1)

                def normalise(i):
                    t, p, pairs, lo, hi = tn.steps[i]
                    sm = SM[:, i % 3, 0:2 * pairs]
                    dve.wait_ge(pexp, n0 + i + 1)
                    if sink:
                        after(V.tensor_tensor(sm, sm, SKE[:, i % 3, 0:2 * pairs], ALU.add))
                    after(V.reciprocal(sm, sm))
                    for j, (e, g, at) in enumerate(tn.heads_at(i)):
                        x = PB[:, i % 3, at:at + (hi - lo) * P]
                        ins = V.tensor_scalar(x, x, SM[:, i % 3, j:j + 1], None, ALU.mult)
                    ins.then_inc(pnorm, 1)

                def out_low(i):
                    t, p, pairs, lo, hi = tn.steps[i]
                    dve.wait_ge(o_hi, n0 + i + 1)
                    m, c = slice(p, p + pairs), slice(t * P, (t + 1) * P)
                    V.tensor_tensor(XL[:, m, c], PS[:, 6 + i % 2, 0:pairs * P].rearrange(
                        "p (g q) -> p g q", q=P), XH[:, m, c].bitcast(F32), ALU.subtract
                        ).then_inc(o_lo, 1)

                softmax_in(0)
                softmax_in(1)
                if between:
                    between(-1)
                for i in range(tn.N + 1):
                    if i < tn.N:
                        normalise(i)
                    if i + 2 < tn.N:
                        softmax_in(i + 2)
                    if between:
                        between(i)
                    if i >= 2:
                        out_low(i - 2)
                out_low(tn.N - 1)

            V.memset(EPSC[:], EPS).then_inc(own, 1)
            count[0] += 1
            dve.wait_ge(x_hi, 1)
            for q in range(4):
                dve.wait_ge(x_in[q], 32)
            V.tensor_tensor(XL[:], X32[:], XH[:].bitcast(F32), ALU.subtract).then_inc(x_lo, 1)
            for u in range(2):
                low_part(u, u)
            dve.wait_ge(nat_ev, 5)
            dve.wait_ge(cst_in, 16 * 9)
            V.tensor_tensor(WD[:].rearrange("p (b h) -> p b h", b=DB),
                            NAT[0:DB, 4:5, HD:HD + IDXH].broadcast_to([DB, DB, IDXH]),
                            CST[0:DB, C_WD:C_WD + HD].rearrange("p (b h) -> p b h", b=DB),
                            ALU.mult).then_inc(wd_ready, 1)
            for t in range(5):
                ins = V.bn_stats(KST[:, t, :], NAT[:, t, 0:HD])
            after(ins)
            for t in range(5):
                ins = V.bn_aggr(KMV[:, t, :], KST[:, t, :])
            ins.then_inc(kstat, 1)
            dve.wait_ge(kstat, 1)
            dve.wait_ge(ksd, 1)
            after(V.reciprocal(KSD[:], KSD[:]))
            z = KID[:, :, 0, :]

            def over_d(ap):
                return ap.rearrange("p (t o) -> p t o", o=1).broadcast_to([P, 5, HD])

            def over_t(ap):
                return ap.rearrange("p (o d) -> p o d", o=1).broadcast_to([P, 5, HD])

            after(V.tensor_tensor(z, NAT[:, :, 0:HD], over_d(KMV[:, :, 0]), ALU.subtract))
            after(V.tensor_tensor(z, z, over_d(KSD[:]), ALU.mult))
            after(V.tensor_tensor(z, z, over_t(IGB[:, 0, :]), ALU.mult))
            after(V.tensor_tensor(z, z, over_t(IGB[:, 1, :]), ALU.add))
            V.tensor_copy(KID[:, :, 1, :], z).then_inc(kid, 1)
            def sample_queries():
                dve.wait_ge(kit_ev, 2)
                dve.wait_ge(idx_in, 16 * NPG * (8 - IDX_SP))
                dve.wait_ge(idx_sp, 16 * NPG * IDX_SP)
                for half in range(2):
                    r = slice(HD * half, HD * half + HD)
                    ins = V.tensor_copy(
                        IK[r, :, 1024:1025],
                        KIT[r, SEQ:TOK].rearrange("p (c s) -> p c s", s=2)[:, :, half:half + 1])
                ins.then_inc(ikn_ready, 1)
                dve.wait_ge(z_qb, 1)
                dve.wait_ge(ev_act, 4)
                qv = QB[:, 0:320].rearrange("p (c x) -> p c x", x=80)
                for half in range(2):
                    for par in range(2):
                        src = UQ[HD * par:HD * par + HD, 0:4, SEQ:TOK].rearrange(
                            "p f (c s) -> p c s f", s=2)
                        ins = V.tensor_copy(qv[HD * half:HD * half + HD, :, 8 * half + par:
                                               8 * half + par + 8:2][:, :, 0:4], src[:, :, half, :])
                ins.then_inc(qib_ready, 1)

            items = [(t, h) for t in range(1, QT) for h in range(IDXH)]
            for u in range(2, 6):
                low_part(u, u % 2)
            sample_queries()
            low_part(6, 0)
            low_part(7, 1)
            def take_rounds(sc, rows, rounds):
                for _ in range(rounds):
                    after(V.max(MX8[0:rows, :], sc))
                    after(V.match_replace(sc, MX8[0:rows, :], sc, TAKEN))

            def to_mask(sc):
                return V.tensor_scalar(sc, sc, -2.0e38, NEG, ALU.is_gt, ALU.mult)

            dve.wait_ge(ds_sum, 1)
            V.tensor_scalar(DS[:], PSF[0:DB, 2048:2048 + 1025], float(ISCALE), None, ALU.mult
                            ).then_inc(ds_ev, 1)
            dve.wait_ge(ds_ev, 1)
            for n, (t, h) in enumerate(items):
                if n % IDXH == 0:
                    take_rounds(DS[:], DB, 3)
                dve.wait_ge(is_relu, n + 1)
                w = (t + 1) * P
                wi = NAT[:, t, HD + h:HD + h + 1]
                if h == 0:
                    ins = V.tensor_scalar(SC[:, t - 1, 0:w], RS[:, n % 2, 0:w], wi, None, ALU.mult)
                else:
                    ins = V.scalar_tensor_tensor(out=SC[:, t - 1, 0:w], in0=RS[:, n % 2, 0:w],
                                                 scalar=wi, in1=SC[:, t - 1, 0:w],
                                                 op0=ALU.mult, op1=ALU.add)
                ins.then_inc(is_acc, 1)
                dve.wait_ge(is_acc, n + 1)
            for t in range(1, QT):
                V.tensor_scalar(SC[:, t - 1, 0:t * P], SC[:, t - 1, 0:t * P], float(ISCALE), None,
                                ALU.mult)
                d = SC[:, t - 1, t * P:(t + 1) * P]
                after(V.scalar_tensor_tensor(out=d, in0=d, scalar=float(ISCALE), in1=caus,
                                             op0=ALU.mult, op1=ALU.add))

            take_rounds(DS[:], DB, EARLY_ROUNDS - 9)
            dve.wait_ge(ev_act, A_OUT)
            dve.wait_ge(z_qb, 2)
            qv = QB[:].rearrange("p (b x) -> p b x", x=272)
            for gp in range(2):
                for e in range(2):
                    r = slice(HD * e, HD * e + HD)
                    o = gp * 136 + 4 * e
                    src = UQ[r, 6 + 4 * gp:10 + 4 * gp, SEQ:TOK].rearrange("p j b -> p b j")
                    ins = V.tensor_copy(qv[r, :, o:o + 4], src)
            ins.then_inc(qb_ready, 1)
            take_rounds(DS[:], DB, TOPK_S // 8 - EARLY_ROUNDS)
            to_mask(DS[:]).then_inc(top_s, 1)

            def sample_max(n, logits, sink):
                dve.wait_ge(dl_mm, n)
                after(V.tensor_reduce(DST[:, 0:1], logits, AXX, ALU.max))
                if sink:
                    after(V.tensor_tensor(DST[:, 0:1], DST[:, 0:1], SND[:], ALU.max))
                V.tensor_scalar(DST[:, 1:2], DST[:, 0:1], -1.0, None, ALU.mult).then_inc(d_mx, 1)

            def sample_normalise(n, probs, sink):
                dve.wait_ge(d_exp, n)
                if sink:
                    after(V.tensor_tensor(DST[:, 2:3], DST[:, 2:3], DST[:, 3:4], ALU.add))
                after(V.reciprocal(DST[:, 2:3], DST[:, 2:3]))
                V.tensor_scalar(probs, probs, DST[:, 2:3], None, ALU.mult).then_inc(d_p, 1)

            sample_max(1, PSF[:, 0:1025], False)
            sample_normalise(1, PD[:], False)
            for t in range(1, QT - 1):
                sc = SC[:, t - 1, 0:(t + 1) * P]
                take_rounds(sc, P, TOPK_P // 8)
                to_mask(sc).then_inc(top_p, 1)
            take_rounds(SC[:, QT - 2, :], P, EARLY_TOP)
            dve.wait_ge(do_hi, 1)
            for gp in range(2):
                for e in range(2):
                    r = slice(HD * e, HD * e + HD)
                    src = PS[r, 0, 0:2 * P].rearrange("p (b g j) -> p g j b", b=DB, g=2)
                    m, h = slice(4 * gp, 4 * gp + 4), 8 * gp + 4 * e
                    ins = V.tensor_tensor(XL[r, m, SEQ:TOK], src[:, gp, h:h + 4, :],
                                          XH[r, m, SEQ:TOK].bitcast(F32), ALU.subtract)
            ins.then_inc(do_lo, 1)

            def last_top(i):
                sc = SC[:, QT - 2, :]
                rounds = TOPK_P // 8 - EARLY_TOP
                if 0 <= i < TOP_STEPS:
                    take_rounds(sc, P, (i + 1) * rounds // TOP_STEPS - i * rounds // TOP_STEPS)
                if i == TOP_STEPS - 1:
                    to_mask(sc).then_inc(top_p, 1)

            prompt_attention(turns_a, False, last_top)
            output_units(0, A_OUT, 0)
            layer_norm(0, A_OUT + 6, True)
            mlp(1, MLP0, 8)
            layer_norm(1, MLP0 + 62, False)
            def low_parts(i0, i1):
                with dve.Fori(i0, i1) as i:
                    for s in range(2):
                        dve.wait_ge(hi_done, i * 2 + (B_IN + s + 3))
                        low_part(None, s)

            low_parts(0, 2)
            dve.wait_ge(ev_act, A_OUT + 1)
            dve.wait_ge(win_in, 32)
            V.tensor_copy(KW[:, :, P:P + 1],
                          UQ[:, 4, SEQ:TOK].rearrange("p (b o) -> p b o", o=1))
            low_parts(2, 5)
            dve.wait_ge(ev_act, A_OUT + 10)
            dve.wait_ge(z_qb, 3)
            qv = QB[:, 0:DB * 144].rearrange("p (b x) -> p b x", x=144)
            for e in range(2):
                r = slice(HD * e, HD * e + HD)
                ins = V.tensor_copy(qv[r, :, 8 * e:8 * e + 8],
                                    UQ[r, 6:14, SEQ:TOK].rearrange("p j b -> p b j"))
            ins.then_inc(qb_ready, 1)
            dve.wait_ge(bwin, NH)

            def sample_b(i):
                if i == -1:
                    sample_max(2, PS[:, 6, 0:P], True)
                if i == 0:
                    sample_normalise(2, PDW[:], True)
                if i == 2:
                    dve.wait_ge(do_hi, 2)
                    for e in range(2):
                        r = slice(HD * e, HD * e + HD)
                        src = PS[r, 7, 0:P].rearrange("p (b j) -> p j b", b=DB)
                        ins = V.tensor_tensor(XL[r, :, SEQ:TOK], src[:, 8 * e:8 * e + 8, :],
                                              XH[r, :, SEQ:TOK].bitcast(F32), ALU.subtract)
                    ins.then_inc(do_lo, 1)

            prompt_attention(turns_b, True, sample_b)
            output_units(2, B_OUT, 72)
            layer_norm(2, B_OUT + 6, True)
            dve.wait_ge(outs, 16 * 9)
            mlp(3, MLP1, 80)
            layer_norm(3, MLP1 + 62, False, True)


def w_unit_list(w, cols):
    k = w.shape[0]
    u = w[:, np.concatenate(cols)].reshape(k // P, P, len(cols), P)
    return u.transpose(2, 1, 0, 3).reshape(len(cols), P, (k // P) * P)


def kernel(**inputs):
    import concourse.bacc as bacc
    from concourse.bass_utils import run_bass_kernel_spmd

    a = {k: np.asarray(v) for k, v in inputs.items()}
    ar = np.arange
    hcols = lambda h: ar(HD * h, HD * h + HD)
    wa, wb = a["a_w_in"][0], a["b_w_in"][0]
    q_a = [np.concatenate([hcols(h) for h in a_heads(p)]) for p in range(PAIRS)]
    q_b = [np.concatenate([hcols(h) for h in b_heads(p)]) for p in range(PAIRS)]
    o_k, o_v, o_qi, o_ki, o_wi = 1024, 1280, 1536, 2048, 2112
    tiles = lambda o, n: [ar(o + P * i, o + P * i + P) for i in range(n)]
    parts = [w_unit_list(wa, tiles(o_qi, 4) + tiles(o_k, 2) + q_a),
             w_unit_list(a["a_w_out"][0][np.concatenate(q_a)], tiles(0, 8))]

    def mlp_units(l):
        w1, w2 = a["mlp_w1"][l], a["mlp_w2"][l]
        out = []
        for c in range(CHUNKS):
            out.append(w_unit_list(w1, tiles(D * c, 8)))
            out.append(w_unit_list(w2[D * c:D * c + D], tiles(0, 8)))
        return out

    parts += mlp_units(0)
    parts += [w_unit_list(wb, tiles(1024, 2) + q_b),
              w_unit_list(a["b_w_out"][0][np.concatenate(q_b)], tiles(0, 8))]
    parts += mlp_units(1) + [np.zeros((2, P, D), np.float32)]
    x = np.concatenate([a["x_prompt"][0], a["x_sample"][:, 0]], axis=0)
    cst, csth = constants()
    ck = a["cache_k"][0].reshape(POOL_PAGES, PAGE, 2, P).transpose(0, 3, 2, 1)
    lnp = np.stack([np.stack([a[n][l].reshape(KT, P).T for n in (f"ln{i}_g", f"ln{i}_b")], 1)
                    for l in range(2) for i in (1, 2)], 1)
    arrays = {
        "xT": x.T.reshape(KT, P, TOK).transpose(1, 0, 2),
        "wn": wa[:, np.concatenate([ar(o_ki, o_ki + 72), ar(o_v, o_v + 256)])]
        .reshape(KT, P, NATW).transpose(1, 0, 2),
        "wall": np.concatenate(parts),
        "cacheK": ck.reshape(POOL_PAGES, P, 256),
        "cacheV": a["cache_v"][0].reshape(POOL_PAGES, P, 256),
        "cacheI": a["cache_idx_k"][0].transpose(0, 2, 1),
        "pt": a["page_table"].reshape(1, 64),
        "table": a["rel_bias_table"],
        "trep": np.tile(a["rel_bias_table"], (1, DB)),
        "lnp": lnp,
        "igb": np.broadcast_to(np.stack([a["a_idx_ln_g"][0], a["a_idx_ln_b"][0]]), (P, 2, HD)),
        "snk": np.broadcast_to(a["b_sink"], (P, NH)),
        "snd": np.tile(a["b_sink"][0], DB).reshape(P, 1),
        "swk": a["state_win_k"][0].reshape(DB, P, P).transpose(2, 0, 1),
        "swv": a["state_win_v"][0].reshape(DB, P, P),
        "cst": cst,
        "csth": csth,
    }
    out_shapes = {"yT": (P, KT, TOK), "kT": (P, 2, TOK), "vp": (P, QT, 256), "vs": (DB, 256),
                  "kip": (P, QT, HD), "kis": (DB, HD), "wkT": (P, P), "wv": (P, P),
                  "wksT": (P, DB, P), "wvs": (P, DB, P)}
    nc = bacc.Bacc("TRN2", target_bir_lowering=False, num_devices=1)
    io, feeds = {}, {}
    for n, v in arrays.items():
        feeds[n] = np.ascontiguousarray(v)
        io[n] = nc.dram_tensor(n, v.shape, mybir.dt.from_np(v.dtype), kind="ExternalInput").ap()
    for n, s in out_shapes.items():
        io[n] = nc.dram_tensor(n, s, F32, kind="ExternalOutput").ap()
    program(nc, io)
    r = run_bass_kernel_spmd(nc, [feeds], core_ids=[0]).results[0]
    y = r["yT"].transpose(2, 1, 0).reshape(TOK, D)
    k = r["kT"].transpose(2, 1, 0).reshape(TOK, 256)
    blocks = lambda v, w: v.transpose(1, 0, 2).reshape(1, 1, QT, P, *w)
    return (y[:SEQ].reshape(1, SEQ, D), y[SEQ:].reshape(DB, 1, D),
            k[:SEQ].reshape(1, 1, QT, P, 4, HD), blocks(r["vp"], (4, HD)), blocks(r["kip"], (HD,)),
            k[SEQ:].reshape(1, DB, 1, 4, HD), r["vs"].reshape(1, DB, 1, 4, HD),
            r["kis"].reshape(1, DB, 1, HD),
            r["wkT"].T.reshape(1, 1, P, 2, HD), r["wv"].reshape(1, 1, P, 2, HD),
            r["wksT"].transpose(1, 2, 0).reshape(1, DB, P, 2, HD),
            r["wvs"].transpose(1, 0, 2).reshape(1, DB, P, 2, HD))
```
